# Optimizing a Trainium2 kernel written in Bass

```python
import math
import jax
import jax.numpy as jnp
from jax import lax
import numpy as np
import jax, jax.numpy as jnp

D_MODEL = 2048
BATCH = 1
SEQ = 256
DEPTH = 1

GRID_W = 64
CTX_LEN = 256
NORM_EPS = 1e-6

RW_HEADS = 16
RW_HEAD_DIM = 64
RW_WIDTH = RW_HEADS * RW_HEAD_DIM
RW_DECAY_RANK = 96
RW_ICLR_RANK = 96
RW_GATE_RANK = 64
RW_GN_EPS = 64e-5
RW_COLS = 3 * RW_WIDTH + 2 * RW_DECAY_RANK + 2 * RW_ICLR_RANK + RW_GATE_RANK
RW_SPLITS = (RW_WIDTH, 2 * RW_WIDTH, 3 * RW_WIDTH, 3 * RW_WIDTH + 2 * RW_DECAY_RANK,
             3 * RW_WIDTH + 2 * RW_DECAY_RANK + 2 * RW_ICLR_RANK)

GDN_HEADS = 8
GDN_HEAD_DIM = 128
GDN_WIDTH = GDN_HEADS * GDN_HEAD_DIM
GDN_CONV = 5
GDN_CHUNK = 64
GDN_CONV_COLS = 3 * GDN_WIDTH
GDN_AB_COLS = 4 * GDN_HEADS

GATE_COLS = 2 * D_MODEL
IN_SPLITS = (RW_COLS, RW_COLS + GDN_CONV_COLS, RW_COLS + GDN_CONV_COLS + GDN_WIDTH,
             RW_COLS + GDN_CONV_COLS + GDN_WIDTH + GDN_AB_COLS)
N_IN = IN_SPLITS[-1] + GATE_COLS

FFN_HIDDEN = -(-8 * D_MODEL // (3 * 256)) * 256


def rmsnorm(x, w):
    xf = x.astype(jnp.float32)
    y = xf * lax.rsqrt(jnp.mean(xf * xf, axis=-1, keepdims=True) + NORM_EPS)
    return (y * w.astype(jnp.float32)).astype(x.dtype)

def modulate(x, shift, scale):
    return x * (1.0 + scale) + shift

def l2norm(x):
    return x * lax.rsqrt(jnp.sum(x * x, axis=-1, keepdims=True) + NORM_EPS)

def grid_shift(p, rows):
    b, t, ch = p.shape
    g = p.reshape(b, rows, GRID_W, ch // 4, 4)
    left = jnp.pad(g[:, :, :-1, :, 0], ((0, 0), (0, 0), (1, 0), (0, 0)))
    right = jnp.pad(g[:, :, 1:, :, 1], ((0, 0), (0, 0), (0, 1), (0, 0)))
    up = jnp.pad(g[:, :-1, :, :, 2], ((0, 0), (1, 0), (0, 0), (0, 0)))
    down = jnp.pad(g[:, 1:, :, :, 3], ((0, 0), (0, 1), (0, 0), (0, 0)))
    return jnp.stack([left, right, up, down], axis=-1).reshape(b, t, ch)

def seq_shift(p):
    b, t, ch = p.shape
    g = p.reshape(b, t, ch // 2, 2)
    prev = jnp.pad(g[:, :-1, :, 0], ((0, 0), (1, 0), (0, 0)))
    nxt = jnp.pad(g[:, 1:, :, 1], ((0, 0), (0, 1), (0, 0)))
    return jnp.stack([prev, nxt], axis=-1).reshape(b, t, ch)

def depthwise_conv(x, w):
    return lax.conv_general_dilated(x, w[:, None, :], window_strides=(1,),
                                    padding=[(GDN_CONV // 2, GDN_CONV // 2)],
                                    dimension_numbers=('NWC', 'WIO', 'NWC'),
                                    feature_group_count=x.shape[-1])

def prefix_scan(scan_fn, ctx_in, lat_in, s0, reverse):
    flip = (lambda a: jnp.flip(a, axis=1)) if reverse else (lambda a: a)
    y_ctx, s_ctx = scan_fn(*[flip(a) for a in ctx_in], s0)
    y_lat, _ = scan_fn(*[flip(a) for a in lat_in], s_ctx)
    return flip(y_lat), flip(y_ctx)

def rwkv7_scan(r, w, k, v, kk, bb, s0):
    def step(s, inp):
        r_t, w_t, k_t, v_t, kk_t, b_t = inp
        sa = jnp.einsum('bhij,bhj->bhi', s, kk_t)
        s = s * w_t[:, :, None, :] - sa[..., None] * b_t[:, :, None, :] + v_t[..., None] * k_t[:, :, None, :]
        return s, jnp.einsum('bhij,bhj->bhi', s, r_t)
    xs = tuple(jnp.moveaxis(a, 1, 0) for a in (r, w, k, v, kk, bb))
    s_fin, y = lax.scan(step, s0, xs)
    return jnp.moveaxis(y, 0, 1), s_fin

def rwkv_features(p, p_shift, mu, w0, w2, a0, a2, g2, k_k, k_a):
    b, t, _ = p.shape
    xs = (p + (p_shift - p) * mu).astype(jnp.float32)
    r, k, v, wd, ad, gd = jnp.split(xs, RW_SPLITS, axis=-1)
    heads = lambda a: a.reshape(a.shape[:-1] + (RW_HEADS, RW_HEAD_DIM))
    lora_w = jnp.einsum('btdr,drc->btdc', jnp.tanh(wd.reshape(b, t, 2, RW_DECAY_RANK)), w2)
    w_log = -jax.nn.softplus(-(w0 + lora_w)) - 0.5
    decay = jnp.exp(-jnp.exp(w_log))
    iclr = jax.nn.sigmoid(a0 + jnp.einsum('btdr,drc->btdc', ad.reshape(b, t, 2, RW_ICLR_RANK), a2))
    gate = jax.nn.sigmoid(gd) @ g2
    kk = l2norm(heads(k * k_k))
    k_dir = heads(k[:, :, None, :] * (1.0 + (iclr - 1.0) * k_a))
    b_dir = kk[:, :, None] * heads(iclr)
    return heads(r), heads(v), gate, kk, heads(decay), k_dir, b_dir

def rwkv_dir_inputs(f, d):
    r, v, _, kk, decay, k_dir, b_dir = f
    return (r, decay[:, :, d], k_dir[:, :, d], v, kk, b_dir[:, :, d])

def rwkv_readout(y, f, r_k, ln_w, ln_b):
    r, v, gate, _, _, k_dir, _ = f
    b, t = y.shape[:2]
    mu = jnp.mean(y, axis=-1, keepdims=True)
    var = jnp.mean(jnp.square(y - mu), axis=-1, keepdims=True)
    yn = ((y - mu) * lax.rsqrt(var + RW_GN_EPS)).reshape(b, t, RW_WIDTH) * ln_w + ln_b
    k_bonus = jnp.mean(k_dir, axis=2)
    bonus = (jnp.sum(r * k_bonus * r_k, axis=-1, keepdims=True) * v).reshape(b, t, RW_WIDTH)
    return (yn + bonus) * gate

def gdn_chunked(q, k, v, g, beta, s0):
    b, t, h, dk = q.shape
    dv = v.shape[-1]
    n = t // GDN_CHUNK

    def chunks(a):
        a = a.reshape((b, n, GDN_CHUNK, h) + a.shape[3:])
        return jnp.moveaxis(a, (1, 3), (0, 2))

    qc, kc, vc = chunks(q * dk ** -0.5), chunks(k), chunks(v)
    bc = chunks(beta)
    gc = jnp.cumsum(chunks(g), axis=-1)
    idx = jnp.arange(GDN_CHUNK)
    incl = idx[:, None] >= idx[None, :]
    strict = idx[:, None] > idx[None, :]
    diff = gc[..., :, None] - gc[..., None, :]
    decay = jnp.where(incl, jnp.exp(jnp.where(incl, diff, 0.0)), 0.0)
    kb = kc * bc[..., None]
    lmat = jnp.where(strict, jnp.einsum('nbhik,nbhjk->nbhij', kb, kc) * decay, 0.0)
    rhs = jnp.concatenate([vc * bc[..., None], kb * jnp.exp(gc)[..., None]], axis=-1)
    sol = lax.linalg.triangular_solve(lmat, rhs, left_side=True, lower=True, unit_diagonal=True)
    u, wk = sol[..., :dv], sol[..., dv:]
    qk = jnp.where(incl, jnp.einsum('nbhik,nbhjk->nbhij', qc, kc) * decay, 0.0)
    q_dec = qc * jnp.exp(gc)[..., None]
    k_tail = kc * jnp.exp(gc[..., -1:] - gc)[..., None]
    g_last = jnp.exp(gc[..., -1])

    def step(s, inp):
        qk_i, u_i, w_i, qd_i, kt_i, gl_i = inp
        v_new = u_i - jnp.einsum('bhck,bhkv->bhcv', w_i, s)
        o = jnp.einsum('bhck,bhkv->bhcv', qd_i, s) + jnp.einsum('bhcj,bhjv->bhcv', qk_i, v_new)
        s = s * gl_i[..., None, None] + jnp.einsum('bhck,bhcv->bhkv', kt_i, v_new)
        return s, o

    s_fin, o = lax.scan(step, s0, (qk, u, wk, q_dec, k_tail, g_last))
    o = jnp.moveaxis(o, (0, 2), (1, 3)).reshape(b, t, h, dv)
    return o, s_fin

def gdn_features(p_conv, p_ab, conv_w, a_log, dt_bias):
    b, t, _ = p_conv.shape
    u = jax.nn.silu(depthwise_conv(p_conv, conv_w)).astype(jnp.float32)
    q, k, v = jnp.split(u, 3, axis=-1)
    heads = lambda a: a.reshape(b, t, GDN_HEADS, GDN_HEAD_DIM)
    ab = p_ab.astype(jnp.float32).reshape(b, t, 2, 2, GDN_HEADS)
    g = -jnp.exp(a_log.astype(jnp.float32)) * jax.nn.softplus(ab[:, :, 0] + dt_bias)
    beta = jax.nn.sigmoid(ab[:, :, 1])
    return l2norm(heads(q)), l2norm(heads(k)), heads(v), g, beta

def gdn_dir_inputs(f, d):
    q, k, v, g, beta = f
    return (q, k, v, g[:, :, d], beta[:, :, d])

def gdn_readout(o, z, norm_w):
    b, t = o.shape[:2]
    on = o * lax.rsqrt(jnp.mean(o * o, axis=-1, keepdims=True) + NORM_EPS) * norm_w
    return (on * jax.nn.silu(z.astype(jnp.float32)).reshape(o.shape)).reshape(b, t, GDN_WIDTH)

def gated_merge(o_a, o_b, gate_cols, p_a, p_b, w_out):
    g_a, g_b = jnp.split(gate_cols, 2, axis=-1)
    m = jax.nn.sigmoid(g_a) * (o_a @ p_a) + jax.nn.sigmoid(g_b) * (o_b @ p_b)
    return m @ w_out

def swiglu(h, w_gate_up, w_down):
    gate, up = jnp.split(h @ w_gate_up, 2, axis=-1)
    return (jax.nn.silu(gate) * up) @ w_down

def mix_tokens(h, hc, w_in, rw_mu, rw_w0, rw_w2, rw_a0, rw_a2, rw_g2, rw_k_k, rw_k_a, rw_r_k,
               rw_ln_w, rw_ln_b, gdn_conv_w, gdn_a_log, gdn_dt_bias, gdn_norm_w,
               merge_p_a, merge_p_b, w_out, need_ctx):
    rows = h.shape[1] // GRID_W
    bsz = h.shape[0]
    rw, cv, z, ab, gt = jnp.split(h @ w_in, IN_SPLITS, axis=-1)
    rw_c, cv_c, z_c, ab_c, gt_c = jnp.split(hc @ w_in, IN_SPLITS, axis=-1)

    fa = rwkv_features(rw, grid_shift(rw, rows), rw_mu, rw_w0, rw_w2, rw_a0, rw_a2, rw_g2, rw_k_k, rw_k_a)
    fa_c = rwkv_features(rw_c, seq_shift(rw_c), rw_mu, rw_w0, rw_w2, rw_a0, rw_a2, rw_g2, rw_k_k, rw_k_a)
    s0a = jnp.zeros((bsz, RW_HEADS, RW_HEAD_DIM, RW_HEAD_DIM), jnp.float32)
    out_a = [prefix_scan(rwkv7_scan, rwkv_dir_inputs(fa_c, d), rwkv_dir_inputs(fa, d), s0a, d == 1)
             for d in range(2)]
    o_a = rwkv_readout(out_a[0][0] + out_a[1][0], fa, rw_r_k, rw_ln_w, rw_ln_b).astype(h.dtype)

    fb = gdn_features(cv, ab, gdn_conv_w, gdn_a_log, gdn_dt_bias)
    fb_c = gdn_features(cv_c, ab_c, gdn_conv_w, gdn_a_log, gdn_dt_bias)
    s0b = jnp.zeros((bsz, GDN_HEADS, GDN_HEAD_DIM, GDN_HEAD_DIM), jnp.float32)
    out_b = [prefix_scan(gdn_chunked, gdn_dir_inputs(fb_c, d), gdn_dir_inputs(fb, d), s0b, d == 1)
             for d in range(2)]
    o_b = gdn_readout(out_b[0][0] + out_b[1][0], z, gdn_norm_w).astype(h.dtype)

    y = gated_merge(o_a, o_b, gt, merge_p_a, merge_p_b, w_out)
    if not need_ctx:
        return y, None
    o_a_c = rwkv_readout(out_a[0][1] + out_a[1][1], fa_c, rw_r_k, rw_ln_w, rw_ln_b).astype(hc.dtype)
    o_b_c = gdn_readout(out_b[0][1] + out_b[1][1], z_c, gdn_norm_w).astype(hc.dtype)
    return y, gated_merge(o_a_c, o_b_c, gt_c, merge_p_a, merge_p_b, w_out)

def first_inputs(seed: int = 0) -> dict:
    key = jax.random.key(seed)
    ks = jax.random.split(key, 32)
    f32 = jnp.float32
    L, D = DEPTH, D_MODEL

    def nrm(k, shape, scale):
        return scale * jax.random.normal(k, shape, f32)

    dt = jnp.exp(jax.random.uniform(ks[21], (L, 2, GDN_HEADS), f32, math.log(1e-3), math.log(1e-1)))
    return {
        'x': nrm(ks[0], (BATCH, SEQ, D), 1.0),
        'c': nrm(ks[1], (BATCH, D), 1.0),
        'ctx': nrm(ks[2], (BATCH, CTX_LEN, D), 1.0),
        'c_ctx': nrm(ks[3], (D,), 1.0),
        'w_ada': nrm(ks[4], (L, D, 6 * D), 0.5 * D ** -0.5),
        'b_ada': nrm(ks[5], (L, 6 * D), 0.02),
        'norm1_w': 1.0 + nrm(ks[6], (L, D), 0.1),
        'w_in': nrm(ks[7], (L, D, N_IN), D ** -0.5),
        'rw_mu': jax.random.uniform(ks[8], (L, RW_COLS), f32),
        'rw_w0': jnp.linspace(-6.0, 2.0, RW_WIDTH, dtype=f32) + nrm(ks[9], (L, 2, RW_WIDTH), 0.1),
        'rw_w2': nrm(ks[10], (L, 2, RW_DECAY_RANK, RW_WIDTH), 0.5 * RW_DECAY_RANK ** -0.5),
        'rw_a0': nrm(ks[11], (L, 2, RW_WIDTH), 0.5),
        'rw_a2': nrm(ks[12], (L, 2, RW_ICLR_RANK, RW_WIDTH), RW_ICLR_RANK ** -0.5),
        'rw_g2': nrm(ks[13], (L, RW_GATE_RANK, RW_WIDTH), RW_GATE_RANK ** -0.5),
        'rw_k_k': 0.85 + nrm(ks[14], (L, RW_WIDTH), 0.1),
        'rw_k_a': 1.0 + nrm(ks[15], (L, RW_WIDTH), 0.1),
        'rw_r_k': nrm(ks[16], (L, RW_HEADS, RW_HEAD_DIM), 0.1),
        'rw_ln_w': 1.0 + nrm(ks[17], (L, RW_WIDTH), 0.1),
        'rw_ln_b': nrm(ks[18], (L, RW_WIDTH), 0.01),
        'gdn_conv_w': nrm(ks[19], (L, GDN_CONV, GDN_CONV_COLS), GDN_CONV ** -0.5),
        'gdn_a_log': jnp.log(jax.random.uniform(ks[20], (L, 2, GDN_HEADS), f32, 1.0, 16.0)),
        'gdn_dt_bias': dt + jnp.log(-jnp.expm1(-dt)),
        'gdn_norm_w': 1.0 + nrm(ks[22], (L, GDN_HEAD_DIM), 0.1),
        'merge_p_a': nrm(ks[23], (L, RW_WIDTH, D), RW_WIDTH ** -0.5),
        'merge_p_b': nrm(ks[24], (L, GDN_WIDTH, D), GDN_WIDTH ** -0.5),
        'w_out': nrm(ks[25], (L, D, D), D ** -0.5),
        'norm2_w': 1.0 + nrm(ks[26], (L, D), 0.1),
        'ffn_w_gate_up': nrm(ks[27], (L, D, 2 * FFN_HIDDEN), D ** -0.5),
        'ffn_w_down': nrm(ks[28], (L, FFN_HIDDEN, D), FFN_HIDDEN ** -0.5),
        'final_norm_w': 1.0 + nrm(ks[29], (D,), 0.1),
    }

def first_block(x, c, ctx, c_ctx, w_ada, b_ada, norm1_w, w_in, rw_mu, rw_w0, rw_w2, rw_a0, rw_a2,
              rw_g2, rw_k_k, rw_k_a, rw_r_k, rw_ln_w, rw_ln_b, gdn_conv_w, gdn_a_log,
              gdn_dt_bias, gdn_norm_w, merge_p_a, merge_p_b, w_out, norm2_w, ffn_w_gate_up,
              ffn_w_down, final_norm_w):
    silu_c = jax.nn.silu(c)[:, None, :]
    silu_cc = jax.nn.silu(c_ctx)
    for layer in range(DEPTH):
        need_ctx = layer < DEPTH - 1
        mod = silu_c @ w_ada[layer] + b_ada[layer]
        mod_ctx = silu_cc @ w_ada[layer] + b_ada[layer]
        sh1, sc1, gt1, sh2, sc2, gt2 = jnp.split(mod, 6, axis=-1)
        csh1, csc1, cgt1, csh2, csc2, cgt2 = jnp.split(mod_ctx, 6, axis=-1)
        h = modulate(rmsnorm(x, norm1_w[layer]), sh1, sc1)
        hc = modulate(rmsnorm(ctx, norm1_w[layer]), csh1, csc1)
        y, yc = mix_tokens(h, hc, w_in[layer], rw_mu[layer], rw_w0[layer], rw_w2[layer],
                           rw_a0[layer], rw_a2[layer], rw_g2[layer], rw_k_k[layer], rw_k_a[layer],
                           rw_r_k[layer], rw_ln_w[layer], rw_ln_b[layer], gdn_conv_w[layer],
                           gdn_a_log[layer], gdn_dt_bias[layer], gdn_norm_w[layer],
                           merge_p_a[layer], merge_p_b[layer], w_out[layer], need_ctx)
        x = x + gt1 * y
        x = x + gt2 * swiglu(modulate(rmsnorm(x, norm2_w[layer]), sh2, sc2),
                             ffn_w_gate_up[layer], ffn_w_down[layer])
        if need_ctx:
            ctx = ctx + cgt1 * yc
            ctx = ctx + cgt2 * swiglu(modulate(rmsnorm(ctx, norm2_w[layer]), csh2, csc2),
                                      ffn_w_gate_up[layer], ffn_w_down[layer])
    return rmsnorm(x, final_norm_w)


HEAD_DIM = 64
GROUP_HEADS = 8
GROUP_WIDTH = GROUP_HEADS * HEAD_DIM
N_GROUPS = 4
MIX_WIDTH = N_GROUPS * GROUP_WIDTH
D_FF = 4 * D_MODEL
Q_BLOCK = 128
EPS = 1e-6
NEG_INF = -1e30
BIG = 1e9

MLA_Q_RANK = 384
MLA_KV_RANK = 128
MLA_NOPE = 64
MLA_ROPE = 32
MLA_V = HEAD_DIM
ROPE_THETA = 10000.0

NSA_KV_HEADS = 2
NSA_KV_WIDTH = NSA_KV_HEADS * HEAD_DIM
NSA_CMP_LEN = 32
NSA_CMP_STRIDE = 16
NSA_SEL_LEN = 64
NSA_TOP_N = 8
NSA_WINDOW = 256

SWA_KV_HEADS = 2
SWA_KV_WIDTH = SWA_KV_HEADS * HEAD_DIM
SWA_WINDOW = 128

REL_BUCKETS = 32
REL_MAX_DIST = 128
REL_HEADS = 2 * GROUP_HEADS

IN_SPLITS_2 = (
    MLA_Q_RANK, MLA_KV_RANK, MLA_ROPE,
    GROUP_WIDTH, GROUP_WIDTH, GROUP_WIDTH, GROUP_HEADS,
    GROUP_WIDTH, NSA_KV_WIDTH, NSA_KV_WIDTH, NSA_KV_WIDTH,
    NSA_KV_WIDTH, NSA_KV_WIDTH, NSA_KV_WIDTH, 3 * GROUP_HEADS,
    GROUP_WIDTH, SWA_KV_WIDTH, SWA_KV_WIDTH,
)
IN_COLS = sum(IN_SPLITS_2)


def rmsnorm_2(x, g):
    xf = x.astype(jnp.float32)
    y = xf * lax.rsqrt(jnp.mean(xf * xf, axis=-1, keepdims=True) + EPS)
    return (y * g.astype(jnp.float32)).astype(x.dtype)

def split_heads(x, h):
    b, t, _ = x.shape
    return x.reshape(b, t, h, -1).transpose(0, 2, 1, 3)

def merge_heads(x):
    b, h, t, d = x.shape
    return x.transpose(0, 2, 1, 3).reshape(b, t, h * d)

def rope(x, pos):
    d = x.shape[-1]
    inv = ROPE_THETA ** (-jnp.arange(0, d, 2, dtype=jnp.float32) / d)
    ang = pos.astype(jnp.float32)[:, None] * inv[None, :]
    cos, sin = jnp.cos(ang), jnp.sin(ang)
    x1 = x[..., : d // 2].astype(jnp.float32)
    x2 = x[..., d // 2:].astype(jnp.float32)
    return jnp.concatenate([x1 * cos - x2 * sin, x1 * sin + x2 * cos], axis=-1).astype(x.dtype)

def t5_bucket(dist):
    max_exact = REL_BUCKETS // 2
    d = jnp.maximum(dist, 0)
    large = max_exact + (jnp.log(jnp.maximum(d, 1).astype(jnp.float32) / max_exact)
                         / math.log(REL_MAX_DIST / max_exact)
                         * (REL_BUCKETS - max_exact)).astype(jnp.int32)
    large = jnp.minimum(large, REL_BUCKETS - 1)
    return jnp.where(d < max_exact, d, large)

def dense_causal_attention(q, k, v, scale, fcum=None):
    b, h, t, dk = q.shape
    nb = t // Q_BLOCK
    kpos = jnp.arange(t)
    qb = q.reshape(b, h, nb, Q_BLOCK, dk).transpose(2, 0, 1, 3, 4)
    xs = (jnp.arange(nb), qb)
    if fcum is not None:
        xs = xs + (fcum.reshape(b, h, nb, Q_BLOCK).transpose(2, 0, 1, 3),)

    def one_block(args):
        i, qi = args[0], args[1]
        s = jnp.einsum('bhqd,bhkd->bhqk', qi, k, preferred_element_type=jnp.float32) * scale
        if fcum is not None:
            s = s + args[2][..., :, None] - fcum[:, :, None, :]
        qpos = i * Q_BLOCK + jnp.arange(Q_BLOCK)
        s = jnp.where(kpos[None, :] <= qpos[:, None], s, NEG_INF)
        p = jax.nn.softmax(s, axis=-1)
        return jnp.einsum('bhqk,bhkd->bhqd', p.astype(v.dtype), v)

    o = lax.map(one_block, xs)
    return o.transpose(1, 2, 0, 3, 4).reshape(b, h, t, v.shape[-1])

def banded_attention(q, k, v, window, tbl, sinks=None):
    b, g, r, t, d = q.shape
    nb, nw = t // Q_BLOCK, window // Q_BLOCK

    def blocks(a):
        ap = jnp.pad(a, ((0, 0), (0, 0), (window, 0), (0, 0))).reshape(b, g, nb + nw, Q_BLOCK, d)
        return jnp.concatenate([ap[:, :, i:i + nb] for i in range(nw + 1)], axis=3)

    kb, vb = blocks(k), blocks(v)
    qb = q.reshape(b, g, r, nb, Q_BLOCK, d)
    s = jnp.einsum('bgrnqd,bgnkd->bgrnqk', qb, kb, preferred_element_type=jnp.float32) * d ** -0.5
    kw = (nw + 1) * Q_BLOCK
    dist = (jnp.arange(Q_BLOCK)[:, None] + window) - jnp.arange(kw)[None, :]
    key_real = jnp.arange(nb)[:, None, None] * Q_BLOCK - window + jnp.arange(kw)[None, None, :]
    mask = (dist >= 0) & (dist < window) & (key_real >= 0)
    s = s + tbl[:, :, t5_bucket(dist)][:, :, None].astype(jnp.float32)
    s = jnp.where(mask, s, NEG_INF)
    if sinks is not None:
        sink = jnp.broadcast_to(sinks.astype(jnp.float32)[None, :, :, None, None, None], s.shape[:-1] + (1,))
        p = jax.nn.softmax(jnp.concatenate([s, sink], axis=-1), axis=-1)[..., :-1]
    else:
        p = jax.nn.softmax(s, axis=-1)
    o = jnp.einsum('bgrnqk,bgnkd->bgrnqd', p.astype(v.dtype), vb)
    return o.reshape(b, g, r, t, d)

def mla_mixer(c_q, c_kv, k_pe, q_norm, w_uq, kv_norm, w_ukv, pos):
    b, t, _ = c_q.shape
    q = split_heads(rmsnorm_2(c_q, q_norm) @ w_uq, GROUP_HEADS)
    q = jnp.concatenate([q[..., :MLA_NOPE], rope(q[..., MLA_NOPE:], pos)], axis=-1)
    kv = split_heads(rmsnorm_2(c_kv, kv_norm) @ w_ukv, GROUP_HEADS)
    k_pe = jnp.broadcast_to(rope(k_pe[:, None], pos), (b, GROUP_HEADS, t, MLA_ROPE))
    k = jnp.concatenate([kv[..., :MLA_NOPE], k_pe], axis=-1)
    v = kv[..., MLA_NOPE:]
    o = dense_causal_attention(q, k, v, (MLA_NOPE + MLA_ROPE) ** -0.5)
    return merge_heads(o)

def fox_mixer(q, k, v, f_logit, b_f):
    log_f = jax.nn.log_sigmoid(f_logit.astype(jnp.float32) + b_f.astype(jnp.float32))
    fcum = jnp.cumsum(log_f, axis=1).transpose(0, 2, 1)
    o = dense_causal_attention(split_heads(q, GROUP_HEADS), split_heads(k, GROUP_HEADS),
                               split_heads(v, GROUP_HEADS), HEAD_DIM ** -0.5, fcum)
    return merge_heads(o)

def nsa_compress(kv, pos_emb, w1, w2):
    b, g, t, d = kv.shape
    nc = (t - NSA_CMP_LEN) // NSA_CMP_STRIDE + 1
    idx = jnp.arange(nc)[:, None] * NSA_CMP_STRIDE + jnp.arange(NSA_CMP_LEN)[None, :]
    blk = kv[:, :, idx] + pos_emb
    flat = blk.reshape(b, g, nc, NSA_CMP_LEN * d)
    return jax.nn.gelu(flat @ w1) @ w2

def nsa_cmp_sel(qg, k_cmp, v_cmp, ks, vs, tbl):
    b, g, r, t, d = qg.shape
    nb = t // Q_BLOCK
    nc = k_cmp.shape[2]
    ns = t // NSA_SEL_LEN
    n_top = min(NSA_TOP_N, ns)
    scale = d ** -0.5
    cmp_end = jnp.arange(nc) * NSA_CMP_STRIDE + NSA_CMP_LEN - 1
    ci = jnp.arange(nc)[:, None]
    sj = jnp.arange(ns)[None, :]
    overlap = ((ci * NSA_CMP_STRIDE + NSA_CMP_LEN - 1 >= sj * NSA_SEL_LEN)
               & (ci * NSA_CMP_STRIDE <= sj * NSA_SEL_LEN + NSA_SEL_LEN - 1)).astype(jnp.float32)
    ks_blk = ks.reshape(b, g, ns, NSA_SEL_LEN, d)
    vs_blk = vs.reshape(b, g, ns, NSA_SEL_LEN, d)
    bi = jnp.arange(b)[:, None, None, None]
    gi = jnp.arange(g)[None, :, None, None]
    g_ix = jnp.arange(g)[None, :, None, None, None]
    r_ix = jnp.arange(r)[None, None, :, None, None]
    jsel = jnp.arange(ns)
    qb = qg.reshape(b, g, r, nb, Q_BLOCK, d).transpose(3, 0, 1, 2, 4, 5)

    def one_block(args):
        n, qi = args
        qpos = n * Q_BLOCK + jnp.arange(Q_BLOCK)
        sc = jnp.einsum('bgrqd,bgcd->bgrqc', qi, k_cmp, preferred_element_type=jnp.float32) * scale
        dist_c = qpos[:, None] - cmp_end[None, :]
        valid_c = dist_c >= 0
        sc = sc + tbl[:, :, t5_bucket(dist_c)].astype(jnp.float32)
        sc = jnp.where(valid_c, sc, NEG_INF)
        pc = jnp.where(valid_c, jax.nn.softmax(sc, axis=-1), 0.0)
        o_cmp = jnp.einsum('bgrqc,bgcd->bgrqd', pc.astype(v_cmp.dtype), v_cmp)
        imp = jnp.einsum('bgrqc,cs->bgqs', pc, overlap)
        cur = (qpos // NSA_SEL_LEN)[:, None]
        forced = (jsel[None, :] == 0) | (jsel[None, :] == cur) | (jsel[None, :] == cur - 1)
        score = jnp.where(jsel[None, :] <= cur, jnp.where(forced, BIG, imp), NEG_INF)
        _, sel = lax.top_k(score, n_top)
        k_sel = ks_blk[bi, gi, sel].reshape(b, g, Q_BLOCK, n_top * NSA_SEL_LEN, d)
        v_sel = vs_blk[bi, gi, sel].reshape(b, g, Q_BLOCK, n_top * NSA_SEL_LEN, d)
        kpos = (sel[..., None] * NSA_SEL_LEN + jnp.arange(NSA_SEL_LEN)).reshape(b, g, Q_BLOCK, n_top * NSA_SEL_LEN)
        dist_s = qpos[None, None, :, None] - kpos
        ss = jnp.einsum('bgrqd,bgqkd->bgrqk', qi, k_sel, preferred_element_type=jnp.float32) * scale
        ss = ss + tbl[g_ix, r_ix, t5_bucket(dist_s)[:, :, None]].astype(jnp.float32)
        ss = jnp.where(dist_s[:, :, None] >= 0, ss, NEG_INF)
        ps = jax.nn.softmax(ss, axis=-1)
        o_sel = jnp.einsum('bgrqk,bgqkd->bgrqd', ps.astype(v_sel.dtype), v_sel)
        return o_cmp, o_sel

    o_cmp, o_sel = lax.map(one_block, (jnp.arange(nb), qb))
    fix = lambda o: o.transpose(1, 2, 3, 0, 4, 5).reshape(b, g, r, t, d)
    return fix(o_cmp), fix(o_sel)

def nsa_mixer(q, kc, vc, ksl, vsl, kwn, vwn, gate, cmp_pos, cmp_w1, cmp_w2, tbl):
    b, t, _ = q.shape
    g, r = NSA_KV_HEADS, GROUP_HEADS // NSA_KV_HEADS
    qg = split_heads(q, GROUP_HEADS).reshape(b, g, r, t, HEAD_DIM)
    kc, vc = split_heads(kc, g), split_heads(vc, g)
    ksl, vsl = split_heads(ksl, g), split_heads(vsl, g)
    kwn, vwn = split_heads(kwn, g), split_heads(vwn, g)
    k_cmp = nsa_compress(kc, cmp_pos[0], cmp_w1[0], cmp_w2[0])
    v_cmp = nsa_compress(vc, cmp_pos[1], cmp_w1[1], cmp_w2[1])
    o_cmp, o_sel = nsa_cmp_sel(qg, k_cmp, v_cmp, ksl, vsl, tbl)
    o_win = banded_attention(qg, kwn, vwn, NSA_WINDOW, tbl)
    gts = jax.nn.sigmoid(gate).reshape(b, t, g, r, 3).transpose(0, 2, 3, 1, 4)
    o = gts[..., 0:1] * o_cmp + gts[..., 1:2] * o_sel + gts[..., 2:3] * o_win
    return merge_heads(o.reshape(b, GROUP_HEADS, t, HEAD_DIM))

def swa_mixer(q, k, v, sinks, tbl):
    b, t, _ = q.shape
    g, r = SWA_KV_HEADS, GROUP_HEADS // SWA_KV_HEADS
    qg = split_heads(q, GROUP_HEADS).reshape(b, g, r, t, HEAD_DIM)
    o = banded_attention(qg, split_heads(k, g), split_heads(v, g), SWA_WINDOW, tbl, sinks.reshape(g, r))
    return merge_heads(o.reshape(b, GROUP_HEADS, t, HEAD_DIM))

def second_inputs(seed: int = 0) -> dict:
    key = jax.random.key(seed)
    ks = jax.random.split(key, 20)
    nrm = lambda k, shape, fan_in: jax.random.normal(k, shape, jnp.float32) * fan_in ** -0.5
    gain = lambda k, shape: 1.0 + 0.05 * jax.random.normal(k, shape, jnp.float32)
    L = DEPTH
    return {
        'x': jax.random.normal(ks[0], (BATCH, SEQ, D_MODEL), jnp.float32),
        'norm_attn': gain(ks[1], (L, D_MODEL)),
        'w_in': nrm(ks[2], (L, D_MODEL, IN_COLS), D_MODEL),
        'mla_q_norm': gain(ks[3], (L, MLA_Q_RANK)),
        'mla_w_uq': nrm(ks[4], (L, MLA_Q_RANK, GROUP_HEADS * (MLA_NOPE + MLA_ROPE)), MLA_Q_RANK),
        'mla_kv_norm': gain(ks[5], (L, MLA_KV_RANK)),
        'mla_w_ukv': nrm(ks[6], (L, MLA_KV_RANK, GROUP_HEADS * (MLA_NOPE + MLA_V)), MLA_KV_RANK),
        'fox_b_f': 3.0 + 0.5 * jax.random.normal(ks[7], (L, GROUP_HEADS), jnp.float32),
        'nsa_cmp_pos': 0.1 * jax.random.normal(ks[8], (L, 2, NSA_CMP_LEN, HEAD_DIM), jnp.float32),
        'nsa_cmp_w1': nrm(ks[9], (L, 2, NSA_CMP_LEN * HEAD_DIM, HEAD_DIM), NSA_CMP_LEN * HEAD_DIM),
        'nsa_cmp_w2': nrm(ks[10], (L, 2, HEAD_DIM, HEAD_DIM), HEAD_DIM),
        'swa_sinks': 0.5 * jax.random.normal(ks[11], (L, GROUP_HEADS), jnp.float32),
        'group_norm': gain(ks[12], (L, MIX_WIDTH)),
        'w_out': nrm(ks[13], (L, MIX_WIDTH, D_MODEL), MIX_WIDTH),
        'norm_mlp': gain(ks[14], (L, D_MODEL)),
        'w_up': nrm(ks[15], (L, D_MODEL, D_FF), D_MODEL),
        'w_down': nrm(ks[16], (L, D_FF, D_MODEL), D_FF),
        'rel_bias': 0.5 * jax.random.normal(ks[17], (REL_BUCKETS, REL_HEADS), jnp.float32),
        'final_norm': gain(ks[18], (D_MODEL,)),
    }

def second_block(x, norm_attn, w_in, mla_q_norm, mla_w_uq, mla_kv_norm, mla_w_ukv, fox_b_f,
              nsa_cmp_pos, nsa_cmp_w1, nsa_cmp_w2, swa_sinks, group_norm, w_out,
              norm_mlp, w_up, w_down, rel_bias, final_norm):
    b, t, _ = x.shape
    pos = jnp.arange(t)
    r_nsa = GROUP_HEADS // NSA_KV_HEADS
    r_swa = GROUP_HEADS // SWA_KV_HEADS
    tbl_nsa = rel_bias[:, :GROUP_HEADS].T.reshape(NSA_KV_HEADS, r_nsa, REL_BUCKETS)
    tbl_swa = rel_bias[:, GROUP_HEADS:].T.reshape(SWA_KV_HEADS, r_swa, REL_BUCKETS)
    offsets = [int(o) for o in np.cumsum(IN_SPLITS_2)[:-1]]
    h = x
    for l in range(DEPTH):
        u = rmsnorm_2(h, norm_attn[l])
        p = jnp.split(u @ w_in[l], offsets, axis=-1)
        o_mla = mla_mixer(p[0], p[1], p[2], mla_q_norm[l], mla_w_uq[l], mla_kv_norm[l], mla_w_ukv[l], pos)
        o_fox = fox_mixer(p[3], p[4], p[5], p[6], fox_b_f[l])
        o_nsa = nsa_mixer(p[7], p[8], p[9], p[10], p[11], p[12], p[13], p[14],
                          nsa_cmp_pos[l], nsa_cmp_w1[l], nsa_cmp_w2[l], tbl_nsa)
        o_swa = swa_mixer(p[15], p[16], p[17], swa_sinks[l], tbl_swa)
        o = jnp.concatenate([o_mla, o_fox, o_nsa, o_swa], axis=-1).reshape(b, t, N_GROUPS, GROUP_WIDTH)
        o = rmsnorm_2(o, group_norm[l].reshape(N_GROUPS, GROUP_WIDTH)).reshape(b, t, MIX_WIDTH)
        h = h + o @ w_out[l]
        m = rmsnorm_2(h, norm_mlp[l]) @ w_up[l]
        h = h + jnp.square(jax.nn.relu(m)) @ w_down[l]
    return rmsnorm_2(h, final_norm)


def setup_inputs(seed=0):
    out = dict(first_inputs(seed))
    for name, value in second_inputs(seed + 1).items():
        if name != "x":
            out[name + "_2"] = value
    return out


def reference(
    x, c, ctx, c_ctx, w_ada, b_ada, norm1_w, w_in, rw_mu, rw_w0, rw_w2, rw_a0, rw_a2, rw_g2,
    rw_k_k, rw_k_a, rw_r_k, rw_ln_w, rw_ln_b, gdn_conv_w, gdn_a_log, gdn_dt_bias, gdn_norm_w,
    merge_p_a, merge_p_b, w_out, norm2_w, ffn_w_gate_up, ffn_w_down, final_norm_w, norm_attn_2,
    w_in_2, mla_q_norm_2, mla_w_uq_2, mla_kv_norm_2, mla_w_ukv_2, fox_b_f_2, nsa_cmp_pos_2,
    nsa_cmp_w1_2, nsa_cmp_w2_2, swa_sinks_2, group_norm_2, w_out_2, norm_mlp_2, w_up_2,
    w_down_2, rel_bias_2, final_norm_2,
):
    x = first_block(
        x, c, ctx, c_ctx, w_ada, b_ada, norm1_w, w_in, rw_mu, rw_w0, rw_w2, rw_a0, rw_a2, rw_g2,
        rw_k_k, rw_k_a, rw_r_k, rw_ln_w, rw_ln_b, gdn_conv_w, gdn_a_log, gdn_dt_bias,
        gdn_norm_w, merge_p_a, merge_p_b, w_out, norm2_w, ffn_w_gate_up, ffn_w_down,
        final_norm_w,
    )
    return second_block(
        x, norm_attn_2, w_in_2, mla_q_norm_2, mla_w_uq_2, mla_kv_norm_2, mla_w_ukv_2, fox_b_f_2,
        nsa_cmp_pos_2, nsa_cmp_w1_2, nsa_cmp_w2_2, swa_sinks_2, group_norm_2, w_out_2,
        norm_mlp_2, w_up_2, w_down_2, rel_bias_2, final_norm_2,
    )


_drawn_inputs = setup_inputs


def setup_inputs(seed=0):
    import zlib

    import numpy as np

    out = dict(_drawn_inputs(seed))
    spreads = {}
    factors = {'rw_w2': 7.681,
     'rw_k_k': 3.855,
     'rw_k_a': 2.811,
     'rw_ln_w': 4.012,
     'rw_ln_b': 28.598,
     'gdn_norm_w': 3.425,
     'mla_q_norm_2': 3.514,
     'swa_sinks_2': 6.815}
    for name, (base, spread) in spreads.items():
        noise = np.random.default_rng([zlib.crc32(name.encode()), seed]).standard_normal(out[name].shape)
        drawn = base * np.exp(spread * noise) if base else spread * noise
        out[name] = jnp.asarray(drawn.astype(out[name].dtype))
    for name, factor in factors.items():
        out[name] = (out[name] * factor).astype(out[name].dtype)
    return out
```

```python
from contextlib import ExitStack

import concourse.bass as bass
from concourse import mybir

F32 = mybir.dt.float32
F32R = mybir.dt.float32r
I32 = mybir.dt.int32
ALU = mybir.AluOpType
ACT = mybir.ActivationFunctionType
AX_X = mybir.AxisListType.X

P = 128
D = 2048
KT = D // P
LAT = 256
CTX = 256
TOK = LAT + CTX
EPS = 1e-6
SLOTS = 4
SPLITS = 2
CHUNK = 2048

RW_HEADS, RW_DIM = 16, 64
RW_W = RW_HEADS * RW_DIM
RANK = 96
GATE_RANK = 64
RW_COLS = 3 * RW_W + 4 * RANK + GATE_RANK
GDN_HEADS = 8
GDN_W = GDN_HEADS * P
TAPS = 5
CONV0 = RW_COLS
Z0 = CONV0 + 3 * GDN_W
AB0 = Z0 + GDN_W
GATE0 = AB0 + 4 * GDN_HEADS
N_IN = GATE0 + 2 * D
FFN, FFN_2 = 5632, 8192
N_IN2 = 4160


class Scope:

    def __init__(self, nc, stack, name):
        self.nc, self.stack, self.name, self.sems = nc, stack, name, []
        stack.callback(self.clear)

    def clear(self):
        if self.sems:
            self.nc.clear_and_free_semaphores(self.sems)
            self.nc.all_engine_barrier()

    def sb(self, name, shape, dt=F32):
        return self.stack.enter_context(self.nc.sbuf_tensor(f"{self.name}_{name}", shape, dt))

    def ps(self, name, shape):
        return self.stack.enter_context(self.nc.psum_tensor(f"{self.name}_{name}", shape, F32))

    def sem(self, name):
        self.sems.append(self.nc.alloc_semaphore(name=f"{self.name}_{name}"))
        return self.sems[-1]


class Ring:

    def __init__(self, scope):
        self.slots = scope.sb("ring", [P, SLOTS, CHUNK])
        self.full = [scope.sem(f"slot_full{s}") for s in range(SLOTS)]
        self.used, self.highs, self.done = scope.sem("chunks_used"), scope.sem("chunks_high"), scope.sem("chunks_done")
        self.n = self.first = 0

    def place_parts(self, scope):
        self.high = scope.sb("chunk_high", [P, SPLITS, CHUNK], F32R)
        self.low = scope.sb("chunk_low", [P, SPLITS, CHUNK], F32R)
        self.x_high = scope.sb("x_high", [P, SPLITS, LAT], F32R)
        self.x_low = scope.sb("x_low", [P, SPLITS, LAT], F32R)

    def take(self, count):
        at = self.n
        self.n += count
        return at

    def load(self, sp, n, i, src, kt, width):
        sp.wait_ge(self.used, 8 * i + n + 1)
        dst = self.slots[:, n % SLOTS, 0:kt * width].rearrange("p (k n) -> p k n", k=kt)
        sp.dma_start(dst, src).then_inc(self.full[n % SLOTS], 16)

    def wait(self, eng, n, i):
        eng.wait_ge(self.full[n % SLOTS], 16 * (8 // SLOTS) * i + 16 * (n // SLOTS + 1))

    def wait_used(self, eng, n, i):
        eng.wait_ge(self.used, 8 * i + SLOTS + n + 1)

    def wait_done(self, eng, n, i):
        eng.wait_ge(self.done, 8 * i + SPLITS + n - self.first + 1)

    def split_high(self, act, n, i, size, x=None):
        self.wait(act, n, i)
        act.wait_ge(self.done, 8 * i + n - self.first + 1)
        if x is not None:
            act.activation(self.x_high[:, n % SPLITS, :], x, ACT.Copy)
        act.activation(self.high[:, n % SPLITS, 0:size], self.slots[:, n % SLOTS, 0:size], ACT.Copy).then_inc(self.highs, 1)

    def split_low(self, dve, n, i, size, x=None):
        dve.wait_ge(self.highs, 8 * i + n - self.first + 1)
        if x is not None:
            dve.tensor_tensor(self.x_low[:, n % SPLITS, :], x, self.x_high[:, n % SPLITS, :], ALU.subtract)
        dve.tensor_tensor(self.low[:, n % SPLITS, 0:size], self.slots[:, n % SLOTS, 0:size],
                          self.high[:, n % SPLITS, 0:size], ALU.subtract).then_inc(self.used, 1)

    def view(self, n, kt, width):
        return self.slots[:, n % SLOTS, 0:kt * width].rearrange("p (k n) -> p k n", k=kt)

    def parts(self, n, kt, width):
        return [t[:, n % SPLITS, 0:kt * width].rearrange("p (k n) -> p k n", k=kt) for t in (self.high, self.low)]


class Steps:

    def __init__(self, eng, sem, base=0):
        self.eng, self.sem, self.n, self.base = eng, sem, 0, base

    def __call__(self, ins):
        self.n += 1
        ins.then_inc(self.sem, 1)
        self.eng.wait_ge(self.sem, self.base + self.n)


def phase_ada(nc, g):
    blocks = 6 * D // 512
    n0 = g.ring.take(blocks * 4)
    g.ring.first = g.ring.n
    with ExitStack() as stack:
        s = Scope(nc, stack, "ada")
        crow = s.sb("crow", [2 * KT, P])
        ccol = s.sb("ccol", [P, 2 * KT])
        half = s.sb("half", [P, 2 * KT])
        bias = s.sb("bias", [2, 6 * D])
        mod = s.sb("mod", [2, 6 * D])
        ps_t = s.ps("ps_t", [P, 512])
        acc = [s.ps(f"acc{i}", [P, 512]) for i in range(2)]
        rows_in, bias_in = s.sem("rows_in"), s.sem("bias_in")
        turned, halved, stepped, silu_done = s.sem("turned"), s.sem("halved"), s.sem("stepped"), s.sem("silu_done")
        bank_free, stored = s.sem("bank_free"), s.sem("stored")

        with nc.Block() as block:

            @block.sync
            def _(sp):
                w = g.w_ada[0].rearrange("(k p) n -> p k n", p=P)
                with sp.Fori(0, blocks // 2) as i:
                    for j in range(8):
                        g.ring.load(sp, n0 + j, i, w[:, 4 * (j % 4):4 * (j % 4) + 4,
                                                     bass.ds(i * 1024 + (j // 4) * 512, 512)], 4, 512)

            @block.gpsimd
            def _(pool):
                pool.dma_start(g.ident[:], g.c_ident).then_inc(rows_in, 16)
                pool.dma_start(crow[0:KT, :], g.c.rearrange("a (k p) -> (a k) p", p=P)).then_inc(rows_in, 16)
                pool.dma_start(crow[KT:2 * KT, :], g.c_ctx.rearrange("(k p) -> k p", p=P)).then_inc(rows_in, 16)
                for r in range(2):
                    pool.dma_start(bias[r:r + 1, :], g.b_ada).then_inc(bias_in, 16)
                pool.wait_ge(bank_free, blocks + 2)
                pool.dma_start(g.d_mod, mod[:]).then_inc(stored, 16)
                pool.wait_ge(stored, 16)

            @block.tensor
            def _(pe):
                pe.sem_inc(g.ring.used, SLOTS)
                pe.sem_inc(g.ring.done, SPLITS)
                pe.wait_ge(rows_in, 48)
                pe.transpose(ps_t[:, 0:2 * KT], crow[:], g.ident[0:2 * KT, 0:2 * KT]).then_inc(turned, 1)
                pe.wait_ge(silu_done, 1)
                with pe.Fori(0, blocks // 2) as i:
                    for j in range(8):
                        b, q = j // 4, j % 4
                        g.ring.wait(pe, n0 + j, i)
                        if q == 0:
                            pe.wait_ge(bank_free, 2 * i + b + 1)
                        w = g.ring.view(n0 + j, 4, 512)
                        for k in range(4):
                            kt = 4 * q + k
                            ins = pe.matmul(acc[b][0:2, :], ccol[:, kt:kt + KT + 1:KT], w[:, k, :],
                                            start=(kt == 0), stop=(kt == KT - 1))
                        ins.then_inc(g.ring.used, 1)

            @block.scalar
            def _(act):
                act.wait_ge(turned, 1)
                act.activation(half[:], ps_t[:, 0:2 * KT], ACT.Tanh, scale=0.5).then_inc(halved, 1)

            @block.vector
            def _(dve):
                dve.sem_inc(bank_free, 2)
                step = Steps(dve, stepped)
                dve.wait_ge(halved, 1)
                step(dve.tensor_scalar(half[:], half[:], 0.5, 0.5, ALU.mult, ALU.add))
                dve.tensor_tensor(ccol[:], ps_t[:, 0:2 * KT], half[:], ALU.mult).then_inc(silu_done, 1)
                dve.wait_ge(bias_in, 32)
                with dve.Fori(0, blocks // 2) as i:
                    for b in range(2):
                        g.ring.wait_used(dve, n0 + 4 * b + 3, i)
                        cols = bass.ds(i * 1024 + b * 512, 512)
                        dve.tensor_tensor(mod[:, cols], acc[b][0:2, :], bias[:, cols], ALU.add)\
                           .then_inc(bank_free, 1)



def norm_rows(count):
    return [(r, min(8, count - r)) for r in range(0, count, 8)]


def phase_norm1(nc, g):
    with ExitStack() as stack:
        s = Scope(nc, stack, "n1")
        rows = s.sb("rows", [5 * KT, P])
        cols = s.sb("cols", [P, 5 * KT])
        gain = s.sb("gain", [P, 2, KT])
        xin = s.sb("xin", [P, 2, D])
        ctx_t = s.sb("ctx_t", [P, KT, CTX])
        sq = s.sb("sq", [P, 2, TOK])
        rstd = s.sb("rstd", [P, TOK])
        eps = s.sb("eps", [P, 1])
        ps_x = [s.ps(f"ps_x{i}", [P, 4, P]) for i in range(4)]
        ps_s = s.ps("ps_s", [P, TOK])
        ps_r = s.ps("ps_r", [P, 512])
        rows_in = s.sem("rows_in")
        x_in = [s.sem(f"x_in{i}") for i in range(2)]
        rows_turned, cols_done, turned, copied_dve, copied_act = (s.sem(n) for n in (
            "rows_turned", "cols_done", "turned", "copied_dve", "copied_act"))
        squared, summed, rooted, eps_set, stepped = (s.sem(n) for n in ("squared", "summed", "rooted", "eps_set", "stepped"))
        sources = [(g.x[0], 0), (g.x[0], P), (g.ctx[0], 0), (g.ctx[0], P)]

        def dst(t, q):
            tile, c0 = (g.x_t, t * P) if t < 2 else (ctx_t, t * P - LAT)
            return tile[:, 4 * q:4 * q + 4, c0:c0 + P]

        def tokens(kt):
            return ((g.x_t[:, kt, :], slice(0, LAT)), (ctx_t[:, kt, :], slice(LAT, TOK)))

        with nc.Block() as block:

            @block.sync
            def _(sp):
                for t in range(4):
                    src, r0 = sources[t]
                    if t >= 2:
                        sp.wait_ge(turned, 4 * (t - 1))
                    sp.dma_start(xin[:, t % 2, :], src[r0:r0 + P, :]).then_inc(x_in[t % 2], 16)

            @block.gpsimd
            def _(pool):
                m = g.d_mod
                for k, src in enumerate((g.norm1_w[0], m[0, 0:D], m[0, D:2 * D], m[1, 0:D], m[1, D:2 * D])):
                    pool.dma_start(rows[KT * k:KT * (k + 1), :], src.rearrange("(k p) -> k p", p=P)).then_inc(rows_in, 16)
                pool.dma_start(g.ones[:], g.c_ones).then_inc(rows_in, 16)

            @block.tensor
            def _(pe):
                for t in range(4):
                    pe.wait_ge(x_in[t % 2], 16 * (t // 2 + 1))
                    for q in range(4):
                        n = 4 * t + q
                        if n >= 4:
                            pe.wait_ge((copied_dve, copied_act)[n % 2], (n - 4) // 2 + 1)
                        for k in range(4):
                            ins = pe.transpose(ps_x[n % 4][:, k, :], xin[:, t % 2, (4 * q + k) * P:(4 * q + k + 1) * P], g.ident[:])
                        ins.then_inc(turned, 1)
                pe.wait_ge(rows_in, 96)
                pe.transpose(ps_r[:, 0:5 * KT], rows[:], g.ident[0:5 * KT, 0:5 * KT]).then_inc(rows_turned, 1)
                for kt in range(KT):
                    pe.wait_ge(squared, 2 * (kt + 1))
                    pe.matmul(ps_s[:], g.ones[:], sq[:, kt % 2, :], start=(kt == 0), stop=(kt == KT - 1)).then_inc(summed, 1)

            @block.vector
            def _(dve):
                step = Steps(dve, stepped)
                dve.memset(eps[:], EPS).then_inc(eps_set, 1)
                for n in range(0, 16, 2):
                    dve.wait_ge(turned, n + 1)
                    dve.tensor_copy(dst(n // 4, n % 4), ps_x[n % 4][:]).then_inc(copied_dve, 1)
                dve.wait_ge(rows_turned, 1)
                step(dve.tensor_copy(cols[:], ps_r[:, 0:5 * KT]))
                for r in range(2):
                    step(dve.scalar_tensor_tensor(gain[:, r, :], cols[:, (2 + 2 * r) * KT:(3 + 2 * r) * KT], 1.0,
                                                  cols[:, 0:KT], ALU.add, ALU.mult))
                dve.wait_ge(rooted, 1)
                step(dve.reciprocal(rstd[:], rstd[:]))
                for kt in range(KT):
                    for r, (src, tok) in enumerate(tokens(kt)):
                        step(dve.scalar_tensor_tensor(g.h[:, kt, tok], src, gain[:, r, kt:kt + 1], rstd[:, tok],
                                                      ALU.mult, ALU.mult))
                        step(dve.tensor_scalar(g.h[:, kt, tok], g.h[:, kt, tok],
                                               cols[:, (1 + 2 * r) * KT + kt:(1 + 2 * r) * KT + kt + 1], None, ALU.add))

            @block.scalar
            def _(act):
                for n in range(1, 16, 2):
                    act.wait_ge(turned, n + 1)
                    act.activation(dst(n // 4, n % 4), ps_x[n % 4][:], ACT.Copy).then_inc(copied_act, 1)
                act.wait_ge(copied_act, 8)
                act.wait_ge(copied_dve, 8)
                for kt in range(KT):
                    if kt >= 2:
                        act.wait_ge(summed, kt - 1)
                    for src, tok in tokens(kt):
                        act.activation(sq[:, kt % 2, tok], src, ACT.Square).then_inc(squared, 1)
                act.wait_ge(summed, KT)
                act.wait_ge(eps_set, 1)
                act.activation(rstd[:], ps_s[:], ACT.Sqrt, bias=eps[:, 0:1], scale=1.0 / D).then_inc(rooted, 1)


def wide_loads(sp, g, n0, source, blocks, width=512):
    with sp.Fori(0, blocks // 2) as i:
        for j in range(8):
            g.ring.load(sp, n0 + j, i, source(2 * i + j // 4, j % 4), 4, width)


def split_products(pe, out, w, x, start, stop):
    pe.matmul(out, w[0], x[0], start=start, stop=False)
    pe.matmul(out, w[0], x[1], start=False, stop=False)
    return pe.matmul(out, w[1], x[0], start=False, stop=stop)


def wide_products(pe, g, n0, act, tokens, blocks, banks, summed, wait_free):
    with pe.Fori(0, blocks // 2) as i:
        for j in range(8):
            b, q = j // 4, j % 4
            g.ring.wait_used(pe, n0 + j, i)
            w = g.ring.parts(n0 + j, 4, 512)
            for ct in range(4):
                if q == 0:
                    wait_free(i, b, ct)
                for k in range(4):
                    kt = 4 * q + k
                    ins = split_products(pe, banks[4 * b + ct][:, 0:tokens], [a[:, k, P * ct:P * ct + P] for a in w],
                                         [a[:, kt, 0:tokens] for a in act], kt == 0, kt == KT - 1)
                if q == 3 and ct < 3:
                    ins.then_inc(summed, 1)
            ins.then_inc(g.ring.done, 1)


def wide_rounds(eng, n0, blocks, split, evacuate, ahead):
    def one(i, following):
        for j in (2, 3, 4):
            split(n0 + j, i)
        evacuate(i, 0, 0)
        split(n0 + 5, i)
        evacuate(i, 0, 1)
        split(n0 + 6, i)
        split(n0 + 7, i)
        following[0]()
        evacuate(i, 1, 0)
        following[1]()
        evacuate(i, 1, 1)

    if blocks > 2:
        with eng.Fori(0, blocks // 2 - 1) as i:
            one(i, [lambda j=j: split(n0 + j, i + 1) for j in range(2)])
    one(blocks // 2 - 1, ahead)


def split_act(s, h, tokens):
    return s.sb("high", [P, KT, tokens], F32R), s.sb("low", [P, KT, tokens], F32R), s.sem("act_high"), s.sem("act_low")


def split_act_high(act, h, parts):
    for q in range(4):
        act.activation(parts[0][:, 4 * q:4 * q + 4, :], h[:, 4 * q:4 * q + 4, :], ACT.Copy).then_inc(parts[2], 1)


def split_act_low(dve, h, parts):
    for q in range(4):
        dve.wait_ge(parts[2], q + 1)
        dve.tensor_tensor(parts[1][:, 4 * q:4 * q + 4, :], h[:, 4 * q:4 * q + 4, :], parts[0][:, 4 * q:4 * q + 4, :], ALU.subtract)\
           .then_inc(parts[3], 1)


def phase_project(nc, g, name, weights, dst, h, segments, odd):
    with ExitStack() as stack:
        s = Scope(nc, stack, name)
        g.ring.place_parts(s)
        stage = s.sb("stage", [P, 8, TOK])
        banks = [s.ps(f"bank{i}", [P, TOK]) for i in range(8)]
        summed, staged_dve, staged_act = s.sem("summed"), s.sem("staged_dve"), s.sem("staged_act")
        stored = [s.sem(f"stored{i}") for i in range(8)]
        staged = (staged_dve, staged_act)
        starts, done = [], 0
        for _, blocks, _ in segments:
            starts.append((g.ring.take(4 * blocks), done))
            done += blocks
        tiles, chunks = [], []
        for c0, width, tokens in odd:
            per = 4 if width > P else KT
            n = g.ring.take(KT // per)
            chunks.append((n, c0, width, per))
            tiles.append([(len(sum(tiles, [])) + k, min(P, width - k * P), c0 + k * P, k * P, tokens) for k in range(-(-width // P))])
        assert len(sum(tiles, [])) <= 8 and done % 2 == 0
        w = weights.rearrange("(k p) n -> p k n", p=P)
        parts = split_act(s, h, h.shape[2])

        def source(c0):
            return lambda b, q: w[:, 4 * q:4 * q + 4, bass.ds(c0 + b * 512, 512)]

        def evacuate(eng, mine, copy, split, store=None):
            sizes = [4 * 512] * 4 * done + sum([[per * width] * (KT // per) for _, _, width, per in chunks], [])
            first = starts[0][0]

            def chunk(n, i=0):
                split(eng, n, i, sizes[n - first])

            chunk(first)
            chunk(first + 1)
            for k, ((c0, blocks, tokens), (n0, base)) in enumerate(zip(segments, starts)):

                def half(i, b, part):
                    ct = mine + 2 * part
                    if ct < 3:
                        eng.wait_ge(summed, 3 * base + 6 * i + 3 * b + ct + 1)
                    else:
                        g.ring.wait_done(eng, n0 + 4 * b + 3, i)
                    eng.wait_ge(stored[4 * b + ct], 16 * i + 8 * base + 16)
                    copy(stage[:, 4 * b + ct, 0:tokens], banks[4 * b + ct][:, 0:tokens]).then_inc(staged[mine], 1)
                    if store:
                        for ct in (2 * part, 2 * part + 1):
                            eng.wait_ge(staged[ct % 2], 4 + 2 * base + 4 * i + 2 * b + part + 1)
                            store(dst[bass.ds(i * 1024 + (c0 + b * 512 + ct * P), P), 0:tokens],
                                  stage[:, 4 * b + ct, 0:tokens]).then_inc(stored[4 * b + ct], 16)

                following = n0 + 4 * blocks
                wide_rounds(eng, n0, blocks, chunk, half,
                            [(lambda n=n: chunk(n)) if n < first + len(sizes) else (lambda: None) for n in (following, following + 1)])
            for n in range(first + 4 * done + 2, first + len(sizes)):
                chunk(n)
            counts = 3 * done
            for (n, _, _, per), group in zip(chunks, tiles):
                for bank, m, _, _, tokens in group:
                    last = (bank, m) == group[-1][0:2]
                    counts += not last
                    if bank % 2 != mine:
                        continue
                    if last:
                        g.ring.wait_done(eng, n + KT // per - 1, 0)
                    else:
                        eng.wait_ge(summed, counts)
                    eng.wait_ge(stored[bank], 16 + 8 * done)
                    copy(stage[0:m, bank, 0:tokens], banks[bank][0:m, 0:tokens]).then_inc(staged[mine], 1)
            if store:
                for bank, m, r0, _, tokens in sum(tiles, []):
                    eng.wait_ge(staged[bank % 2], 4 + 2 * done + bank // 2 + 1)
                    store(dst[r0:r0 + m, 0:tokens], stage[0:m, bank, 0:tokens]).then_inc(stored[bank], 16)
                for bank in range(8):
                    eng.wait_ge(stored[bank], 16 + 8 * done + 16 * (bank < len(sum(tiles, []))))

        with nc.Block() as block:

            @block.sync
            def _(sp):
                for (c0, blocks, _), (n0, _) in zip(segments, starts):
                    wide_loads(sp, g, n0, source(c0), blocks)
                for n, c0, width, per in chunks:
                    for j in range(KT // per):
                        g.ring.load(sp, n + j, 0, w[:, per * j:per * j + per, c0:c0 + width], per, width)

            @block.tensor
            def _(pe):
                pe.wait_ge(parts[3], 4)
                for (_, blocks, tokens), (n0, base) in zip(segments, starts):
                    wide_products(pe, g, n0, parts[0:2], tokens, blocks, banks, summed,
                                  lambda i, b, ct, base=base: pe.wait_ge(staged[ct % 2], base * 2 + 4 * i + 2 * b + ct // 2 + 1))
                for (n, _, width, per), group in zip(chunks, tiles):
                    for j in range(KT // per):
                        g.ring.wait_used(pe, n + j, 0)
                        wj = g.ring.parts(n + j, per, width)
                        for bank, m, _, off, tokens in group:
                            if j == 0:
                                pe.wait_ge(staged[bank % 2], 2 * done + bank // 2 + 1)
                            for k in range(per):
                                kt = per * j + k
                                ins = split_products(pe, banks[bank][0:m, 0:tokens], [a[:, k, off:off + m] for a in wj],
                                                     [a[:, kt, 0:tokens] for a in parts[0:2]], kt == 0, kt == KT - 1)
                            if kt == KT - 1 and bank != group[-1][0]:
                                ins.then_inc(summed, 1)
                        ins.then_inc(g.ring.done, 1)

            @block.vector
            def _(dve):
                dve.sem_inc(staged_dve, 4)
                split_act_low(dve, h, parts)
                evacuate(dve, 0, lambda o, i: dve.tensor_copy(o, i), g.ring.split_low)

            @block.scalar
            def _(act):
                act.sem_inc(staged_act, 4)
                for i in range(8):
                    act.sem_inc(stored[i], 16)
                split_act_high(act, h, parts)
                evacuate(act, 1, lambda o, i: act.activation(o, i, ACT.Copy), g.ring.split_high, act.dma_start)


def deep_loads(sp, g, n0, w, k_tiles):
    if k_tiles // 8:
        with sp.Fori(0, k_tiles // 8) as i:
            for j in range(8):
                g.ring.load(sp, n0 + j, i, w[bass.ds(i * 1024 + j * P, P), :].unsqueeze(1), 1, D)
    for j in range(k_tiles // 8 * 8, k_tiles):
        g.ring.load(sp, n0 + j, 0, w[j * P:(j + 1) * P, :].unsqueeze(1), 1, D)


def deep_splits(eng, split, n0, act, k_tiles):
    if k_tiles // 8:
        with eng.Fori(0, k_tiles // 8) as i:
            for j in range(8):
                split(eng, n0 + j, i, D, act[:, bass.ds(8 * i + j, 1), :].rearrange("p a t -> p (a t)"))
    for j in range(k_tiles // 8 * 8, k_tiles):
        split(eng, n0 + j, 0, D, act[:, j, :])


def deep_products(pe, g, n0, k_tiles, banks, zeros):
    for b in banks:
        pe.matmul(b[:, 0:2], zeros, zeros[:, 0:2], start=True, stop=False, skip_group_check=True)

    def k_tile(n, i):
        g.ring.wait_used(pe, n, i)
        w = g.ring.parts(n, 1, D)
        x = [t[:, n % SPLITS, :] for t in (g.ring.x_high, g.ring.x_low)]
        for ct in range(KT):
            out = banks[ct // 2][:, LAT * (ct % 2):LAT * (ct % 2) + LAT]
            for a, b in ((0, 0), (0, 1), (1, 0)):
                ins = pe.matmul(out, w[a][:, 0, P * ct:P * ct + P], x[b], start=False, stop=False, skip_group_check=True)
        ins.then_inc(g.ring.done, 1)

    with pe.Fori(0, k_tiles // 8) as i:
        for j in range(8):
            k_tile(n0 + j, i)
    for j in range(k_tiles // 8 * 8, k_tiles):
        k_tile(n0 + j, 0)


def phase_norm(nc, g, name, vectors, out, cols, modulated):
    count = len(vectors) * KT
    with ExitStack() as stack:
        s = Scope(nc, stack, name)
        rows = s.sb("rows", [count, P])
        gain = s.sb("gain", [P, KT])
        sq = s.sb("sq", [P, 4, 4, LAT])
        rstd = s.sb("rstd", [P, LAT])
        eps = s.sb("eps", [P, 1])
        ps_s, ps_r = s.ps("ps_s", [P, 512]), s.ps("ps_r", [P, 512])
        rows_in, turned, squared, summed, rooted, stepped, eps_set = (s.sem(n) for n in (
            "rows_in", "turned", "squared", "summed", "rooted", "stepped", "eps_set"))

        with nc.Block() as block:

            @block.sync
            def _(sp):
                for k, v in enumerate(vectors):
                    sp.dma_start(rows[KT * k:KT * (k + 1), :], v.rearrange("(k p) -> k p", p=P)).then_inc(rows_in, 16)

            @block.tensor
            def _(pe):
                pe.wait_ge(rows_in, 16 * len(vectors))
                pe.transpose(ps_r[:, 0:count], rows[:], g.ident[0:count, 0:count]).then_inc(turned, 1)
                for q in range(4):
                    pe.wait_ge(squared, q + 1)
                    for k in range(4):
                        ins = pe.matmul(ps_s[:, 0:LAT], g.ones[:], sq[:, q, k, :], start=(q + k == 0), stop=(q + k == 6))
                ins.then_inc(summed, 1)

            @block.scalar
            def _(act):
                for q in range(4):
                    act.activation(sq[:, q], g.x_t[:, 4 * q:4 * q + 4, :], ACT.Square).then_inc(squared, 1)
                act.wait_ge(summed, 1)
                act.wait_ge(eps_set, 1)
                act.activation(rstd[:], ps_s[:, 0:LAT], ACT.Sqrt, bias=eps[:, 0:1], scale=1.0 / D).then_inc(rooted, 1)

            @block.vector
            def _(dve):
                step = Steps(dve, stepped)
                dve.memset(eps[:], EPS).then_inc(eps_set, 1)
                dve.wait_ge(turned, 1)
                step(dve.tensor_copy(cols[:], ps_r[:, 0:count]))
                if modulated:
                    step(dve.scalar_tensor_tensor(gain[:], cols[:, 2 * KT:3 * KT], 1.0, cols[:, 0:KT], ALU.add, ALU.mult))
                else:
                    step(dve.tensor_copy(gain[:], cols[:, 0:KT]))
                dve.wait_ge(rooted, 1)
                step(dve.reciprocal(rstd[:], rstd[:]))
                for kt in range(KT):
                    step(dve.scalar_tensor_tensor(out[:, kt, :], g.x_t[:, kt, :], gain[:, kt:kt + 1], rstd[:], ALU.mult, ALU.mult))
                if modulated:
                    for kt in range(KT):
                        step(dve.tensor_scalar(out[:, kt, :], out[:, kt, :], cols[:, KT + kt:KT + kt + 1], None, ALU.add))


def phase_merge(nc, g):
    with ExitStack() as stack:
        s = Scope(nc, stack, "me")
        g.ring.place_parts(s)
        gates = s.sb("gates", [P, 2, KT, LAT])
        m = s.sb("m", [P, KT, LAT])
        t = s.sb("t", [P, 2, LAT])
        rows, cols = s.sb("rows", [KT, P]), s.sb("cols", [P, KT])
        zeros = s.sb("zeros", [P, P])
        banks = [s.ps(f"bank{i}", [P, 512]) for i in range(8)]
        gates_in, rows_in, gates_bent, stepped, zeroed, turned, cols_done, read, merged = (s.sem(n) for n in (
            "gates_in", "rows_in", "gates_bent", "stepped", "zeroed", "turned", "cols_done", "read", "merged"))
        n_a, n_b, n_o = g.ring.take(8), g.ring.take(8), g.ring.take(KT)

        with nc.Block() as block:

            @block.sync
            def _(sp):
                deep_loads(sp, g, n_a, g.merge_p_a[0], 8)
                deep_loads(sp, g, n_b, g.merge_p_b[0], 8)
                deep_loads(sp, g, n_o, g.w_out[0], KT)

            @block.scalar
            def _(act):
                act.dma_start(rows[:], g.d_mod[0, 2 * D:3 * D].rearrange("(k p) -> k p", p=P)).then_inc(rows_in, 16)
                for r in range(2):
                    act.dma_start(gates[:, r], g.d_p[GATE0 + r * D:GATE0 + (r + 1) * D, 0:LAT].rearrange("(k p) t -> p k t", p=P))\
                        .then_inc(gates_in, 16)
                act.wait_ge(gates_in, 32)
                for r in range(2):
                    act.activation(gates[:, r], gates[:, r], ACT.Tanh, scale=0.5).then_inc(gates_bent, 1)
                deep_splits(act, g.ring.split_high, n_a, g.o_a, 8)
                deep_splits(act, g.ring.split_high, n_b, g.o_b, 8)
                act.wait_ge(merged, 1)
                deep_splits(act, g.ring.split_high, n_o, m, KT)

            @block.tensor
            def _(pe):
                pe.wait_ge(zeroed, 1)
                pe.wait_ge(rows_in, 16)
                pe.transpose(banks[0][:, 0:KT], rows[:], g.ident[0:KT, 0:KT]).then_inc(turned, 1)
                pe.wait_ge(cols_done, 1)
                deep_products(pe, g, n_a, 8, banks, zeros[:])
                pe.wait_ge(read, 1)
                deep_products(pe, g, n_b, 8, banks, zeros[:])
                pe.wait_ge(merged, 1)
                deep_products(pe, g, n_o, KT, banks, zeros[:])

            @block.vector
            def _(dve):
                step = Steps(dve, stepped)
                dve.memset(zeros[:], 0.0).then_inc(zeroed, 1)
                dve.wait_ge(turned, 1)
                dve.tensor_copy(cols[:], banks[0][:, 0:KT]).then_inc(cols_done, 1)
                dve.wait_ge(cols_done, 1)
                for r, (n, o, then) in enumerate(((n_a, g.o_a, read), (n_b, g.o_b, merged))):
                    dve.wait_ge(gates_bent, 2)
                    step(dve.tensor_scalar(gates[:, r], gates[:, r], 0.5, 0.5, ALU.mult, ALU.add))
                    deep_splits(dve, g.ring.split_low, n, o, 8)
                    g.ring.wait_done(dve, n + 7, 0)
                    for b in range(8):
                        ga = gates[:, r, 2 * b:2 * b + 2, :]
                        out = m[:, 2 * b:2 * b + 2, :]
                        ps = banks[b][:].rearrange("p (k t) -> p k t", k=2)
                        if r == 0:
                            step(dve.tensor_tensor(out, ga, ps, ALU.mult))
                        else:
                            step(dve.tensor_tensor(ga, ga, ps, ALU.mult))
                            step(dve.tensor_tensor(out, out, ga, ALU.add))
                    dve.sem_inc(then, 1)
                deep_splits(dve, g.ring.split_low, n_o, m, KT)
                g.ring.wait_done(dve, n_o + KT - 1, 0)
                add_scaled(dve, step, g, banks, cols)


def add_scaled(dve, step, g, banks, cols):
    for kt in range(KT):
        ps = banks[kt // 2][:, LAT * (kt % 2):LAT * (kt % 2) + LAT]
        x = g.x_t[:, kt, :]
        if cols is None:
            step(dve.tensor_tensor(x, x, ps, ALU.add))
        else:
            step(dve.scalar_tensor_tensor(x, ps, cols[:, kt:kt + 1], x, ALU.mult, ALU.add))


def phase_ffn(nc, g, name, h, w_up, w_down, hidden, gated, cols):
    tiles = hidden // P
    blocks = tiles // (2 if gated else 4)
    with ExitStack() as stack:
        s = Scope(nc, stack, name)
        g.ring.place_parts(s)
        hid = s.sb("hid", [P, tiles, LAT])
        zeros = s.sb("zeros", [P, P])
        t = s.sb("t", [P, 8, LAT])
        banks = [s.ps(f"bank{i}", [P, 512]) for i in range(8)]
        summed, bent, gate_done, hidden_done, stepped, zeroed = (s.sem(n) for n in (
            "summed", "bent", "gate_done", "hidden_done", "stepped", "zeroed"))
        n_up, n_down = g.ring.take(4 * blocks), g.ring.take(tiles)
        v = w_up.rearrange("(k p) n -> p k n", p=P)
        parts = split_act(s, h, LAT)

        def up_columns(b, q):
            return v[:, 4 * q:4 * q + 4, bass.ds(b * 512, 512)]

        def load_up(sp):
            if not gated:
                return wide_loads(sp, g, n_up, up_columns, blocks)
            with sp.Fori(0, blocks // 2) as i:
                for j in range(8):
                    g.ring.load(sp, n_up + j, i, v[:, 4 * (j % 4):4 * (j % 4) + 4,
                                                   bass.ds(i * 512 + (j // 4) * hidden, 512)], 4, 512)

        def wait_free(pe, i, b, ct):
            if gated:
                pe.wait_ge((gate_done, hidden_done)[b], 4 * i + ct + 1)
            else:
                pe.wait_ge(hidden_done, 8 * i + 4 * b + ct + 1)

        with nc.Block() as block:

            @block.sync
            def _(sp):
                load_up(sp)
                deep_loads(sp, g, n_down, w_down, tiles)

            @block.tensor
            def _(pe):
                pe.wait_ge(parts[3], 4)
                wide_products(pe, g, n_up, parts[0:2], LAT, blocks, banks, summed, lambda i, b, ct: wait_free(pe, i, b, ct))
                pe.wait_ge(zeroed, 1)
                pe.wait_ge(hidden_done, tiles + (4 if gated else 8))
                deep_products(pe, g, n_down, tiles, banks, zeros[:])

            @block.scalar
            def _(act):
                split_act_high(act, h, parts)

                def chunk(n, i=0):
                    g.ring.split_high(act, n, i, 4 * 512)

                def bend(i, b, part):
                    if gated and b:
                        return
                    for ct in (2 * part, 2 * part + 1):
                        if ct < 3:
                            act.wait_ge(summed, 6 * i + 3 * b + ct + 1)
                        else:
                            g.ring.wait_done(act, n_up + 4 * b + 3, i)
                        act.wait_ge(hidden_done, (4 if gated else 8) * i + 4 * b + ct + 1)
                        act.activation(t[:, 4 * b + ct, :], banks[4 * b + ct][:, 0:LAT],
                                       ACT.Tanh if gated else ACT.Relu, scale=0.5 if gated else 1.0).then_inc(bent, 1)

                chunk(n_up)
                chunk(n_up + 1)
                wide_rounds(act, n_up, blocks, chunk, bend, [lambda: None] * 2)
                act.wait_ge(hidden_done, tiles + (4 if gated else 8))
                deep_splits(act, g.ring.split_high, n_down, hid, tiles)

            @block.vector
            def _(dve):
                dve.memset(zeros[:], 0.0).then_inc(zeroed, 1)
                dve.sem_inc(hidden_done, 4 if gated else 8)
                dve.sem_inc(gate_done, 4)
                split_act_low(dve, h, parts)

                def chunk(n, i=0):
                    g.ring.split_low(dve, n, i, 4 * 512)

                def tile(i, ct):
                    return hid[:, bass.ds(ct + i * (4 if gated else 8), 1), :].rearrange("p a t -> p (a t)")

                def finish(i, b, part):
                    for ct in (2 * part, 2 * part + 1):
                        if not gated:
                            dve.wait_ge(bent, 8 * i + 4 * b + ct + 1)
                            dve.tensor_tensor(tile(i, 4 * b + ct), t[:, 4 * b + ct, :], banks[4 * b + ct][:, 0:LAT], ALU.mult)\
                               .then_inc(hidden_done, 1)
                        elif b == 0:
                            dve.wait_ge(bent, 4 * i + ct + 1)
                            dve.scalar_tensor_tensor(t[:, ct, :], t[:, ct, :], 1.0, banks[ct][:, 0:LAT], ALU.add, ALU.mult)\
                               .then_inc(gate_done, 1)
                        else:
                            dve.wait_ge(gate_done, 4 * i + ct + 5)
                            if ct < 3:
                                dve.wait_ge(summed, 6 * i + ct + 4)
                            else:
                                g.ring.wait_done(dve, n_up + 7, i)
                            dve.scalar_tensor_tensor(tile(i, ct), t[:, ct, :], 0.5, banks[4 + ct][:, 0:LAT], ALU.mult, ALU.mult)\
                               .then_inc(hidden_done, 1)

                chunk(n_up)
                chunk(n_up + 1)
                wide_rounds(dve, n_up, blocks, chunk, finish, [lambda: None] * 2)
                deep_splits(dve, g.ring.split_low, n_down, hid, tiles)
                g.ring.wait_done(dve, n_down + tiles - 1, 0)
                step = Steps(dve, stepped)
                add_scaled(dve, step, g, banks, cols)


def phase_out(nc, g, h):
    with ExitStack() as stack:
        s = Scope(nc, stack, "out")
        o = s.sb("o", [P, 2, D])
        ps = [s.ps(f"ps{i}", [P, 512]) for i in range(2)]
        turned, copied, stored = s.sem("turned"), s.sem("copied"), s.sem("stored")
        with nc.Block() as block:

            @block.tensor
            def _(pe):
                for n in range(8):
                    t, q = n // 4, n % 4
                    if n >= 2:
                        pe.wait_ge(copied, n - 1)
                    for k in range(4):
                        ins = pe.transpose(ps[n % 2][:, P * k:P * k + P], h[:, 4 * q + k, t * P:(t + 1) * P], g.ident[:])
                    ins.then_inc(turned, 1)

            @block.vector
            def _(dve):
                for n in range(8):
                    dve.wait_ge(turned, n + 1)
                    dve.tensor_copy(o[:, n // 4, 512 * (n % 4):512 * (n % 4) + 512], ps[n % 2][:]).then_inc(copied, 1)

            @block.sync
            def _(sp):
                for t in range(2):
                    sp.wait_ge(copied, 4 * t + 4)
                    sp.dma_start(g.out[0, t * P:(t + 1) * P, :], o[:, t, :]).then_inc(stored, 16)
                sp.wait_ge(stored, 32)


class Signal:

    def __init__(self, scope, name, per=1):
        self.sem, self.per = scope.sem(name), per

    def wait(self, eng, i, k=1):
        eng.wait_ge(self.sem, self.per * i + k)


class Chain:

    def __init__(self, eng, signal, i):
        self.eng, self.source, self.i, self.n = eng, signal, i, 0

    def __call__(self, ins):
        self.n += 1
        ins.then_inc(self.source.sem, 1)
        self.source.wait(self.eng, self.i, self.n)

    def tell(self, ins, signal, k=1):
        ins.then_inc(signal.sem, 1)
        signal.wait(self.eng, self.i, k)

    def end(self):
        assert self.n == self.source.per, (self.source.sem, self.n)


def shift_mix(dve, step, out, src, co, ctx):
    step(dve.tensor_scalar(out, src, co[:, 0:1], None, ALU.mult))
    og, sg = (a[:, 0:LAT].rearrange("p (r c) -> p r c", c=64) for a in (out, src))
    moves = [(og[:, :, 1:64], sg[:, :, 0:63]), (og[:, :, 0:63], sg[:, :, 1:64]),
             (out[:, 64:LAT], src[:, 0:LAT - 64]), (out[:, 0:LAT - 64], src[:, 64:LAT])]
    if ctx:
        moves += [(out[:, LAT + 1:TOK], src[:, LAT:TOK - 1]), (out[:, LAT:TOK - 1], src[:, LAT + 1:TOK])]
    for k, (o, s) in enumerate(moves):
        step(dve.scalar_tensor_tensor(o, s, co[:, k + 1:k + 2], o, ALU.mult, ALU.add))


def phase_lora(nc, g, lora_w, lora_a, lora_g):
    with ExitStack() as stack:
        s = Scope(nc, stack, "lo")
        raw = s.sb("raw", [P, 5, TOK])
        mixed = s.sb("mixed", [P, 2, TOK])
        rows = s.sb("rows", [80, P])
        mu_rows = s.sb("mu_rows", [5, RANK])
        mu = s.sb("mu", [P, 5])
        co = s.sb("co", [P, 5, 7])
        ps_a, ps_b = s.ps("ps_a", [P, 512]), s.ps("ps_b", [P, 512])
        loaded, rows_in, mu_in = s.sem("loaded"), s.sem("rows_in"), s.sem("mu_in")
        turned, stepped, mixed_wd, ones_set, mu_zero = (s.sem(n) for n in ("turned", "stepped", "mixed_wd", "ones_set", "mu_zero"))
        r0 = 3 * RW_W

        with nc.Block() as block:

            @block.sync
            def _(sp):
                for j in range(4):
                    sp.dma_start(raw[0:RANK, j, :], g.d_p[r0 + RANK * j:r0 + RANK * (j + 1), :]).then_inc(loaded, 16)
                sp.dma_start(raw[0:GATE_RANK, 4, 0:LAT], g.d_p[r0 + 4 * RANK:RW_COLS, 0:LAT]).then_inc(loaded, 16)
                for dst, src in ((g.tri, g.c_tri), (g.mid, g.c_mid), (g.mask, g.c_mask), (g.level, g.c_level),
                                 (g.pairs, g.c_pairs), (g.residue, g.c_residue)):
                    sp.dma_start(dst[:], src).then_inc(loaded, 16)

            @block.scalar
            def _(act):
                src = [g.rw_mu[0, 0:RW_W], g.rw_mu[0, RW_W:2 * RW_W], g.rw_mu[0, 2 * RW_W:3 * RW_W],
                       g.rw_a0[0, 0], g.rw_a0[0, 1], g.rw_k_k[0], g.rw_k_a[0], g.rw_r_k[0].rearrange("h c -> (h c)"),
                       g.rw_ln_w[0], g.rw_ln_b[0]]
                for k, v in enumerate(src):
                    act.dma_start(rows[8 * k:8 * k + 8, :], v.rearrange("(a p) -> a p", p=P)).then_inc(rows_in, 16)
                act.wait_ge(mu_zero, 1)
                act.dma_start(mu_rows[0:4, :], g.rw_mu[0, r0:r0 + 4 * RANK].rearrange("(a p) -> a p", p=RANK)).then_inc(mu_in, 16)
                act.dma_start(mu_rows[4:5, 0:GATE_RANK], g.rw_mu[0, r0 + 4 * RANK:RW_COLS].unsqueeze(0)).then_inc(mu_in, 16)
                for d in range(2):
                    act.wait_ge(mixed_wd, d + 1)
                    act.activation(lora_w[0:RANK, d, :], mixed[0:RANK, d, :], ACT.Tanh).then_inc(ones_set, 1)
                act.wait_ge(mixed_wd, 3)
                act.activation(lora_g[0:GATE_RANK, :], lora_g[0:GATE_RANK, :], ACT.Tanh, scale=0.5).then_inc(ones_set, 1)

            @block.tensor
            def _(pe):
                pe.wait_ge(rows_in, 160)
                pe.transpose(ps_a[:, 0:80], rows[:], g.ident[0:80, 0:80]).then_inc(turned, 1)
                pe.wait_ge(mu_in, 32)
                pe.transpose(ps_b[0:RANK, 0:5], mu_rows[:], g.ident[0:5, 0:5]).then_inc(turned, 1)

            @block.vector
            def _(dve):
                step = Steps(dve, stepped)
                dve.memset(mu_rows[:], 0.0).then_inc(mu_zero, 1)
                step(dve.memset(lora_w[RANK:RANK + 1, :, :], 1.0))
                dve.wait_ge(turned, 1)
                step(dve.tensor_copy(g.prm[:], ps_a[:, 0:80].rearrange("p (k a) -> p k a", a=8)))
                dve.wait_ge(turned, 2)
                step(dve.tensor_copy(mu[0:RANK, :], ps_b[0:RANK, 0:5]))
                dve.wait_ge(loaded, 16 * 11)
                for j in range(5):
                    m = RANK if j < 4 else GATE_RANK
                    step(dve.tensor_scalar(co[0:m, j, 0:1], mu[0:m, j:j + 1], -1.0, 1.0, ALU.mult, ALU.add))
                    step(dve.tensor_scalar(co[0:m, j, 1:7], g.residue[0:m, :], mu[0:m, j:j + 1], None, ALU.mult))
                    if j == 4:
                        shift_mix(dve, step, lora_g[0:m, :], raw[0:m, 4, 0:LAT], co[0:m, 4, :], False)
                    else:
                        out = mixed[0:m, j, :] if j < 2 else lora_a[0:m, j - 2, :]
                        shift_mix(dve, step, out, raw[0:m, j, :], co[0:m, j, :], True)
                    if j in (0, 1, 4):
                        dve.sem_inc(mixed_wd, 1)
                dve.wait_ge(ones_set, 3)
                step(dve.tensor_scalar(lora_g[0:GATE_RANK, :], lora_g[0:GATE_RANK, :], 0.5, 0.5, ALU.mult, ALU.add))


DECAY = 0.6065306597126334
RW_EPS = 64e-5
LEVELS = (2, 4, 8, 16, 32, 64)


def phase_rwkv(nc, g):
    with ExitStack() as stack:
        s = Scope(nc, stack, "rw")
        lora_w = s.sb("lora_w", [RANK + 1, 2, TOK])
        lora_a = s.sb("lora_a", [RANK, 2, TOK])
        lora_g = s.sb("lora_g", [GATE_RANK, LAT])
        g.prm, g.mid, g.pairs, g.residue = (s.sb(n, sh) for n, sh in (
            ("prm", [P, 10, 8]), ("mid", [P, 2]), ("pairs", [P, P]), ("residue", [P, 6])))
        phase_lora(nc, g, lora_w, lora_a, lora_g)

        raw = {"r": s.sb("raw_r", [P, LAT]), "k": s.sb("raw_k", [P, TOK]), "v": s.sb("raw_v", [P, TOK])}
        mix = {"r": s.sb("mix_r", [P, LAT]), "k": s.sb("mix_k", [P, TOK]), "v": s.sb("mix_v", [P, TOK])}
        w2, a2, g2 = s.sb("w2", [RANK + 1, 2, P]), s.sb("a2", [RANK, 2, P]), s.sb("g2", [GATE_RANK, P])
        cur = s.sb("cur", [P, 13])
        co = s.sb("co", [P, 3, 7])
        kk = s.sb("kk", [P, TOK])
        tmp = s.sb("tmp", [P, TOK])
        iclr = s.sb("iclr", [P, 2, TOK])
        kdir = s.sb("kdir", [P, 2, TOK])
        logw = s.sb("logw", [P, 2, 4, P])
        gate = s.sb("gate", [P, LAT])
        bonus = s.sb("bonus", [P, LAT])
        e_in, e_neg, e_ex = (s.sb(n, [P, 4, P]) for n in ("e_in", "e_neg", "e_ex"))
        e_mid = s.sb("e_mid", [P, 4])
        carry = s.sb("carry", [P, 3])
        kk_s, b_s, k_s, v_s = (s.sb(n, [P, 4, P]) for n in ("kk_s", "b_s", "k_s", "v_s"))
        r_s = s.sb("r_s", [P, 2, P])
        k_tok, b_tok, v_tok = (s.sb(n, [P, 4, P]) for n in ("k_tok", "b_tok", "v_tok"))
        a_t = [e_in, s.sb("a_t1", [P, 4, P])]
        n_t = [e_neg, s.sb("n_t1", [P, 4, P])]
        m_t = [e_ex, s.sb("m_t1", [P, 4, P])]
        inv = [s.sb(f"inv{h}", [P, 4, P]) for h in range(2)]
        inv_t = [s.sb(f"inv_t{h}", [P, 4, P]) for h in range(2)]
        inv2 = [s.sb(f"inv2_{h}", [P, 4, P]) for h in range(2)]
        inv2_t = [s.sb(f"inv2_t{h}", [P, 4, P]) for h in range(2)]
        grown = [[s.sb(f"grown{h}_{n}", [P, 4, P]) for n in LEVELS] for h in range(2)]
        rhs, u, state = (s.sb(n, [P, P]) for n in ("rhs", "u", "state"))
        y = s.sb("y", [P, LAT])
        eps = s.sb("eps", [P, 2])
        held = s.sb("held", [1, 1])
        bank = [s.ps(f"bank{b}", [P, 512]) for b in range(8)]
        b4 = [b[:].rearrange("p (c t) -> p c t", c=4) for b in bank]

        pair_loaded = s.sem("pair_loaded")
        (v_step, a_step, shifted, k_squared, k_summed, k_rooted, lora_summed, lora_bent, decay_logged, gate_copied,
         decay_summed, exps_done, scaled, bonus_in, bonus_summed, turned, turned_copied, products, at_copied, products_masked,
         inv2_ready, x_summed, x_masked, t_summed, t_copied, r_summed, r_copied, u_summed, u_copied, s_summed,
         s_ready, y_summed, y_added, stats_in, stats_summed, var_rooted, round_done, x_filled) = (
            Signal(s, n, per) for n, per in (
                ("v_step", 93), ("a_step", 6), ("shifted", 1), ("k_squared", 1), ("k_summed", 1), ("k_rooted", 1),
                ("lora_summed", 5), ("lora_bent", 4), ("decay_logged", 2), ("gate_copied", 1), ("decay_summed", 2),
                ("exps_done", 2), ("scaled", 2), ("bonus_in", 1), ("bonus_summed", 1), ("turned", 2),
                ("turned_copied", 6), ("products", 16), ("at_copied", 4), ("products_masked", 8), ("inv2_ready", 8),
                ("x_summed", 24), ("x_masked", 24), ("t_summed", 44), ("t_copied", 44), ("r_summed", 8), ("r_copied", 8),
                ("u_summed", 8), ("u_copied", 8), ("s_summed", 6), ("s_ready", 6), ("y_summed", 4), ("y_added", 4),
                ("stats_in", 2), ("stats_summed", 2), ("var_rooted", 1), ("round_done", 3), ("x_filled", 1)))

        def end_round(eng, i):
            round_done.wait(eng, i, 3)

        def seq(ap, d, n, count=1):
            out = []
            for m in range(n, n + count):
                c = (2, 3, 0, 1)[m] if d == 0 else (3, 2, 1, 0)[m]
                out.append(ap[:, c * P:(c + 1) * P] if d == 0 else ap[:, c * P:(c + 1) * P][:, ::-1])
            return out

        with nc.Block() as block:

            @block.sync
            def _(sp):
                def load(i):
                    rows = bass.ds(i * P, P)
                    sp.dma_start(raw["r"][:], g.d_p[rows, 0:LAT]).then_inc(pair_loaded, 16)
                    sp.dma_start(raw["k"][:], g.d_p[bass.ds(i * P + RW_W, P), :]).then_inc(pair_loaded, 16)
                    sp.dma_start(raw["v"][:], g.d_p[bass.ds(i * P + 2 * RW_W, P), :]).then_inc(pair_loaded, 16)
                    sp.dma_start(w2[0:RANK, :, :], g.rw_w2[0].rearrange("d r c -> r d c")[:, :, rows]).then_inc(pair_loaded, 16)
                    sp.dma_start(w2[RANK:RANK + 1, :, :], g.rw_w0[:, :, rows]).then_inc(pair_loaded, 16)
                    sp.dma_start(a2[:], g.rw_a2[0].rearrange("d r c -> r d c")[:, :, rows]).then_inc(pair_loaded, 16)
                    sp.dma_start(g2[:], g.rw_g2[0][:, rows]).then_inc(pair_loaded, 16)

                load(0)
                with sp.Fori(0, 7) as i:
                    shifted.wait(sp, i)
                    lora_summed.wait(sp, i, 5)
                    load(i + 1)

            @block.tensor
            def _(pe):
                with pe.Fori(0, 8) as i:
                    pe.wait_ge(pair_loaded, 112 * i + 112)
                    for d in range(2):
                        pe.matmul(bank[1 + d][:], a2[:, d, :], lora_a[:, d, :], start=True, stop=True).then_inc(lora_summed.sem, 1)
                    for d in range(2):
                        for c in range(4):
                            ch = (2, 3, 0, 1)[c] if d == 0 else (3, 2, 1, 0)[c]
                            ins = pe.matmul(b4[3 + d][:, c, :], lora_w[:, d, ch * P:(ch + 1) * P], w2[:, d, :], start=True, stop=True)
                        ins.then_inc(lora_summed.sem, 1)
                    pe.matmul(bank[5][:, 0:LAT], g2[:], lora_g[:], start=True, stop=True).then_inc(lora_summed.sem, 1)
                    k_squared.wait(pe, i)
                    pe.matmul(bank[0][:], g.pairs[:], tmp[:], start=True, stop=True).then_inc(k_summed.sem, 1)
                    bonus_in.wait(pe, i)
                    pe.matmul(bank[6][:, 0:LAT], g.pairs[:], tmp[:, 0:LAT], start=True, stop=True).then_inc(bonus_summed.sem, 1)
                    for d in range(2):
                        decay_logged.wait(pe, i, d + 1)
                        if d == 0:
                            k_rooted.wait(pe, i)
                            lora_bent.wait(pe, i, 4)
                        else:
                            y_added.wait(pe, i, 2)
                        for c in range(4):
                            pe.matmul(b4[0][:, c, :], logw[:, d, c, :], g.tri[:, d, 0, :], start=True, stop=True)
                            pe.matmul(b4[1][:, c, :], logw[:, d, c, :], g.tri[:, d, 1, :], start=True, stop=True)
                            ins = pe.matmul(bank[2][:, c:c + 1], logw[:, d, c, :], g.mid[:, d:d + 1], start=True, stop=True)
                        ins.then_inc(decay_summed.sem, 1)
                        scaled.wait(pe, i, d + 1)
                        if d == 0:
                            gate_copied.wait(pe, i)
                        for b, src in ((3, k_s), (4, b_s), (5, v_s)):
                            for c in range(4):
                                ins = pe.transpose(b4[b][:, c, :], src[:, c, :], g.ident[:])
                        ins.then_inc(turned.sem, 1)
                        for h in range(2):
                            ch = slice(64 * h, 64 * h + 64)
                            ba = (0, 1, 2, 6) if h == 0 else (3, 4, 5, 7)
                            if h == 0:
                                exps_done.wait(pe, i, d + 1)
                                if d == 0:
                                    gate_copied.wait(pe, i)
                            else:
                                turned_copied.wait(pe, i, 3 * d + 3)
                            for k, (l, r) in enumerate(((b_s, kk_s), (kk_s, b_s), (k_s, kk_s))):
                                for c in range(4):
                                    ins = pe.matmul(b4[ba[k]][:, c, :], l[ch, c, :], r[ch, c, :], start=True, stop=True)
                                ins.then_inc(products.sem, 1)
                            for k, l in enumerate((k_s, b_s)):
                                for c in range(2):
                                    ins = pe.matmul(b4[ba[3]][:, 2 * k + c, :], l[ch, 2 + c, :], r_s[ch, c, :], start=True, stop=True)
                            ins.then_inc(products.sem, 1)
                        for lv, _ in enumerate(LEVELS):
                            for h in range(2):
                                ba = (0, 1, 2) if h == 0 else (3, 4, 5)
                                if lv == 0:
                                    at_copied.wait(pe, i, 2 * d + h + 1)
                                    inv2_ready.wait(pe, i, 4 * d + 2 * h + 2)
                                    products_masked.wait(pe, i, 4 * d + 2 * h + 1)
                                else:
                                    t_copied.wait(pe, i, 22 * d + 4 * lv + 2 * h - 2)
                                    x_masked.wait(pe, i, 12 * d + 2 * lv + h - 1)
                                src = inv2[h] if lv == 0 else inv[h]
                                for c in range(4):
                                    ins = pe.matmul(b4[ba[0]][:, c, :], a_t[h][:, c, :], src[:, c, :], start=True, stop=True)
                                ins.then_inc(x_summed.sem, 1)
                            for h in range(2):
                                ba = (0, 1, 2) if h == 0 else (3, 4, 5)
                                src_t = inv2_t[h] if lv == 0 else inv_t[h]
                                x_masked.wait(pe, i, 12 * d + 2 * lv + h + 1)
                                if lv < 5:
                                    for c in range(4):
                                        ins = pe.matmul(b4[ba[1]][:, c, :], src_t[:, c, :], grown[h][lv][:, c, :], start=True, stop=True)
                                    ins.then_inc(t_summed.sem, 1)
                                for c in range(4):
                                    ins = pe.matmul(b4[ba[2]][:, c, :], grown[h][lv][:, c, :], src_t[:, c, :], start=True, stop=True)
                                ins.then_inc(t_summed.sem, 1)
                        for n in range(4):
                            last = n == 3
                            if n == 0:
                                t_copied.wait(pe, i, 22 * d + 22)
                                products_masked.wait(pe, i, 4 * d + 4)
                            else:
                                s_ready.wait(pe, i, 3 * d + n)
                                pe.matmul(bank[0][:, 0:P], kk_s[:, n, :], state[:], start=True, stop=False, skip_group_check=True)
                            for h in range(2):
                                ins = pe.matmul(bank[0][:, 64 * h:64 * h + 64], n_t[h][:, n, :], v_tok[:, n, 64 * h:64 * h + 64],
                                                start=(n == 0), stop=(h == 1), skip_group_check=True)
                            ins.then_inc(r_summed.sem, 1)
                            r_copied.wait(pe, i, 4 * d + n + 1)
                            for h in range(2):
                                ins = pe.matmul(bank[1][:, 64 * h:64 * h + 64], inv_t[h][:, n, :], rhs[:, 64 * h:64 * h + 64],
                                                start=True, stop=True, skip_group_check=True)
                            ins.then_inc(u_summed.sem, 1)
                            u_copied.wait(pe, i, 4 * d + n + 1)
                            if not last:
                                pe.matmul(bank[2][:, 0:P], k_tok[:, n, :], v_tok[:, n, :], start=True, stop=False)
                                pe.matmul(bank[2][:, 0:P], b_tok[:, n, :], u[:], start=False, stop=True).then_inc(s_summed.sem, 1)
                            if n >= 2:
                                yb = bank[4 + n]
                                pe.matmul(yb[:, 0:P], state[:], r_s[:, n - 2, :], start=True, stop=False, skip_group_check=True)
                                for h in range(2):
                                    ch = slice(64 * h, 64 * h + 64)
                                    pe.matmul(yb[ch, 0:P], v_tok[:, n, ch], m_t[h][:, n - 2, :], start=False, stop=False, skip_group_check=True)
                                    ins = pe.matmul(yb[ch, 0:P], u[:, ch], m_t[h][:, n, :], start=False, stop=(h == 1), skip_group_check=True)
                                ins.then_inc(y_summed.sem, 1)
                    stats_in.wait(pe, i, 1)
                    pe.matmul(bank[0][:, 0:LAT], g.pairs[:], y[:], start=True, stop=True).then_inc(stats_summed.sem, 1)
                    stats_in.wait(pe, i, 2)
                    pe.matmul(bank[1][:, 0:LAT], g.pairs[:], tmp[:, 0:LAT], start=True, stop=True).then_inc(stats_summed.sem, 1)
                    end_round(pe, i)

            @block.scalar
            def _(act):
                x_filled.wait(act, 0)
                with act.Fori(0, 8) as i:
                    step = Chain(act, a_step, i)
                    k_summed.wait(act, i)
                    act.activation(kk_s[:].rearrange("p c t -> p (c t)"), bank[0][:], ACT.Sqrt, bias=eps[:, 0:1]).then_inc(k_rooted.sem, 1)
                    for d in range(2):
                        lora_summed.wait(act, i, d + 1)
                        act.activation(iclr[:, d, :], bank[1 + d][:], ACT.Tanh, scale=0.5, bias=cur[:, 10 + d:11 + d]).then_inc(lora_bent.sem, 1)
                    for d in range(2):
                        lora_summed.wait(act, i, d + 3)
                        act.activation(logw[:, d], b4[3 + d][:], ACT.Tanh, scale=0.5).then_inc(lora_bent.sem, 1)
                    for d in range(2):
                        decay_summed.wait(act, i, d + 1)
                        act.activation(e_mid[:], bank[2][:, 0:4], ACT.Exp).then_inc(a_step.sem, 1)
                        act.activation(e_in[:], b4[0][:], ACT.Exp).then_inc(a_step.sem, 1)
                        act.activation(e_neg[:], b4[0][:], ACT.Exp, scale=-1.0).then_inc(a_step.sem, 1)
                        a_step.wait(act, i, 3 * d + 3)
                        act.activation(e_ex[:], b4[1][:], ACT.Exp).then_inc(exps_done.sem, 1)
                        turned.wait(act, i, d + 1)
                        for k, (b, dst) in enumerate(((3, k_tok), (4, b_tok), (5, v_tok))):
                            act.activation(dst[:], b4[b][:], ACT.Copy).then_inc(turned_copied.sem, 1)
                        for h in range(2):
                            products.wait(act, i, 8 * d + 4 * h + 1)
                            inv2_ready.wait(act, i, 4 * d + 2 * h + 1)
                            act.activation(a_t[h][:], b4[3 * h][:], ACT.Copy).then_inc(at_copied.sem, 1)
                        for lv in range(6):
                            for h in range(2):
                                if lv < 5:
                                    t_summed.wait(act, i, 22 * d + 4 * lv + 2 * h + 2)
                                    act.activation(inv[h][:], b4[3 * h + 1][:], ACT.Copy).then_inc(t_copied.sem, 1)
                                else:
                                    t_summed.wait(act, i, 22 * d + 20 + h + 1)
                                act.activation(inv_t[h][:], b4[3 * h + 2][:], ACT.Copy).then_inc(t_copied.sem, 1)
                        for n in range(4):
                            r_summed.wait(act, i, 4 * d + n + 1)
                            act.activation(rhs[:], bank[0][:, 0:P], ACT.Copy).then_inc(r_copied.sem, 1)
                            u_summed.wait(act, i, 4 * d + n + 1)
                            act.activation(u[:], bank[1][:, 0:P], ACT.Copy).then_inc(u_copied.sem, 1)
                    stats_summed.wait(act, i, 2)
                    act.activation(bonus_root(tmp), bank[1][:, 0:LAT], ACT.Sqrt, bias=eps[:, 1:2], scale=1.0 / RW_DIM).then_inc(var_rooted.sem, 1)
                    var_rooted.wait(act, i)
                    act.sem_inc(round_done.sem, 1)
                    end_round(act, i)

            @block.gpsimd
            def _(pool):
                for t in inv2 + inv2_t + grown[0] + grown[1]:
                    for c in range(4):
                        ins = pool.tensor_copy(t[:, c, :], g.ident[:])
                ins.then_inc(x_filled.sem, 1)

            @block.vector
            def _(dve):
                boot = Steps(dve, s.sem("boot"))
                boot(dve.memset(eps[:, 0:1], EPS))
                boot(dve.memset(eps[:, 1:2], RW_EPS))
                x_filled.wait(dve, 0)
                with dve.Fori(0, 8) as i:
                    step = Chain(dve, v_step, i)
                    step(dve.tensor_copy(cur[:, 0:10], g.prm[:, :, bass.ds(i, 1)].rearrange("p k a -> p (k a)")))
                    step(dve.tensor_scalar(cur[:, 10:12], cur[:, 3:5], 0.5, None, ALU.mult))
                    step(dve.tensor_scalar(cur[:, 12:13], cur[:, 6:7], -1.0, 1.0, ALU.mult, ALU.add))
                    for j in range(3):
                        step(dve.tensor_scalar(co[:, j, 0:1], cur[:, j:j + 1], -1.0, 1.0, ALU.mult, ALU.add))
                        step(dve.tensor_scalar(co[:, j, 1:7], g.residue[:], cur[:, j:j + 1], None, ALU.mult))
                    dve.wait_ge(pair_loaded, 112 * i + 112)
                    shift_mix(dve, step, mix["k"][:], raw["k"][:], co[:, 1, :], True)
                    shift_mix(dve, step, mix["v"][:], raw["v"][:], co[:, 2, :], True)
                    shift_mix(dve, step, mix["r"][:], raw["r"][:], co[:, 0, :], False)
                    step.tell(dve.tensor_scalar(kk[:], mix["k"][:], cur[:, 5:6], None, ALU.mult), shifted)
                    step.tell(dve.tensor_tensor(tmp[:], kk[:], kk[:], ALU.mult), k_squared)
                    k_rooted.wait(dve, i)
                    root = kk_s[:].rearrange("p c t -> p (c t)")
                    step(dve.reciprocal(root, root))
                    step(dve.tensor_tensor(kk[:], kk[:], root, ALU.mult))
                    lora_summed.wait(dve, i, 5)
                    step.tell(dve.tensor_copy(gate[:], bank[5][:, 0:LAT]), gate_copied)
                    for d in range(2):
                        lora_bent.wait(dve, i, d + 1)
                        step(dve.tensor_scalar(iclr[:, d, :], iclr[:, d, :], 0.5, 0.5, ALU.mult, ALU.add))
                        step(dve.tensor_scalar(kdir[:, d, :], iclr[:, d, :], cur[:, 6:7], cur[:, 12:13], ALU.mult, ALU.add))
                        step(dve.tensor_tensor(kdir[:, d, :], kdir[:, d, :], mix["k"][:], ALU.mult))
                    step(dve.tensor_tensor(tmp[:, 0:LAT], kdir[:, 0, 0:LAT], kdir[:, 1, 0:LAT], ALU.add))
                    step(dve.scalar_tensor_tensor(tmp[:, 0:LAT], tmp[:, 0:LAT], 0.5, mix["r"][:], ALU.mult, ALU.mult))
                    step.tell(dve.tensor_scalar(tmp[:, 0:LAT], tmp[:, 0:LAT], cur[:, 7:8], None, ALU.mult), bonus_in)
                    for d in range(2):
                        lora_bent.wait(dve, i, d + 3)
                        step.tell(dve.tensor_scalar(logw[:, d], logw[:, d], -0.5 * DECAY, -0.5 * DECAY, ALU.mult, ALU.add),
                                  decay_logged, d + 1)
                    bonus_summed.wait(dve, i)
                    step(dve.tensor_tensor(bonus[:], bank[6][:, 0:LAT], mix["v"][:, 0:LAT], ALU.mult))
                    for d in range(2):
                        exps_done.wait(dve, i, d + 1)
                        step(dve.tensor_tensor(carry[:], e_in[:, 0:3, P - 1], e_mid[:, 1:4], ALU.mult))
                        for n in range(4):
                            kkn, = seq(kk[:], d, n)
                            icn, = seq(iclr[:, d, :], d, n)
                            kdn, = seq(kdir[:, d, :], d, n)
                            vn, = seq(mix["v"][:], d, n)
                            dve.tensor_tensor(kk_s[:, n, :], kkn, e_ex[:, n, :], ALU.mult).then_inc(v_step.sem, 1)
                            dve.scalar_tensor_tensor(b_s[:, n, :], kkn, -1.0, icn, ALU.mult, ALU.mult).then_inc(v_step.sem, 1)
                            dve.tensor_tensor(k_s[:, n, :], kdn, e_neg[:, n, :], ALU.mult).then_inc(v_step.sem, 1)
                            dve.tensor_copy(v_s[:, n, :], vn).then_inc(v_step.sem, 1)
                            step.n += 4
                            v_step.wait(dve, i, step.n)
                            step(dve.tensor_tensor(b_s[:, n, :], b_s[:, n, :], e_neg[:, n, :], ALU.mult))
                        for n in (2, 3):
                            rn, = seq(mix["r"][:], d, n)
                            ins = dve.tensor_tensor(r_s[:, n - 2, :], rn, e_in[:, n, :], ALU.mult)
                            if n == 2:
                                step(ins)
                            else:
                                step.tell(ins, scaled, d + 1)
                        for h in range(2):
                            lo = 3 * h
                            products.wait(dve, i, 8 * d + 4 * h + 1)
                            dve.memset(held[:], 0.0)
                            step.tell(dve.copy_predicated(inv2_t[h][:], g.level[:, 7, :].unsqueeze(1).broadcast_to([P, 4, P]), b4[lo][:]),
                                      inv2_ready, 4 * d + 2 * h + 1)
                            products.wait(dve, i, 8 * d + 4 * h + 2)
                            dve.memset(held[:], 0.0)
                            step.tell(dve.copy_predicated(inv2[h][:], g.level[:, 0, :].unsqueeze(1).broadcast_to([P, 4, P]), b4[lo + 1][:]),
                                      inv2_ready, 4 * d + 2 * h + 2)
                            products.wait(dve, i, 8 * d + 4 * h + 3)
                            step.tell(dve.tensor_tensor(n_t[h][:], b4[lo + 2][:], g.mask[:, 0, :].unsqueeze(1).broadcast_to([P, 4, P]), ALU.mult),
                                      products_masked, 4 * d + 2 * h + 1)
                            products.wait(dve, i, 8 * d + 4 * h + 4)
                            step.tell(dve.tensor_tensor(m_t[h][:], b4[6 + h][:], g.mask[:, 1, :].unsqueeze(1).broadcast_to([P, 4, P]), ALU.mult),
                                      products_masked, 4 * d + 2 * h + 2)
                        for lv in range(6):
                            for h in range(2):
                                x_summed.wait(dve, i, 12 * d + 2 * lv + h + 1)
                                dve.memset(held[:], 0.0)
                                step.tell(dve.copy_predicated(grown[h][lv][:], g.level[:, lv + 1, :].unsqueeze(1).broadcast_to([P, 4, P]),
                                                              b4[3 * h][:]), x_masked, 12 * d + 2 * lv + h + 1)
                        for n in range(4):
                            if n < 3:
                                s_summed.wait(dve, i, 3 * d + n + 1)
                                if n == 0:
                                    step.tell(dve.scalar_tensor_tensor(state[:], bank[2][:, 0:P], carry[:, 0:1], g.pairs[:], ALU.mult, ALU.mult),
                                              s_ready, 3 * d + 1)
                                else:
                                    if n == 2:
                                        y_summed.wait(dve, i, 2 * d + 1)
                                    step(dve.tensor_tensor(state[:], state[:], bank[2][:, 0:P], ALU.add))
                                    step.tell(dve.scalar_tensor_tensor(state[:], state[:], carry[:, n:n + 1], g.pairs[:], ALU.mult, ALU.mult),
                                              s_ready, 3 * d + n + 1)
                            if n >= 2:
                                y_summed.wait(dve, i, 2 * d + n - 1)
                                dst, = seq(y[:], d, n)
                                if d == 0:
                                    ins = dve.tensor_copy(dst, bank[4 + n][:, 0:P])
                                else:
                                    ins = dve.tensor_tensor(dst, dst, bank[4 + n][:, 0:P], ALU.add)
                                step.tell(ins, y_added, 2 * d + n - 1)
                    dve.sem_inc(stats_in.sem, 1)
                    stats_summed.wait(dve, i, 1)
                    step(dve.scalar_tensor_tensor(y[:], bank[0][:, 0:LAT], -1.0 / RW_DIM, y[:], ALU.mult, ALU.add))
                    step.tell(dve.tensor_tensor(tmp[:, 0:LAT], y[:], y[:], ALU.mult), stats_in, 2)
                    var_rooted.wait(dve, i)
                    step(dve.reciprocal(bonus_root(tmp), bonus_root(tmp)))
                    step(dve.tensor_tensor(y[:], y[:], bonus_root(tmp), ALU.mult))
                    step(dve.tensor_scalar(y[:], y[:], cur[:, 8:9], cur[:, 9:10], ALU.mult, ALU.add))
                    step(dve.tensor_tensor(y[:], y[:], bonus[:], ALU.add))
                    step(dve.tensor_tensor(g.o_a[:, bass.ds(i, 1), :].rearrange("p a t -> p (a t)"), y[:], gate[:], ALU.mult))
                    step.end()
                    dve.sem_inc(round_done.sem, 2)
                    end_round(dve, i)


def bonus_root(tmp):
    return tmp[:, LAT:TOK]


def phase_gdn_gates(nc, g, g_seq, gc_seq, be_seq, taps, norm_w):
    with ExitStack() as stack:
        s = Scope(nc, stack, "gg")
        a, b = s.sb("a", [16, TOK]), s.sb("b", [16, TOK])
        t = s.sb("t", [16, TOK])
        par = s.sb("par", [16, 3])
        rows = s.sb("rows", [120, P])
        nrow = s.sb("nrow", [1, P])
        b_seq = s.sb("b_seq", [P, 2, 4, 8])
        ps_g, ps_b, ps_c, ps_t = (s.ps(n, [P, 512]) for n in ("ps_g", "ps_b", "ps_c", "ps_t"))
        loaded, bent, stepped, ready, turned, ordered, summed = (s.sem(n) for n in (
            "loaded", "bent", "stepped", "ready", "turned", "ordered", "summed"))

        with nc.Block() as block:

            @block.sync
            def _(sp):
                for dst, src in ((a[:], g.d_p[AB0:AB0 + 16, :]), (b[:], g.d_p[AB0 + 16:AB0 + 32, :]),
                                 (par[:, 0:1], g.gdn_a_log[0].rearrange("d h -> (d h)").unsqueeze(1)),
                                 (par[:, 1:2], g.gdn_dt_bias[0].rearrange("d h -> (d h)").unsqueeze(1)),
                                 (rows[:], g.gdn_conv_w[0].rearrange("t (a p) -> (t a) p", p=P)),
                                 (nrow[:], g.gdn_norm_w), (g.back[:], g.c_back)):
                    sp.dma_start(dst, src).then_inc(loaded, 16)

            @block.scalar
            def _(act):
                act.wait_ge(loaded, 112)
                act.activation(par[:, 2:3], par[:, 0:1], ACT.Exp).then_inc(bent, 1)
                act.activation(b[:], b[:], ACT.Tanh, scale=0.5).then_inc(bent, 1)
                act.wait_ge(ready, 1)
                act.activation(t[:], t[:], ACT.Exp).then_inc(bent, 1)
                act.wait_ge(ready, 2)
                act.activation(t[:], t[:], ACT.Ln).then_inc(bent, 1)

            @block.vector
            def _(dve):
                step = Steps(dve, stepped)
                dve.wait_ge(loaded, 112)
                step(dve.tensor_scalar(a[:], a[:], par[:, 1:2], None, ALU.add))
                step(dve.tensor_scalar(t[:], a[:], -1.0, None, ALU.mult))
                dve.tensor_tensor(t[:], t[:], a[:], ALU.min).then_inc(ready, 1)
                dve.wait_ge(bent, 3)
                dve.tensor_scalar(t[:], t[:], 1.0, None, ALU.add).then_inc(ready, 1)
                step(dve.tensor_scalar(b[:], b[:], 0.5, 0.5, ALU.mult, ALU.add))
                dve.wait_ge(bent, 4)
                step(dve.scalar_tensor_tensor(a[:], a[:], 0.0, t[:], ALU.max, ALU.add))
                step(dve.tensor_scalar(par[:, 2:3], par[:, 2:3], -1.0, None, ALU.mult))
                dve.tensor_scalar(a[:], a[:], par[:, 2:3], None, ALU.mult).then_inc(ready, 1)
                dve.wait_ge(turned, 1)
                for src, dst in ((ps_g, g_seq), (ps_b, b_seq)):
                    v = src[:, 0:64].rearrange("p (c d h) -> p c d h", c=4, d=2)
                    for d in range(2):
                        for n in range(4):
                            c = (2, 3, 0, 1)[n] if d == 0 else (3, 2, 1, 0)[n]
                            step(dve.tensor_copy(dst[:, d, n, :], v[:, c, d, :]))
                dve.sem_inc(ordered, 1)
                step(dve.tensor_copy(taps[:], ps_t[:, 0:120].rearrange("p (t j a) -> p t j a", t=5, j=3)))
                step(dve.tensor_copy(norm_w[:], ps_t[:, 120:121]))
                dve.wait_ge(summed, 1)
                step(dve.tensor_copy(gc_seq[:], ps_c[:, 0:64].rearrange("p (d n h) -> p d n h", d=2, n=4)))
                step(dve.tensor_copy(be_seq[:], ps_c[:, 64:128].rearrange("p (d n h) -> p d n h", d=2, n=4)))

            @block.tensor
            def _(pe):
                pe.wait_ge(loaded, 112)
                pe.transpose(ps_t[:, 0:120], rows[:], g.ident[0:120, 0:120])
                pe.transpose(ps_t[:, 120:121], nrow[:], g.ident[0:1, 0:1])
                pe.wait_ge(ready, 3)
                for src, dst in ((a, ps_g), (b, ps_b)):
                    for c in range(4):
                        ins = pe.transpose(dst[:, 16 * c:16 * c + 16], src[:, c * P:(c + 1) * P], g.ident[0:16, 0:16])
                ins.then_inc(turned, 1)
                pe.wait_ge(ordered, 1)
                for d in range(2):
                    order = g.mask[:, 1, :] if d == 0 else g.back[:, 0, :]
                    pe.matmul(ps_c[:, 32 * d:32 * d + 32], order, g_seq[:, d].rearrange("p n h -> p (n h)"), start=True, stop=True)
                for d in range(2):
                    order = g.ident[:] if d == 0 else g.back[:, 1, :]
                    ins = pe.matmul(ps_c[:, 64 + 32 * d:96 + 32 * d], order, b_seq[:, d].rearrange("p n h -> p (n h)"), start=True, stop=True)
                ins.then_inc(summed, 1)


def phase_gdn(nc, g):
    with ExitStack() as stack:
        s = Scope(nc, stack, "gd")
        g_seq, gc_seq, be_seq = (s.sb(n, [P, 2, 4, 8]) for n in ("g_seq", "gc_seq", "be_seq"))
        taps = s.sb("taps", [P, 5, 3, 8])
        norm_w = s.sb("norm_w", [P, 1])
        g.back = s.sb("back", [P, 3, P])
        phase_gdn_gates(nc, g, g_seq, gc_seq, be_seq, taps, norm_w)

        raw = [s.sb("raw_q", [P, LAT]), s.sb("raw_k", [P, TOK]), s.sb("raw_v", [P, TOK])]
        conv = [s.sb("q", [P, LAT]), s.sb("k", [P, TOK]), s.sb("v", [P, TOK])]
        half = s.sb("half", [P, 3, TOK])
        z = s.sb("z", [P, LAT])
        cur_g, cur_gc, cur_be, g_end, e_end, tail, nbe, nbeta = (s.sb(n, [P, 2, 4]) for n in (
            "cur_g", "cur_gc", "cur_be", "g_end", "e_end", "tail", "nbe", "nbeta"))
        cur_w = s.sb("cur_w", [P, 5, 3])
        g_wide = s.sb("g_wide", [P, 2, 4, P])
        k_s = [s.sb(f"k_s{d}", [P, 4, P]) for d in range(2)]
        v_s = [s.sb(f"v_s{d}", [P, 4, P]) for d in range(2)]
        q_s = [s.sb(f"q_s{d}", [P, 2, P]) for d in range(2)]
        qd = [s.sb(f"qd{d}", [P, 2, P]) for d in range(2)]
        k_tok = [s.sb(f"k_tok{d}", [P, 4, P]) for d in range(2)]
        v_tok = [s.sb(f"v_tok{d}", [P, 4, P]) for d in range(2)]
        low = [s.sb(f"low{d}", [P, 4, P]) for d in range(2)]
        m_t = [s.sb(f"m_t{d}", [P, 2, P]) for d in range(2)]
        a_t = [s.sb(f"a_t{d}", [P, 4, P]) for d in range(2)]
        inv = [s.sb(f"inv{d}", [P, 4, P]) for d in range(2)]
        inv_t = [s.sb(f"inv_t{d}", [P, 4, P]) for d in range(2)]
        inv2 = [s.sb(f"inv2_{d}", [P, 4, P]) for d in range(2)]
        inv2_t = [s.sb(f"inv2_t{d}", [P, 4, P]) for d in range(2)]
        grown = [[s.sb(f"grown{d}_{n}", [P, 4, P]) for n in LEVELS] for d in range(2)]
        rhs, u, state = ([s.sb(f"{n}{d}", [P, P]) for d in range(2)] for n in ("rhs", "u", "state"))
        o = s.sb("o", [P, LAT])
        eps = s.sb("eps", [P, 1])
        held = s.sb("held", [1, 1])
        bank = [s.ps(f"bank{b}", [P, 512]) for b in range(8)]
        b4 = [b[:].rearrange("p (c t) -> p c t", c=4) for b in bank]

        head_loaded = s.sem("head_loaded")
        (v_step, a_step, convolved, bent, squared, sq_summed, rooted, widened, g_summed, end_read, sides_ready, turned,
         tok_copied, grams, low_ready, low_turned, at_copied, inv2_ready, m_summed, m_ready, qd_ready, d_bent, dt_bent, d_in, dt_in,
         x_summed, x_masked, t_summed, t_copied, r_summed, r_ready, u_summed, u_copied, s_summed, s_ready,
         y_summed, y_added, o_squared, o_summed, o_rooted, round_done, x_filled, cols_bent) = (
            Signal(s, n, per) for n, per in (
                ("v_step", 83), ("a_step", 2), ("convolved", 3), ("bent", 4), ("squared", 2), ("sq_summed", 2),
                ("rooted", 2), ("widened", 1), ("g_summed", 2), ("end_read", 1), ("sides_ready", 2), ("turned", 4),
                ("tok_copied", 4), ("grams", 2), ("low_ready", 2), ("low_turned", 2), ("at_copied", 2), ("inv2_ready", 2),
                ("m_summed", 1), ("m_ready", 2), ("qd_ready", 2), ("d_bent", 2), ("dt_bent", 2), ("d_in", 2), ("dt_in", 2),
                ("x_summed", 12), ("x_masked", 12), ("t_summed", 22), ("t_copied", 22), ("r_summed", 6), ("r_ready", 8),
                ("u_summed", 8), ("u_copied", 8), ("s_summed", 6), ("s_ready", 6), ("y_summed", 4), ("y_added", 4),
                ("o_squared", 1), ("o_summed", 1), ("o_rooted", 1), ("round_done", 3), ("x_filled", 1), ("cols_bent", 3)))

        def seq(ap, d, n):
            c = (2, 3, 0, 1)[n] if d == 0 else (3, 2, 1, 0)[n]
            return ap[:, c * P:(c + 1) * P] if d == 0 else ap[:, c * P:(c + 1) * P][:, ::-1]

        def wide(ap):
            return ap.unsqueeze(1).broadcast_to([P, 4, P])

        with nc.Block() as block:

            @block.sync
            def _(sp):
                def load(i):
                    for j, cols in ((0, LAT), (1, TOK), (2, TOK)):
                        sp.dma_start(raw[j][:], g.d_p[bass.ds(i * P + (CONV0 + j * GDN_W), P), 0:cols]).then_inc(head_loaded, 16)
                load(0)
                with sp.Fori(0, 7) as i:
                    convolved.wait(sp, i, 3)
                    load(i + 1)

            @block.gpsimd
            def _(pool):
                for t in inv2 + inv2_t + grown[0] + grown[1]:
                    for c in range(4):
                        ins = pool.tensor_copy(t[:, c, :], g.ident[:])
                ins.then_inc(x_filled.sem, 1)

            @block.tensor
            def _(pe):
                with pe.Fori(0, 8) as i:
                    squared.wait(pe, i, 1)
                    pe.matmul(bank[0][:], g.ones[:], half[:, 1, :], start=True, stop=True).then_inc(sq_summed.sem, 1)
                    squared.wait(pe, i, 2)
                    pe.matmul(bank[1][:, 0:LAT], g.ones[:], half[:, 0, 0:LAT], start=True, stop=True).then_inc(sq_summed.sem, 1)
                    widened.wait(pe, i)
                    for d in range(2):
                        order = g.mask[:, 1, :] if d == 0 else g.back[:, 0, :]
                        for n in range(4):
                            ins = pe.matmul(b4[2 + d][:, n, :], g_wide[:, d, n, :], order, start=True, stop=True)
                        ins.then_inc(g_summed.sem, 1)
                    for d in range(2):
                        sides_ready.wait(pe, i, d + 1)
                        if d == 0:
                            rooted.wait(pe, i, 2)
                        else:
                            tok_copied.wait(pe, i, 2)
                        for k, src in enumerate((k_s[d], v_s[d])):
                            for c in range(4):
                                ins = pe.transpose(b4[k][:, c, :], src[:, c, :], g.ident[:])
                            ins.then_inc(turned.sem, 1)
                        for c in range(4):
                            ins = pe.matmul(b4[4 + d][:, c, :], k_s[d][:, c, :], k_s[d][:, c, :], start=True, stop=True)
                        ins.then_inc(grams.sem, 1)
                        for c in range(2):
                            ins = pe.matmul(b4[6][:, 2 * d + c, :], k_s[d][:, 2 + c, :], q_s[d][:, c, :], start=True, stop=True)
                        if d == 1:
                            ins.then_inc(m_summed.sem, 1)
                    for d in range(2):
                        tok_copied.wait(pe, i, 4)
                        low_ready.wait(pe, i, d + 1)
                        for c in range(4):
                            ins = pe.transpose(b4[d][:, c, :], low[d][:, c, :], g.ident[:])
                        ins.then_inc(low_turned.sem, 1)
                    for lv, _ in enumerate(LEVELS):
                        for d in range(2):
                            if lv == 0:
                                at_copied.wait(pe, i, d + 1)
                                inv2_ready.wait(pe, i, d + 1)
                                qd_ready.wait(pe, i, 2)
                                m_ready.wait(pe, i, 2)
                                inv2_ready.wait(pe, i, 2)
                                at_copied.wait(pe, i, 2)
                            else:
                                t_copied.wait(pe, i, 4 * lv + 2 * d - 2)
                                x_masked.wait(pe, i, 2 * lv + d - 1)
                            src = inv2[d] if lv == 0 else inv[d]
                            for c in range(4):
                                ins = pe.matmul(b4[3 * d][:, c, :], a_t[d][:, c, :], src[:, c, :], start=True, stop=True)
                            ins.then_inc(x_summed.sem, 1)
                        for d in range(2):
                            src_t = inv2_t[d] if lv == 0 else inv_t[d]
                            x_masked.wait(pe, i, 2 * lv + d + 1)
                            if lv < 5:
                                for c in range(4):
                                    ins = pe.matmul(b4[3 * d + 1][:, c, :], src_t[:, c, :], grown[d][lv][:, c, :], start=True, stop=True)
                                ins.then_inc(t_summed.sem, 1)
                            for c in range(4):
                                ins = pe.matmul(b4[3 * d + 2][:, c, :], grown[d][lv][:, c, :], src_t[:, c, :], start=True, stop=True)
                            ins.then_inc(t_summed.sem, 1)
                    for n in range(4):
                        for d in range(2):
                            if n:
                                s_ready.wait(pe, i, 2 * (n - 1) + d + 1)
                                pe.matmul(bank[3 * d][:, 0:P], k_s[d][:, n, :], state[d][:], start=True, stop=True).then_inc(r_summed.sem, 1)
                            else:
                                t_copied.wait(pe, i, 22)
                        for d in range(2):
                            r_ready.wait(pe, i, 2 * n + d + 1)
                            pe.matmul(bank[3 * d + 1][:, 0:P], inv_t[d][:, n, :], rhs[d][:], start=True, stop=True).then_inc(u_summed.sem, 1)
                        for d in range(2):
                            u_copied.wait(pe, i, 2 * n + d + 1)
                            if n < 3:
                                pe.matmul(bank[3 * d + 2][:, 0:P], k_tok[d][:, n, :], u[d][:], start=True, stop=True).then_inc(s_summed.sem, 1)
                            if n >= 2:
                                if n == 3:
                                    y_added.wait(pe, i, d + 1)
                                pe.matmul(bank[6 + d][:, 0:P], state[d][:], qd[d][:, n - 2, :], start=True, stop=False)
                                pe.matmul(bank[6 + d][:, 0:P], u[d][:], m_t[d][:, n - 2, :], start=False, stop=True).then_inc(y_summed.sem, 1)
                    o_squared.wait(pe, i)
                    pe.matmul(bank[0][:, 0:LAT], g.ones[:], half[:, 0, 0:LAT], start=True, stop=True).then_inc(o_summed.sem, 1)
                    round_done.wait(pe, i, 3)

            @block.scalar
            def _(act):
                z_in = s.sem("z_in")
                x_filled.wait(act, 0)
                with act.Fori(0, 8) as i:
                    act.dma_start(z[:], g.d_p[bass.ds(i * P + Z0, P), 0:LAT]).then_inc(z_in, 16)
                    for j in (1, 2, 0):
                        cols = LAT if j == 0 else TOK
                        convolved.wait(act, i, (3, 1, 2)[j])
                        act.activation(half[:, j, 0:cols], conv[j][:], ACT.Tanh, scale=0.5).then_inc(bent.sem, 1)
                    act.wait_ge(z_in, 16 * i + 16)
                    for d in range(2):
                        d_in.wait(act, i, d + 1)
                        act.activation(low[d][:], low[d][:], ACT.Exp, scale=-1.0).then_inc(d_bent.sem, 1)
                        dt_in.wait(act, i, d + 1)
                        act.activation(m_t[d][:], m_t[d][:], ACT.Exp).then_inc(dt_bent.sem, 1)
                    end_read.wait(act, i)
                    act.activation(e_end[:], g_end[:], ACT.Exp).then_inc(cols_bent.sem, 1)
                    act.activation(tail[:], tail[:], ACT.Exp).then_inc(cols_bent.sem, 1)
                    act.activation(nbe[:], cur_gc[:], ACT.Exp).then_inc(cols_bent.sem, 1)
                    for d in range(2):
                        g_summed.wait(act, i, d + 1)
                        act.activation(qd[d][:], b4[2 + d][:, 2:4, :], ACT.Exp).then_inc(a_step.sem, 1)
                    sq_summed.wait(act, i, 1)
                    act.activation(half[:, 1, :], bank[0][:], ACT.Sqrt, bias=eps[:, 0:1], scale=0.25).then_inc(rooted.sem, 1)
                    sq_summed.wait(act, i, 2)
                    act.activation(half[:, 0, 0:LAT], bank[1][:, 0:LAT], ACT.Sqrt, bias=eps[:, 0:1], scale=0.25).then_inc(rooted.sem, 1)
                    for d in range(2):
                        low_turned.wait(act, i, d + 1)
                        inv2_ready.wait(act, i, d + 1)
                        act.activation(a_t[d][:], b4[d][:], ACT.Copy).then_inc(at_copied.sem, 1)
                    for lv in range(6):
                        for d in range(2):
                            if lv < 5:
                                t_summed.wait(act, i, 4 * lv + 2 * d + 2)
                                act.activation(inv[d][:], b4[3 * d + 1][:], ACT.Copy).then_inc(t_copied.sem, 1)
                            else:
                                t_summed.wait(act, i, 20 + d + 1)
                            act.activation(inv_t[d][:], b4[3 * d + 2][:], ACT.Copy).then_inc(t_copied.sem, 1)
                    for n in range(4):
                        for d in range(2):
                            u_summed.wait(act, i, 2 * n + d + 1)
                            act.activation(u[d][:], bank[3 * d + 1][:, 0:P], ACT.Copy).then_inc(u_copied.sem, 1)
                    act.activation(half[:, 2, 0:LAT], z[:], ACT.Tanh, scale=0.5).then_inc(bent.sem, 1)
                    o_summed.wait(act, i)
                    act.activation(half[:, 0, 0:LAT], bank[0][:, 0:LAT], ACT.Sqrt, bias=eps[:, 0:1], scale=1.0 / P).then_inc(o_rooted.sem, 1)
                    o_rooted.wait(act, i)
                    act.sem_inc(round_done.sem, 1)
                    round_done.wait(act, i, 3)

            @block.vector
            def _(dve):
                boot = Steps(dve, s.sem("boot"))
                boot(dve.memset(eps[:], EPS))
                x_filled.wait(dve, 0)
                with dve.Fori(0, 8) as i:
                    step = Chain(dve, v_step, i)
                    at = bass.ds(i, 1)
                    step(dve.tensor_copy(cur_w[:], taps[:, :, :, at].rearrange("p t j a -> p t (j a)")))
                    for dst, src in ((cur_g, g_seq), (cur_gc, gc_seq), (cur_be, be_seq)):
                        step(dve.tensor_copy(dst[:], src[:, :, :, at].rearrange("p d n a -> p d (n a)")))
                    step.tell(dve.tensor_copy(g_wide[:], cur_g[:].unsqueeze(3).broadcast_to([P, 2, 4, P])), widened)
                    dve.wait_ge(head_loaded, 48 * i + 48)
                    for k, j in enumerate((1, 2, 0)):
                        parts = 1 if j == 0 else 2
                        src = raw[j][:].rearrange("p (a t) -> p a t", a=parts)
                        out = conv[j][:].rearrange("p (a t) -> p a t", a=parts)
                        step(dve.tensor_scalar(out, src, cur_w[:, 2, j:j + 1], None, ALU.mult))
                        for tap in (0, 1, 3, 4):
                            by = tap - 2
                            lo, hi = max(0, -by), min(LAT, LAT - by)
                            ins = dve.scalar_tensor_tensor(out[:, :, lo:hi], src[:, :, lo + by:hi + by], cur_w[:, tap, j:j + 1],
                                                           out[:, :, lo:hi], ALU.mult, ALU.add)
                            if tap == 4:
                                step.tell(ins, convolved, k + 1)
                            else:
                                step(ins)
                    for k, j in enumerate((1, 2, 0)):
                        cols = LAT if j == 0 else TOK
                        bent.wait(dve, i, k + 1)
                        step(dve.scalar_tensor_tensor(conv[j][:], half[:, j, 0:cols], 1.0, conv[j][:], ALU.add, ALU.mult))
                        if j != 2:
                            step.tell(dve.tensor_tensor(half[:, j, 0:cols], conv[j][:], conv[j][:], ALU.mult), squared, 1 if j else 2)
                    for d in range(2):
                        g_summed.wait(dve, i, d + 1)
                        step(dve.tensor_copy(g_end[:, d, :], b4[2 + d][:, :, P - 1]))
                        for n in range(4):
                            ins = dve.tensor_scalar(low[d][:, n, :], b4[2 + d][:, n, :], cur_gc[:, d, n:n + 1], 0.0, ALU.subtract, ALU.max)
                            if n == 3:
                                step.tell(ins, d_in, d + 1)
                            else:
                                step(ins)
                        for n in (2, 3):
                            ins = dve.tensor_scalar(m_t[d][:, n - 2, :], b4[2 + d][:, n, :], cur_gc[:, d, n:n + 1], 0.0, ALU.subtract, ALU.min)
                            if n == 3:
                                step.tell(ins, dt_in, d + 1)
                            else:
                                step(ins)
                    step.tell(dve.tensor_tensor(tail[:], g_end[:], cur_gc[:], ALU.subtract), end_read)
                    step(dve.tensor_scalar(nbeta[:], cur_be[:], -1.0, None, ALU.mult))
                    cols_bent.wait(dve, i, 3)
                    step(dve.tensor_tensor(nbe[:], nbe[:], nbeta[:], ALU.mult))
                    rooted.wait(dve, i, 2)
                    step(dve.reciprocal(half[:, 1, :], half[:, 1, :]))
                    step(dve.reciprocal(half[:, 0, 0:LAT], half[:, 0, 0:LAT]))
                    step(dve.scalar_tensor_tensor(conv[1][:], conv[1][:], 0.5, half[:, 1, :], ALU.mult, ALU.mult))
                    step(dve.scalar_tensor_tensor(conv[0][:], conv[0][:], 0.5 * P ** -0.5, half[:, 0, 0:LAT], ALU.mult, ALU.mult))
                    a_step.wait(dve, i, 2)
                    for d in range(2):
                        for n in range(4):
                            step(dve.tensor_copy(k_s[d][:, n, :], seq(conv[1][:], d, n)))
                            step(dve.tensor_scalar(v_s[d][:, n, :], seq(conv[2][:], d, n), 0.5, None, ALU.mult))
                        for n in (2, 3):
                            step(dve.tensor_copy(q_s[d][:, n - 2, :], seq(conv[0][:], d, n)))
                        step.tell(dve.tensor_tensor(qd[d][:], qd[d][:], q_s[d][:], ALU.mult), sides_ready, d + 1)
                        for k, (dst, col) in enumerate(((k_tok[d], tail), (v_tok[d], cur_be))):
                            turned.wait(dve, i, 2 * d + k + 1)
                            for n in range(4):
                                ins = dve.tensor_scalar(dst[:, n, :], b4[k][:, n, :], col[:, d, n:n + 1], None, ALU.mult)
                                if n == 3:
                                    step.tell(ins, tok_copied, 2 * d + k + 1)
                                else:
                                    step(ins)
                    dve.sem_inc(qd_ready.sem, 2)
                    for d in range(2):
                        d_bent.wait(dve, i, d + 1)
                        grams.wait(dve, i, d + 1)
                        step(dve.tensor_tensor(low[d][:], low[d][:], b4[4 + d][:], ALU.mult))
                        for n in range(4):
                            ins = dve.scalar_tensor_tensor(low[d][:, n, :], low[d][:, n, :], nbeta[:, d, n:n + 1], g.back[:, 2, :],
                                                           ALU.mult, ALU.mult)
                            if n == 3:
                                step.tell(ins, low_ready, d + 1)
                            else:
                                step(ins)
                        dve.memset(held[:], 0.0)
                        step(dve.copy_predicated(inv2[d][:], wide(g.level[:, 0, :]), low[d][:]))
                    for d in range(2):
                        dt_bent.wait(dve, i, d + 1)
                        m_summed.wait(dve, i)
                        step(dve.tensor_tensor(m_t[d][:], m_t[d][:], g.mask[:, 1, :].unsqueeze(1).broadcast_to([P, 2, P]), ALU.mult))
                        step.tell(dve.tensor_tensor(m_t[d][:], m_t[d][:], b4[6][:, 2 * d:2 * d + 2, :], ALU.mult), m_ready, d + 1)
                    for d in range(2):
                        low_turned.wait(dve, i, d + 1)
                        dve.memset(held[:], 0.0)
                        step.tell(dve.copy_predicated(inv2_t[d][:], wide(g.level[:, 7, :]), b4[d][:]), inv2_ready, d + 1)
                    for lv in range(6):
                        for d in range(2):
                            x_summed.wait(dve, i, 2 * lv + d + 1)
                            dve.memset(held[:], 0.0)
                            step.tell(dve.copy_predicated(grown[d][lv][:], wide(g.level[:, lv + 1, :]), b4[3 * d][:]),
                                      x_masked, 2 * lv + d + 1)
                    for n in range(4):
                        for d in range(2):
                            if n == 0:
                                step.tell(dve.tensor_copy(rhs[d][:], v_tok[d][:, 0, :]), r_ready, d + 1)
                            else:
                                r_summed.wait(dve, i, 2 * (n - 1) + d + 1)
                                step.tell(dve.scalar_tensor_tensor(rhs[d][:], bank[3 * d][:, 0:P], nbe[:, d, n:n + 1], v_tok[d][:, n, :],
                                                                   ALU.mult, ALU.add), r_ready, 2 * n + d + 1)
                        for d in range(2):
                            if n == 0:
                                s_summed.wait(dve, i, d + 1)
                                step.tell(dve.tensor_copy(state[d][:], bank[3 * d + 2][:, 0:P]), s_ready, d + 1)
                            elif n < 3:
                                s_summed.wait(dve, i, 2 * n + d + 1)
                                if n == 2:
                                    y_summed.wait(dve, i, d + 1)
                                step.tell(dve.scalar_tensor_tensor(state[d][:], state[d][:], e_end[:, d, n:n + 1], bank[3 * d + 2][:, 0:P],
                                                                   ALU.mult, ALU.add), s_ready, 2 * n + d + 1)
                            if n >= 2:
                                y_summed.wait(dve, i, 2 * (n - 2) + d + 1)
                                dst = seq(o[:], d, n)
                                first = (n == 2)
                                ins = (dve.tensor_copy(dst, bank[6 + d][:, 0:P]) if first else
                                       dve.tensor_tensor(dst, dst, bank[6 + d][:, 0:P], ALU.add))
                                step.tell(ins, y_added, 2 * (n - 2) + d + 1)
                    step.tell(dve.tensor_tensor(half[:, 0, 0:LAT], o[:], o[:], ALU.mult), o_squared)
                    o_rooted.wait(dve, i)
                    step(dve.reciprocal(half[:, 0, 0:LAT], half[:, 0, 0:LAT]))
                    step(dve.scalar_tensor_tensor(o[:], o[:], norm_w[:, 0:1], half[:, 0, 0:LAT], ALU.mult, ALU.mult))
                    bent.wait(dve, i, 4)
                    step(dve.scalar_tensor_tensor(half[:, 2, 0:LAT], half[:, 2, 0:LAT], 1.0, z[:], ALU.add, ALU.mult))
                    step(dve.scalar_tensor_tensor(g.o_b[:, at, :].rearrange("p a t -> p (a t)"), o[:], 0.5, half[:, 2, 0:LAT],
                                                  ALU.mult, ALU.mult))
                    step.end()
                    dve.sem_inc(round_done.sem, 2)
                    round_done.wait(dve, i, 3)


HD = 64
HEADS = 8
MLA_Q, MLA_DK = 384, 96
C_KV, K_PE = 384, 512
FOX_Q, FOX_K, FOX_V, FOX_F = 544, 1056, 1568, 2080
NSA_Q, NSA_KC, NSA_VC, NSA_KS, NSA_VS, NSA_KW, NSA_VW, NSA_GATE = 2088, 2600, 2728, 2856, 2984, 3112, 3240, 3368
SWA_Q, SWA_K, SWA_V = 3392, 3904, 4032
CMP_LEN, CMP_STRIDE = 32, 16
CMP = (LAT - CMP_LEN) // CMP_STRIDE + 1
REL_MAX = 128
NEG = -1e30
V_COLS = 2 * 512 + 3 * P


def phase_latent(nc, g):
    with ExitStack() as stack:
        s = Scope(nc, stack, "la")
        lat = s.sb("lat", [P, 4, LAT])
        sq = s.sb("sq", [P, 4, LAT])
        rows, cols = s.sb("rows", [4, P]), s.sb("cols", [P, 4])
        rstd = s.sb("rstd", [P, 2, LAT])
        eps = s.sb("eps", [P, 1])
        rot, cs = s.sb("rot", [MLA_DK, MLA_DK]), s.sb("cs", [MLA_DK, 2, LAT])
        kp, ko, kr = (s.sb(n, [MLA_DK, LAT]) for n in ("kp", "ko", "kr"))
        w_q, w_kv = s.sb("w_q", [P, 3, MLA_DK]), s.sb("w_kv", [P, P])
        qh, qo, qr = (s.sb(n, [MLA_DK, LAT]) for n in ("qh", "qo", "qr"))
        kvh = s.sb("kvh", [P, LAT])
        vo = s.sb("vo", [P, 2, HD])
        bank = [s.ps(f"bank{i}", [P, 512]) for i in range(8)]
        loaded, pe_in, zeroed, w_in, stored, pe_stored = (s.sem(n) for n in ("loaded", "pe_in", "zeroed", "w_in", "stored", "pe_stored"))
        squared, turned, summed, rooted, stepped, latents_ready, kp_turned, kp_done = (s.sem(n) for n in (
            "squared", "turned", "summed", "rooted", "stepped", "latents_ready", "kp_turned", "kp_done"))
        q_summed, kv_summed, q_copied, kv_copied, rotated, v_turned, q_done, v_done, h_step = (Signal(s, n, per) for n, per in (
            ("q_summed", 1), ("kv_summed", 1), ("q_copied", 1), ("kv_copied", 1), ("rotated", 1), ("v_turned", 1),
            ("q_done", 1), ("v_done", 1), ("h_step", 2)))

        with nc.Block() as block:

            @block.sync
            def _(sp):
                sp.dma_start(lat[:], g.d_p2[0:512, :].rearrange("(k p) t -> p k t", p=P)).then_inc(loaded, 16)
                sp.dma_start(rows[0:3, :], g.mla_q_norm_2[0].rearrange("(k p) -> k p", p=P)).then_inc(loaded, 16)
                sp.dma_start(rows[3:4, :], g.mla_kv_norm_2).then_inc(loaded, 16)
                sp.dma_start(rot[:], g.c_rot).then_inc(loaded, 16)
                sp.dma_start(cs[:], g.c_rope).then_inc(loaded, 16)
                sp.wait_ge(zeroed, 1)
                sp.dma_start(kp[HD:MLA_DK, :], g.d_p2[K_PE:K_PE + 32, :]).then_inc(pe_in, 16)
                with sp.Fori(0, HEADS) as i:
                    kv_summed.wait(sp, i)
                    w = g.mla_w_uq_2[0].rearrange("(k p) n -> p k n", p=P)
                    sp.dma_start(w_q[:], w[:, :, bass.ds(i * MLA_DK, MLA_DK)]).then_inc(w_in, 16)
                    sp.dma_start(w_kv[:], g.mla_w_ukv_2[0][:, bass.ds(i * P, P)]).then_inc(w_in, 16)

            @block.tensor
            def _(pe):
                pe.wait_ge(loaded, 80)
                pe.transpose(bank[7][:, 0:4], rows[:], g.ident[0:4, 0:4]).then_inc(turned, 1)
                pe.wait_ge(squared, 1)
                for k in range(3):
                    pe.matmul(bank[0][:, 0:LAT], g.ones[:], sq[:, k, :], start=(k == 0), stop=(k == 2))
                pe.matmul(bank[1][:, 0:LAT], g.ones[:], sq[:, 3, :], start=True, stop=True).then_inc(summed, 1)
                pe.wait_ge(pe_in, 16)
                pe.matmul(bank[6][0:MLA_DK, 0:LAT], rot[:], kp[:], start=True, stop=True).then_inc(kp_turned, 1)
                pe.wait_ge(latents_ready, 1)
                pe.sem_inc(kv_summed.sem, 1)
                with pe.Fori(0, HEADS) as i:
                    pe.wait_ge(w_in, 32 * i + 32)
                    for k in range(3):
                        ins = pe.matmul(bank[2][0:MLA_DK, 0:LAT], w_q[:, k, :], lat[:, k, :], start=(k == 0), stop=(k == 2))
                    ins.then_inc(q_summed.sem, 1)
                    pe.matmul(bank[3][:, 0:LAT], w_kv[:], lat[:, 3, :], start=True, stop=True).then_inc(kv_summed.sem, 1)
                    q_copied.wait(pe, i)
                    pe.matmul(bank[4][0:MLA_DK, 0:LAT], rot[:], qh[:], start=True, stop=True).then_inc(rotated.sem, 1)
                    kv_copied.wait(pe, i)
                    for t in range(2):
                        ins = pe.transpose(bank[5][:, P * t:P * t + P], kvh[:, P * t:P * t + P], g.ident[:])
                    ins.then_inc(v_turned.sem, 1)
                    q_done.wait(pe, i)
                    v_done.wait(pe, i)

            @block.scalar
            def _(act):
                act.wait_ge(loaded, 80)
                act.activation(sq[:], lat[:], ACT.Square).then_inc(squared, 1)
                act.wait_ge(summed, 1)
                act.wait_ge(zeroed, 2)
                act.activation(rstd[:, 0, :], bank[0][:, 0:LAT], ACT.Sqrt, bias=eps[:, 0:1], scale=1.0 / MLA_Q).then_inc(rooted, 1)
                act.activation(rstd[:, 1, :], bank[1][:, 0:LAT], ACT.Sqrt, bias=eps[:, 0:1], scale=1.0 / P).then_inc(rooted, 1)
                act.wait_ge(kp_done, 1)
                act.dma_start(g.d_mk[:, HD:MLA_DK, :].rearrange("h r t -> r h t"),
                              ko[HD:MLA_DK, :].unsqueeze(1).broadcast_to([32, HEADS, LAT])).then_inc(pe_stored, 16)
                with act.Fori(0, HEADS) as i:
                    q_summed.wait(act, i)
                    act.activation(qh[:], bank[2][0:MLA_DK, 0:LAT], ACT.Copy).then_inc(q_copied.sem, 1)
                    kv_summed.wait(act, i, 2)
                    act.activation(kvh[:], bank[3][:, 0:LAT], ACT.Copy).then_inc(kv_copied.sem, 1)
                    kv_copied.wait(act, i)
                    act.dma_start(g.d_mk[bass.ds(i, 1), 0:HD, :].rearrange("h r t -> (h r) t"), kvh[0:HD, :]).then_inc(stored, 16)
                    q_done.wait(act, i)
                    act.dma_start(g.d_mq[bass.ds(i, 1), :, :].rearrange("h r t -> (h r) t"), qo[:]).then_inc(stored, 16)
                    v_done.wait(act, i)
                    act.dma_start(g.d_v[:, bass.ds(i * HD, HD)].rearrange("(t p) c -> p t c", p=P), vo[:]).then_inc(stored, 16)
                    act.wait_ge(stored, 48 * i + 48)
                act.wait_ge(pe_stored, 16)

            @block.vector
            def _(dve):
                step = Steps(dve, stepped)
                dve.memset(kp[:], 0.0).then_inc(zeroed, 1)
                dve.memset(eps[:], EPS).then_inc(zeroed, 1)
                dve.wait_ge(turned, 1)
                step(dve.tensor_copy(cols[:], bank[7][:, 0:4]))
                dve.wait_ge(rooted, 2)
                step(dve.reciprocal(rstd[:], rstd[:]))
                for k in range(4):
                    step(dve.scalar_tensor_tensor(lat[:, k, :], lat[:, k, :], cols[:, k:k + 1], rstd[:, k // 3, :], ALU.mult, ALU.mult))
                dve.sem_inc(latents_ready, 1)
                dve.wait_ge(pe_in, 16)
                step(dve.tensor_tensor(ko[:], kp[:], cs[:, 0, :], ALU.mult))
                dve.wait_ge(kp_turned, 1)
                step(dve.tensor_tensor(kr[:], bank[6][0:MLA_DK, 0:LAT], cs[:, 1, :], ALU.mult))
                dve.tensor_tensor(ko[:], ko[:], kr[:], ALU.add).then_inc(kp_done, 1)
                with dve.Fori(0, HEADS) as i:
                    hstep = Chain(dve, h_step, i)
                    q_copied.wait(dve, i)
                    hstep(dve.tensor_tensor(qo[:], qh[:], cs[:, 0, :], ALU.mult))
                    rotated.wait(dve, i)
                    hstep(dve.tensor_tensor(qr[:], bank[4][0:MLA_DK, 0:LAT], cs[:, 1, :], ALU.mult))
                    dve.tensor_tensor(qo[:], qo[:], qr[:], ALU.add).then_inc(q_done.sem, 1)
                    v_turned.wait(dve, i)
                    dve.tensor_copy(vo[:], bank[5][:, 0:LAT].rearrange("p (t c) -> p t c", t=2)[:, :, HD:P]).then_inc(v_done.sem, 1)
                    dve.wait_ge(stored, 48 * i + 48)


def phase_tables(nc, g):
    tiles = [FOX_V + P * k for k in range(4)] + [NSA_VS, NSA_VW, SWA_V]
    with ExitStack() as stack:
        s = Scope(nc, stack, "tb")
        vch = s.sb("vch", [P, 7, LAT])
        vt = s.sb("vt", [P, 2, 7 * P])
        f, ft = s.sb("f", [HEADS, LAT]), s.sb("ft", [HEADS, LAT])
        bf = s.sb("bf", [HEADS, 1])
        f_tok, f_sum = s.sb("f_tok", [P, 2, HEADS]), s.sb("f_sum", [P, 2, HEADS])
        f_row = s.sb("f_row", [HEADS, LAT])
        fb = s.sb("fb", [P, HEADS, LAT])
        fox = s.sb("fox", [P, HEADS, 2, LAT])
        causal = s.sb("causal", [P, 2, LAT])
        mask = s.sb("mask", [P, 2, P])
        rel = s.sb("rel", [33, 2 * HEADS])
        rel_w = s.sb("rel_w", [33, 2 * HEADS, P])
        hot = s.sb("hot", [33, 2, 512])
        tz = s.sb("tz", [P, 4, 512])
        bank = [s.ps(f"bank{i}", [P, 512]) for i in range(8)]
        loaded, rel_in, ones_set, turned, v_copied, v_stored = (s.sem(n) for n in (
            "loaded", "rel_in", "ones_set", "turned", "v_copied", "v_stored"))
        neg_ready, bent, stepped, f_ready, f_turned, f_tok_ready, f_summed, row_ready, row_out, row_in, fox_ready, fox_out = (
            s.sem(n) for n in ("neg_ready", "bent", "stepped", "f_ready", "f_turned", "f_tok_ready", "f_summed",
                               "row_ready", "row_out", "row_in", "fox_ready", "fox_out"))
        rel_ready, tz_summed, tz_copied = s.sem("rel_ready"), s.sem("tz_summed"), s.sem("tz_copied")
        tz_out = [s.sem(f"tz_out{k}") for k in range(4)]

        with nc.Block() as block:

            @block.sync
            def _(sp):
                sp.wait_ge(ones_set, 1)
                sp.dma_start(rel[0:32, :], g.rel_bias_2).then_inc(rel_in, 16)
                for dst, src in ((f[:], g.d_p2[FOX_F:FOX_F + HEADS, :]), (bf[:], g.fox_b_f_2[0].unsqueeze(1)),
                                 (hot[:], g.c_bucket), (mask[:], g.c_mask), (causal[:], g.c_causal),
                                 (vch[:, 0:4, :], g.d_p2[FOX_V:FOX_V + 512, :].rearrange("(k p) t -> p k t", p=P))):
                    sp.dma_start(dst, src).then_inc(loaded, 16)
                for k in range(4, 7):
                    sp.dma_start(vch[:, k, :], g.d_p2[tiles[k]:tiles[k] + P, :]).then_inc(loaded, 16)
                sp.wait_ge(row_ready, 1)
                sp.dma_start(g.d_frow, f_row[:]).then_inc(row_out, 16)
                sp.wait_ge(row_out, 16)
                for h in range(HEADS):
                    sp.dma_start(fb[:, h, :], g.d_frow[h].partition_broadcast(P)).then_inc(row_in, 16)
                for h in range(2 * HEADS):
                    sp.wait_ge(tz_copied, h + 1)
                    sp.dma_start(g.d_skew[h, 0:P * 512].rearrange("(p x) -> p x", p=P), tz[:, h % 4, :]).then_inc(tz_out[h % 4], 16)
                sp.wait_ge(fox_ready, 1)
                sp.dma_start(g.d_fox.rearrange("h p q k -> p h (q k)"), fox[:].rearrange("p h q k -> p h (q k)")).then_inc(fox_out, 16)
                sp.wait_ge(fox_out, 16)
                for k in range(4):
                    sp.wait_ge(tz_out[k], 64)

            @block.tensor
            def _(pe):
                pe.wait_ge(rel_ready, 1)
                pe.wait_ge(loaded, 144)
                for k in range(7):
                    if k >= 2:
                        pe.wait_ge(v_copied, k - 1)
                    for t in range(2):
                        ins = pe.transpose(bank[k % 2][:, P * t:P * t + P], vch[:, k, P * t:P * t + P], g.ident[:])
                    ins.then_inc(turned, 1)
                pe.wait_ge(f_ready, 1)
                for t in range(2):
                    ins = pe.transpose(bank[2][:, HEADS * t:HEADS * t + HEADS], f[:, P * t:P * t + P], g.ident[0:HEADS, 0:HEADS])
                ins.then_inc(f_turned, 1)
                pe.wait_ge(f_tok_ready, 1)
                upto = mask[:, 1, :]
                pe.matmul(bank[3][:, 0:HEADS], upto, f_tok[:, 0, :], start=True, stop=True)
                pe.matmul(bank[3][:, 16:16 + HEADS], upto, f_tok[:, 1, :], start=True, stop=False)
                pe.matmul(bank[3][:, 16:16 + HEADS], g.ones[:], f_tok[:, 0, :], start=False, stop=True)
                pe.matmul(bank[4][0:HEADS, 0:P], f_tok[:, 0, :], upto, start=True, stop=True)
                pe.matmul(bank[4][0:HEADS, P:LAT], f_tok[:, 1, :], upto, start=True, stop=False)
                pe.matmul(bank[4][0:HEADS, P:LAT], f_tok[:, 0, :], g.ones[:], start=False, stop=True).then_inc(f_summed, 1)
                for h in range(2 * HEADS):
                    if h >= 2:
                        pe.wait_ge(tz_copied, h - 1)
                    pe.matmul(bank[6 + h % 2][:], rel_w[:, h, :], hot[:, h // HEADS, :], start=True, stop=True).then_inc(tz_summed, 1)

            @block.scalar
            def _(act):
                act.wait_ge(neg_ready, 1)
                act.activation(ft[:], ft[:], ACT.Exp).then_inc(bent, 1)
                act.wait_ge(neg_ready, 2)
                act.activation(ft[:], ft[:], ACT.Ln).then_inc(bent, 1)
                for k in range(7):
                    act.wait_ge(turned, k + 1)
                    act.activation(vt[:, :, P * k:P * k + P], bank[k % 2][:, 0:LAT].rearrange("p (t c) -> p t c", t=2), ACT.Copy)\
                       .then_inc(v_copied, 1)
                act.wait_ge(v_copied, 7)
                act.dma_start(g.d_v[:, 512:V_COLS].rearrange("(t p) c -> p t c", p=P), vt[:]).then_inc(v_stored, 16)
                for h in range(2 * HEADS):
                    act.wait_ge(tz_summed, h + 1)
                    if h >= 4:
                        act.wait_ge(tz_out[h % 4], 16 * (h // 4))
                    act.activation(tz[:, h % 4, :], bank[6 + h % 2][:], ACT.Copy).then_inc(tz_copied, 1)
                act.wait_ge(v_stored, 16)

            @block.vector
            def _(dve):
                step = Steps(dve, stepped)
                dve.memset(rel[32:33, :], 1.0).then_inc(ones_set, 1)
                dve.wait_ge(rel_in, 16)
                dve.tensor_copy(rel_w[:], rel[:].unsqueeze(2).broadcast_to([33, 2 * HEADS, P])).then_inc(rel_ready, 1)
                dve.wait_ge(loaded, 144)
                step(dve.tensor_scalar(f[:], f[:], bf[:, 0:1], None, ALU.add))
                step(dve.tensor_scalar(ft[:], f[:], -1.0, None, ALU.mult))
                dve.tensor_tensor(ft[:], ft[:], f[:], ALU.min).then_inc(neg_ready, 1)
                dve.wait_ge(bent, 1)
                dve.tensor_scalar(ft[:], ft[:], 1.0, None, ALU.add).then_inc(neg_ready, 1)
                dve.wait_ge(bent, 2)
                dve.scalar_tensor_tensor(f[:], f[:], 0.0, ft[:], ALU.min, ALU.subtract).then_inc(f_ready, 1)
                dve.wait_ge(f_turned, 1)
                dve.tensor_copy(f_tok[:], bank[2][:, 0:2 * HEADS].rearrange("p (t h) -> p t h", t=2)).then_inc(f_tok_ready, 1)
                dve.wait_ge(f_summed, 1)
                dve.tensor_copy(f_row[:], bank[4][0:HEADS, 0:LAT]).then_inc(row_ready, 1)
                step(dve.tensor_copy(f_sum[:], bank[3][:, 0:32].rearrange("p (t h) -> p t h", t=2)[:, :, 0:HEADS]))
                dve.wait_ge(row_in, 16 * HEADS)
                for h in range(HEADS):
                    for t in range(2):
                        step(dve.tensor_scalar(fox[:, h, t, :], fb[:, h, :], -1.0, f_sum[:, t, h:h + 1], ALU.mult, ALU.add))
                dve.tensor_tensor(fox[:].rearrange("p h q k -> p h (q k)"), fox[:].rearrange("p h q k -> p h (q k)"),
                                  causal[:].rearrange("p q k -> p (q k)").unsqueeze(1).broadcast_to([P, HEADS, 2 * LAT]), ALU.add)\
                   .then_inc(fox_ready, 1)


def skewed(g, h, t):
    start = LAT - 1 - P * t
    return g.d_skew[bass.ds(h, 1), start:start + P * 511].rearrange("h (p x) -> (h p) x", x=511)[:, 0:LAT]


def phase_compressed(nc, g):
    with ExitStack() as stack:
        s = Scope(nc, stack, "co")
        kv = s.sb("kv", [HD, 2, 2, LAT])
        w1, w2 = s.sb("w1", [HD, 2, CMP_LEN, HD]), s.sb("w2", [HD, 2, HD])
        pos, pos_t = s.sb("pos", [2 * CMP_LEN, HD]), s.sb("pos_t", [HD, 2, CMP_LEN])
        blk = s.sb("blk", [HD, 2, CMP_LEN, 2, CMP])
        pre, bend, hid = (s.sb(n, [HD, 2, 2 * CMP]) for n in ("pre", "bend", "hid"))
        k_cmp, v_cmp = s.sb("k_cmp", [HD, 2 * CMP]), s.sb("v_cmp", [CMP, 2, HD])
        q = s.sb("q", [HD, HEADS, LAT])
        bias = s.sb("bias", [P, 2, HEADS, LAT])
        valid = s.sb("valid", [P, 2, CMP])
        sc = s.sb("sc", [P, 2, HEADS, CMP])
        top, tot = s.sb("top", [P, 2, HEADS]), s.sb("tot", [P, 2, HEADS])
        p_t = s.sb("p_t", [CMP, HEADS, LAT])
        o = s.sb("o", [HD, HEADS, LAT])
        bank = [s.ps(f"bank{i}", [P, 512]) for i in range(8)]
        loaded, q_in, bias_in, turned, pos_ready, blk_ready = (s.sem(n) for n in (
            "loaded", "q_in", "bias_in", "turned", "pos_ready", "blk_ready"))
        h_summed, stepped, arg_ready, bent, hid_ready, kv_summed, kv_ready = (s.sem(n) for n in (
            "h_summed", "stepped", "arg_ready", "bent", "hid_ready", "kv_summed", "kv_ready"))
        scored, lowered, raised, weighed, p_turned, p_ready, mixed, copied, stored = (s.sem(n) for n in (
            "scored", "lowered", "raised", "weighed", "p_turned", "p_ready", "mixed", "copied", "stored"))

        with nc.Block() as block:

            @block.sync
            def _(sp):
                sp.dma_start(pos[:], g.nsa_cmp_pos_2[0].rearrange("k l d -> (k l) d")).then_inc(loaded, 16)
                sp.dma_start(w2[:], g.nsa_cmp_w2_2[0].rearrange("k d o -> d k o")).then_inc(loaded, 16)
                for k, row in enumerate((NSA_KC, NSA_VC)):
                    sp.dma_start(kv[:, k], g.d_p2[row:row + P, :].rearrange("(g d) t -> d g t", g=2)).then_inc(loaded, 16)
                    sp.dma_start(w1[:, k], g.nsa_cmp_w1_2[0, k].rearrange("(l d) o -> d l o", d=HD)).then_inc(loaded, 16)
                sp.dma_start(valid[:], g.c_valid).then_inc(loaded, 16)
                sp.dma_start(q[:], g.d_p2[NSA_Q:NSA_Q + 512, :].rearrange("(h d) t -> d h t", d=HD)).then_inc(q_in, 16)

            @block.scalar
            def _(act):
                for h in range(HEADS):
                    for t in range(2):
                        act.dma_start(bias[:, t, h, :], skewed(g, h, t)).then_inc(bias_in, 16)
                act.wait_ge(arg_ready, 1)
                act.activation(bend[:], bend[:], ACT.Tanh, scale=(2 / 3.141592653589793) ** 0.5).then_inc(bent, 1)
                act.wait_ge(lowered, 1)
                act.activation(sc[:], sc[:], ACT.Exp).then_inc(raised, 1)
                for b in range(4):
                    act.wait_ge(mixed, b + 1)
                    act.activation(o[:, 2 * b:2 * b + 2, :], bank[4 + b][0:HD, :].rearrange("p (h t) -> p h t", h=2), ACT.Copy)\
                       .then_inc(copied, 1)
                act.wait_ge(copied, 4)
                act.dma_start(g.d_n[0:512, :].rearrange("(h d) t -> d h t", d=HD), o[:]).then_inc(stored, 16)
                act.wait_ge(stored, 16)

            @block.tensor
            def _(pe):
                pe.wait_ge(loaded, 16 * 7)
                pe.transpose(bank[0][0:HD, 0:2 * CMP_LEN], pos[:], g.ident[0:2 * CMP_LEN, 0:2 * CMP_LEN]).then_inc(turned, 1)
                for k in range(2):
                    pe.wait_ge(blk_ready, k + 1)
                    for l in range(CMP_LEN):
                        ins = pe.matmul(bank[1 + k][0:HD, 0:2 * CMP], w1[:, k, l, :], blk[:, k, l].rearrange("p g c -> p (g c)"),
                                        start=(l == 0), stop=(l == CMP_LEN - 1))
                    ins.then_inc(h_summed, 1)
                pe.wait_ge(hid_ready, 1)
                pe.matmul(bank[0][0:HD, 0:2 * CMP], w2[:, 0, :], hid[:, 0, :], start=True, stop=True)
                for gr in range(2):
                    ins = pe.matmul(bank[3][0:CMP, HD * gr:HD * gr + HD], hid[:, 1, CMP * gr:CMP * gr + CMP], w2[:, 1, :],
                                    start=True, stop=True)
                ins.then_inc(kv_summed, 1)
                pe.wait_ge(kv_ready, 2)
                pe.wait_ge(q_in, 16)
                for t in range(2):
                    for h in range(HEADS):
                        at = CMP * (HEADS * t + h)
                        gr = h // 4
                        ins = pe.matmul(bank[4][:, at:at + CMP], q[:, h, P * t:P * t + P], k_cmp[:, CMP * gr:CMP * gr + CMP],
                                        start=True, stop=True)
                ins.then_inc(scored, 1)
                pe.wait_ge(weighed, 1)
                for h in range(HEADS):
                    for t in range(2):
                        ins = pe.transpose(bank[h // 2][0:CMP, LAT * (h % 2) + P * t:LAT * (h % 2) + P * t + P], sc[:, t, h, :], g.ident[:])
                    if h % 2:
                        ins.then_inc(p_turned, 1)
                for h in range(HEADS):
                    if h % 2 == 0:
                        pe.wait_ge(p_ready, h // 2 + 1)
                    ins = pe.matmul(bank[4 + h // 2][0:HD, LAT * (h % 2):LAT * (h % 2) + LAT], v_cmp[:, h // 4, :], p_t[:, h, :],
                                    start=True, stop=True)
                    if h % 2:
                        ins.then_inc(mixed, 1)

            @block.vector
            def _(dve):
                step = Steps(dve, stepped)
                dve.wait_ge(turned, 1)
                step(dve.tensor_copy(pos_t[:], bank[0][0:HD, 0:2 * CMP_LEN].rearrange("p (k l) -> p k l", k=2)))
                dve.wait_ge(loaded, 16 * 7)
                for k in range(2):
                    for a in range(2):
                        for gr in range(2):
                            src = kv[:, k, gr, 16 * a:16 * a + 16 * CMP].rearrange("p (c b) -> p b c", b=16)
                            step(dve.tensor_tensor(blk[:, k, 16 * a:16 * a + 16, gr, :], src,
                                                   pos_t[:, k, 16 * a:16 * a + 16].unsqueeze(2).broadcast_to([HD, 16, CMP]), ALU.add))
                    dve.sem_inc(blk_ready, 1)
                dve.wait_ge(h_summed, 2)
                for k in range(2):
                    step(dve.tensor_copy(pre[:, k, :], bank[1 + k][0:HD, 0:2 * CMP]))
                step(dve.tensor_tensor(bend[:], pre[:], pre[:], ALU.mult))
                step(dve.tensor_scalar(bend[:], bend[:], 0.044715, 1.0, ALU.mult, ALU.add))
                dve.tensor_tensor(bend[:], bend[:], pre[:], ALU.mult).then_inc(arg_ready, 1)
                step(dve.tensor_scalar(pre[:], pre[:], 0.5, None, ALU.mult))
                dve.wait_ge(bent, 1)
                dve.scalar_tensor_tensor(hid[:], bend[:], 1.0, pre[:], ALU.add, ALU.mult).then_inc(hid_ready, 1)
                dve.wait_ge(kv_summed, 1)
                dve.tensor_copy(k_cmp[:], bank[0][0:HD, 0:2 * CMP]).then_inc(kv_ready, 1)
                dve.tensor_copy(v_cmp[:], bank[3][0:CMP, 0:2 * HD].rearrange("p (g d) -> p g d", g=2)).then_inc(kv_ready, 1)
                dve.wait_ge(scored, 1)
                dve.wait_ge(bias_in, 16 * 2 * HEADS)
                ends = bias[:, :, :, CMP_LEN - 1:LAT:CMP_STRIDE]
                for t in range(2):
                    step(dve.scalar_tensor_tensor(sc[:, t], bank[4][:, CMP * HEADS * t:CMP * HEADS * (t + 1)].rearrange("p (h c) -> p h c", h=HEADS),
                                                  HD ** -0.5, ends[:, t], ALU.mult, ALU.add))
                step(dve.tensor_reduce(top[:], sc[:], AX_X, ALU.max))
                for t in range(2):
                    step(dve.tensor_tensor(sc[:, t], sc[:, t], top[:, t].unsqueeze(2).broadcast_to([P, HEADS, CMP]), ALU.subtract))
                dve.sem_inc(lowered, 1)
                dve.wait_ge(raised, 1)
                step(dve.tensor_reduce(tot[:], sc[:], AX_X, ALU.add))
                step(dve.reciprocal(tot[:], tot[:]))
                for t in range(2):
                    step(dve.tensor_tensor(sc[:, t], sc[:, t], tot[:, t].unsqueeze(2).broadcast_to([P, HEADS, CMP]), ALU.mult))
                    step(dve.tensor_tensor(sc[:, t], sc[:, t], valid[:, t].unsqueeze(1).broadcast_to([P, HEADS, CMP]), ALU.mult))
                dve.sem_inc(weighed, 1)
                for b in range(4):
                    dve.wait_ge(p_turned, b + 1)
                    dve.tensor_copy(p_t[:, 2 * b:2 * b + 2, :], bank[b][0:CMP, :].rearrange("p (h t) -> p h t", h=2)).then_inc(p_ready, 1)


def phase_attend(nc, g):
    rows = lambda c0, h: g.d_p2[bass.ds(h * HD + c0, HD), :]
    one = lambda a, h: a[bass.ds(h, 1)].rearrange("h r t -> (h r) t")
    kinds = [
        (MLA_DK, lambda h, gr: one(g.d_mq, h), lambda h, gr: one(g.d_mk, h), lambda h, gr: h * HD,
         lambda h, t: g.c_causal[:, t, :], (g.d_o, 0), 0),
        (HD, lambda h, gr: rows(FOX_Q, h), lambda h, gr: rows(FOX_K, h), lambda h, gr: h * HD + 512,
         lambda h, t: g.d_fox[bass.ds(h, 1), :, t, :].rearrange("h p k -> (h p) k"), (g.d_o, 512), 0),
        (HD, lambda h, gr: rows(NSA_Q, h), lambda h, gr: rows(NSA_KS, gr), lambda h, gr: gr * HD + 1024,
         lambda h, t: skewed(g, h, t), (g.d_n, 512), 0),
        (HD, lambda h, gr: rows(NSA_Q, h), lambda h, gr: rows(NSA_KW, gr), lambda h, gr: gr * HD + 1152,
         lambda h, t: skewed(g, h, t), (g.d_n, 1024), 0),
        (HD, lambda h, gr: rows(SWA_Q, h), lambda h, gr: rows(SWA_K, gr), lambda h, gr: gr * HD + 1280,
         lambda h, t: skewed(g, h + HEADS, t), (g.d_o, 1536), 1),
    ]
    W0, W1 = P + 1, LAT + 1
    with ExitStack() as stack:
        s = Scope(nc, stack, "at")
        q, k = s.sb("q", [MLA_DK, 4, LAT]), s.sb("k", [MLA_DK, 4, W1])
        v = s.sb("v", [P, 4, 2, HD])
        bias, p = s.sb("bias", [P, 4, W0 + W1]), s.sb("p", [P, 4, W0 + W1])
        p_t = s.sb("p_t", [P, 2, 3 * P])
        neg, tot = s.sb("neg", [P, 4, 2]), s.sb("tot", [P, 4, 2])
        sinks = s.sb("sinks", [P, 2, HEADS])
        o = s.sb("o", [HD, 2, LAT])
        ps_s = [s.ps(f"ps_s{j}", [P, 512]) for j in range(4)]
        ps_t = [s.ps(f"ps_t{j}", [P, 512]) for j in range(2)]
        ps_o = [s.ps(f"ps_o{j}", [P, 512]) for j in range(2)]
        sinks_in, zero_keys, no_sinks = s.sem("sinks_in"), s.sem("zero_keys"), s.sem("no_sinks")
        in_done = [s.sem(f"in_done{j}") for j in range(4)]
        o_stored = [s.sem(f"o_stored{j}") for j in range(2)]
        (scored, biased, peaked, raised, weighed, turned, p_copied, mixed, o_copied, v_step) = (Signal(s, n, per) for n, per in (
            ("scored", 4), ("biased", 4), ("peaked", 4), ("raised", 8), ("weighed", 4), ("turned", 4),
            ("p_copied", 4), ("mixed", 4), ("o_copied", 4), ("v_step", 16)))

        def rounds(eng, body):
            for n, kind in enumerate(kinds):
                with eng.Fori(0, 2) as gr:
                    body(kind, gr + 2 * n, gr)

        with nc.Block() as block:

            @block.sync
            def _(sp):
                sp.dma_start(sinks[:, 1, :], g.swa_sinks_2[0].partition_broadcast(P)).then_inc(sinks_in, 16)

                def body(kind, i, gr):
                    dk, q_of, k_of, v_of, bias_of, _, _ = kind
                    for j in range(4):
                        h = gr * 4 + j
                        mixed.wait(sp, i, j + 1)
                        for dst, src in ((q[0:dk, j, :], q_of(h, gr)), (k[0:dk, j, 1:W1], k_of(h, gr)),
                                         (v[:, j], g.d_v[:, bass.ds(v_of(h, gr), HD)].rearrange("(t p) c -> p t c", p=P)),
                                         (bias[:, j, 1:W0], bias_of(h, 0)[:, 0:P]), (bias[:, j, W0 + 1:W0 + W1], bias_of(h, 1))):
                            sp.dma_start(dst, src).then_inc(in_done[j], 16)

                rounds(sp, body)

            @block.tensor
            def _(pe):
                pe.sem_inc(mixed.sem, 4)
                pe.wait_ge(zero_keys, 1)

                def mix(i, j):
                    p_copied.wait(pe, i, j + 1)
                    o_copied.wait(pe, i, j + 1)
                    pe.matmul(ps_o[j % 2][0:HD, 0:LAT], v[:, j, 0, :], p_t[:, j % 2, 0:LAT], start=True, stop=False)
                    pe.matmul(ps_o[j % 2][0:HD, P:LAT], v[:, j, 1, :], p_t[:, j % 2, LAT:3 * P], start=False, stop=True)\
                      .then_inc(mixed.sem, 1)

                def body(kind, i, gr):
                    dk = kind[0]
                    for j in range(4):
                        pe.wait_ge(in_done[j], 80 * i + 80)
                        pe.matmul(ps_s[j][:, 0:W0], q[0:dk, j, 0:P], k[0:dk, j, 0:W0], start=True, stop=True)
                        pe.matmul(ps_s[j][:, W0:W0 + W1], q[0:dk, j, P:LAT], k[0:dk, j, :], start=True, stop=True).then_inc(scored.sem, 1)
                    for j in range(4):
                        weighed.wait(pe, i, j + 1)
                        for b, at in enumerate((1, W0 + 1, W0 + 1 + P)):
                            ins = pe.transpose(ps_t[j % 2][:, P * b:P * b + P], p[:, j, at:at + P], g.ident[:])
                        ins.then_inc(turned.sem, 1)
                        if j:
                            mix(i, j - 1)
                    mix(i, 3)

                rounds(pe, body)

            @block.vector
            def _(dve):
                dve.memset(k[:, :, 0:1], 0.0).then_inc(zero_keys, 1)
                dve.memset(sinks[:, 0, :], NEG).then_inc(no_sinks, 1)
                dve.wait_ge(sinks_in, 16)
                dve.wait_ge(no_sinks, 1)

                def body(kind, i, gr):
                    scale = kind[0] ** -0.5
                    step = Chain(dve, v_step, i)
                    for j in range(4):
                        at = bass.ds(gr * 4 + j, 1)
                        step(dve.tensor_copy(bias[:, j, 0:W0 + 1:W0], sinks[:, kind[6], at].broadcast_to([P, 2])))
                        scored.wait(dve, i, j + 1)
                        step.tell(dve.scalar_tensor_tensor(p[:, j, :], ps_s[j][:, 0:W0 + W1], scale, bias[:, j, :], ALU.mult, ALU.add),
                                  biased, j + 1)
                        step(dve.tensor_reduce(neg[:, j, 0:1], p[:, j, 0:W0], AX_X, ALU.max, negate=True))
                        step.tell(dve.tensor_reduce(neg[:, j, 1:2], p[:, j, W0:W0 + W1], AX_X, ALU.max, negate=True), peaked, j + 1)
                    for j in range(5):
                        if j < 4:
                            raised.wait(dve, i, 2 * j + 2)
                            step(dve.reciprocal(tot[:, j, :], tot[:, j, :]))
                            step(dve.tensor_scalar(p[:, j, 0:W0], p[:, j, 0:W0], tot[:, j, 0:1], None, ALU.mult))
                            step.tell(dve.tensor_scalar(p[:, j, W0:W0 + W1], p[:, j, W0:W0 + W1], tot[:, j, 1:2], None, ALU.mult),
                                      weighed, j + 1)
                        if j:
                            turned.wait(dve, i, j)
                            step.tell(dve.tensor_copy(p_t[:, (j - 1) % 2, :], ps_t[(j - 1) % 2][:, 0:3 * P]), p_copied, j)
                    step.end()

                rounds(dve, body)

            @block.scalar
            def _(act):
                act.sem_inc(o_copied.sem, 2)
                for j in range(2):
                    act.sem_inc(o_stored[j], 16)

                def body(kind, i, gr):
                    dram, r0 = kind[5]
                    for j in range(4):
                        peaked.wait(act, i, j + 1)
                        for t, cols in enumerate((slice(0, W0), slice(W0, W0 + W1))):
                            act.activation(p[:, j, cols], p[:, j, cols], ACT.Exp, bias=neg[:, j, t:t + 1],
                                           accum_out=tot[:, j, t:t + 1]).then_inc(raised.sem, 1)
                    for j in range(4):
                        mixed.wait(act, i, j + 5)
                        act.wait_ge(o_stored[j % 2], 32 * i + 16 * (j // 2) + 16)
                        act.activation(o[:, j % 2, :], ps_o[j % 2][0:HD, 0:LAT], ACT.Copy).then_inc(o_copied.sem, 1)
                        o_copied.wait(act, i, j + 3)
                        act.dma_start(dram[bass.ds(gr * 256 + (r0 + HD * j), HD), :], o[:, j % 2, :]).then_inc(o_stored[j % 2], 16)

                rounds(act, body)
                for j in range(2):
                    act.wait_ge(o_stored[j], 32 * 2 * len(kinds) + 16)


def phase_gather(nc, g):
    with ExitStack() as stack:
        s = Scope(nc, stack, "ga")
        g.ring.place_parts(s)
        o = s.sb("o", [P, KT, LAT])
        gates, parts = s.sb("gates", [P, 3, 4, LAT]), s.sb("parts", [P, 3, 4, LAT])
        sq = s.sb("sq", [P, 4, LAT])
        rstd = s.sb("rstd", [P, 4, LAT])
        rows, cols, eps = s.sb("rows", [KT, P]), s.sb("cols", [P, KT]), s.sb("eps", [P, 1])
        zeros = s.sb("zeros", [P, P])
        banks = [s.ps(f"bank{i}", [P, 512]) for i in range(8)]
        parts_in, gates_in, o_in, rows_in, bent, stepped, mixed, turned, squared, summed, rooted, ready = (s.sem(n) for n in (
            "parts_in", "gates_in", "o_in", "rows_in", "bent", "stepped", "mixed", "turned", "squared", "summed", "rooted", "ready"))
        eps_set = s.sem("eps_set")
        n_o = g.ring.take(KT)

        with nc.Block() as block:

            @block.sync
            def _(sp):
                deep_loads(sp, g, n_o, g.w_out_2[0], KT)

            @block.scalar
            def _(act):
                act.dma_start(rows[:], g.group_norm_2[0].rearrange("(k p) -> k p", p=P)).then_inc(rows_in, 16)
                for h in range(HEADS):
                    half = slice(HD * (h % 2), HD * (h % 2) + HD)
                    row = NSA_GATE + 3 * h
                    act.dma_start(gates[half, :, h // 2, :], g.d_p2[row:row + 3, :].partition_broadcast(HD)).then_inc(gates_in, 16)
                for j in range(3):
                    act.dma_start(parts[:, j], g.d_n[512 * j:512 * j + 512, :].rearrange("(k p) t -> p k t", p=P)).then_inc(parts_in, 16)
                for k in (0, 4, 12):
                    act.dma_start(o[:, k:k + 4, :], g.d_o[P * k:P * (k + 4), :].rearrange("(k p) t -> p k t", p=P)).then_inc(o_in, 16)
                act.wait_ge(gates_in, 16 * HEADS)
                act.activation(gates[:], gates[:], ACT.Tanh, scale=0.5).then_inc(bent, 1)
                act.wait_ge(o_in, 48)
                act.wait_ge(eps_set, 1)
                for n, k in enumerate((0, 4, 12, 8)):
                    if n == 3:
                        act.wait_ge(mixed, 1)
                    if n:
                        act.wait_ge(summed, n)
                    act.activation(sq[:], o[:, k:k + 4, :], ACT.Square).then_inc(squared, 1)
                for n in range(4):
                    act.wait_ge(summed, n + 1)
                    act.activation(rstd[:, n, :], banks[n][:, 0:LAT], ACT.Sqrt, bias=eps[:, 0:1], scale=1.0 / 512).then_inc(rooted, 1)
                act.wait_ge(ready, 1)
                deep_splits(act, g.ring.split_high, n_o, o, KT)

            @block.tensor
            def _(pe):
                pe.wait_ge(rows_in, 16)
                pe.transpose(banks[4][:, 0:KT], rows[:], g.ident[0:KT, 0:KT]).then_inc(turned, 1)
                for n in range(4):
                    pe.wait_ge(squared, n + 1)
                    for k in range(4):
                        ins = pe.matmul(banks[n][:, 0:LAT], g.ones[:], sq[:, k, :], start=(k == 0), stop=(k == 3))
                    ins.then_inc(summed, 1)
                pe.wait_ge(ready, 1)
                deep_products(pe, g, n_o, KT, banks, zeros[:])

            @block.vector
            def _(dve):
                step = Steps(dve, stepped)
                dve.memset(eps[:], EPS).then_inc(eps_set, 1)
                step(dve.memset(zeros[:], 0.0))
                dve.wait_ge(turned, 1)
                step(dve.tensor_copy(cols[:], banks[4][:, 0:KT]))
                dve.wait_ge(parts_in, 48)
                dve.wait_ge(bent, 1)
                step(dve.scalar_tensor_tensor(parts[:], gates[:], 1.0, parts[:], ALU.add, ALU.mult))
                step(dve.tensor_tensor(parts[:, 0], parts[:, 0], parts[:, 1], ALU.add))
                step(dve.tensor_tensor(parts[:, 0], parts[:, 0], parts[:, 2], ALU.add))
                step(dve.tensor_scalar(o[:, 8:12, :], parts[:, 0], 0.5, None, ALU.mult))
                dve.sem_inc(mixed, 1)
                dve.wait_ge(rooted, 4)
                dve.wait_ge(o_in, 48)
                step(dve.reciprocal(rstd[:], rstd[:]))
                for n, k in enumerate((0, 4, 12, 8)):
                    for kt in range(k, k + 4):
                        step(dve.scalar_tensor_tensor(o[:, kt, :], o[:, kt, :], cols[:, kt:kt + 1], rstd[:, n, :], ALU.mult, ALU.mult))
                dve.sem_inc(ready, 1)
                deep_splits(dve, g.ring.split_low, n_o, o, KT)
                g.ring.wait_done(dve, n_o + KT - 1, 0)
                add_scaled(dve, step, g, banks, None)


def build(nc, g):
    with ExitStack() as stack:
        top = Scope(nc, stack, "all")
        g.ring = Ring(top)
        g.ident = top.sb("ident", [P, P])
        g.ones = top.sb("ones", [P, P])
        g.x_t = top.sb("x_t", [P, KT, LAT])
        cols = top.sb("cols", [P, 4 * KT])
        g.d_mod = nc.dram_tensor("mod", (2, 6 * D), F32).ap()
        g.d_p = nc.dram_tensor("proj", (N_IN, TOK), F32).ap()
        g.d_p2 = nc.dram_tensor("proj2", (N_IN2, LAT), F32).ap()
        g.d_mq = nc.dram_tensor("mla_q", (HEADS, MLA_DK, LAT), F32).ap()
        g.d_mk = nc.dram_tensor("mla_k", (HEADS, MLA_DK, LAT), F32).ap()
        g.d_v = nc.dram_tensor("values", (LAT, V_COLS), F32).ap()
        g.d_frow = nc.dram_tensor("fox_sums", (HEADS, LAT), F32).ap()
        g.d_fox = nc.dram_tensor("fox_bias", (HEADS, P, 2, LAT), F32).ap()
        g.d_skew = nc.dram_tensor("distance_bias", (2 * HEADS, P * 512 + P), F32).ap()
        g.d_n = nc.dram_tensor("nsa_parts", (3 * 512, LAT), F32).ap()
        g.d_o = nc.dram_tensor("mixed", (D, LAT), F32).ap()
        phase_ada(nc, g)
        with ExitStack() as inner:
            g.h = Scope(nc, inner, "h").sb("h", [P, KT, TOK])
            phase_norm1(nc, g)
            phase_project(nc, g, "wi", g.w_in[0], g.d_p, g.h,
                          [(0, 2, LAT), (RW_W, 4, TOK), (CONV0, 2, LAT), (CONV0 + GDN_W, 4, TOK), (Z0, 2, LAT), (GATE0, 8, LAT)],
                          [(3 * RW_W, RW_COLS - 3 * RW_W, TOK), (AB0, 4 * GDN_HEADS, TOK)])
        with ExitStack() as inner:
            mixers = Scope(nc, inner, "mx")
            g.o_a = mixers.sb("o_a", [P, RW_HEADS // 2, LAT])
            with ExitStack() as scans:
                shared = Scope(nc, scans, "sc")
                g.tri = shared.sb("tri", [P, 2, 2, P])
                g.mask = shared.sb("mask", [P, 2, P])
                g.level = shared.sb("level", [P, 8, P], I32)
                phase_rwkv(nc, g)
                g.o_b = shared.sb("o_b", [P, GDN_HEADS, LAT])
                phase_gdn(nc, g)
                phase_merge(nc, g)
        with ExitStack() as inner:
            h = Scope(nc, inner, "h2").sb("h", [P, KT, LAT])
            m = g.d_mod[0]
            phase_norm(nc, g, "n2", [g.norm2_w[0], m[3 * D:4 * D], m[4 * D:5 * D], m[5 * D:6 * D]], h, cols, True)
            phase_ffn(nc, g, "f1", h, g.ffn_w_gate_up[0], g.ffn_w_down[0], FFN, True, cols[:, 3 * KT:4 * KT])
        with ExitStack() as inner:
            h = Scope(nc, inner, "h3").sb("h", [P, KT, LAT])
            phase_norm(nc, g, "n3", [g.final_norm_w], g.x_t, cols[:, 0:KT], False)
            phase_norm(nc, g, "n4", [g.norm_attn_2[0]], h, cols[:, 0:KT], False)
            phase_project(nc, g, "w2", g.w_in_2[0], g.d_p2, h, [(0, 8, LAT)], [(4096, N_IN2 - 4096, LAT)])
        phase_latent(nc, g)
        phase_tables(nc, g)
        phase_compressed(nc, g)
        phase_attend(nc, g)
        phase_gather(nc, g)
        with ExitStack() as inner:
            h = Scope(nc, inner, "h4").sb("h", [P, KT, LAT])
            phase_norm(nc, g, "n5", [g.norm_mlp_2[0]], h, cols[:, 0:KT], False)
            phase_ffn(nc, g, "f2", h, g.w_up_2[0], g.w_down_2[0], FFN_2, False, None)
        phase_norm(nc, g, "n6", [g.final_norm_2], g.x_t, cols[:, 0:KT], False)
        phase_out(nc, g, g.x_t)


class Names:
    pass


_OUT = (1, LAT, D)


def constants():
    import numpy as np

    i = np.arange(32)
    rot = np.zeros((96, 96))
    rot[80 + i[:16], 64 + i[:16]] = -1.0
    rot[64 + i[:16], 80 + i[:16]] = 1.0
    inv = np.float32(10000.0) ** (-np.arange(0, 32, 2, dtype=np.float32) / np.float32(32))
    ang = np.arange(LAT, dtype=np.float32)[None, :] * np.tile(inv, 2)[:, None]
    rope = np.concatenate([np.stack([np.ones((64, LAT)), np.zeros((64, LAT))], 1),
                           np.stack([np.cos(ang), np.sin(ang)], 1)])
    dist = LAT - 1 - np.arange(512)
    d = np.maximum(dist, 0)
    large = 16 + (np.log(np.maximum(d, 1).astype(np.float32) / np.float32(16)) / np.float32(np.log(REL_MAX / 16))
                  * np.float32(16)).astype(np.int32)
    bucket = np.where(d < 16, d, np.minimum(large, 31))
    hot = np.zeros((33, 2, 512))
    hot[bucket, :, np.arange(512)] = 1.0
    hot[32, :, :] = np.where(np.stack([dist < 0, (dist < 0) | (dist >= P)]), NEG, 0.0)
    rows = (np.arange(P)[:, None] + P * np.arange(2)[None, :])[:, :, None]
    s, t = np.arange(P)[:, None], np.arange(P)[None, :]
    lead, half = P - 1 - s, P // 2
    tri = np.stack([[(s <= t) * 1.0 - (s < half), (s < t) * 1.0 - (s < half)],
                    [(lead <= t) * 1.0 - (lead < half), (lead < t) * 1.0 - (lead < half)]])
    level = [(s // n % 2 == 1) & (t // n == s // n - 1) for n in (1, 2, 4, 8, 16, 32, 64)]
    f = lambda a: np.ascontiguousarray(a, np.float32)
    return {
        "c_ident": f(s == t), "c_ones": f(s + t >= 0),
        "c_tri": f(tri.transpose(2, 0, 1, 3)),
        "c_mid": f(np.concatenate([s < half, lead < half], 1)),
        "c_mask": f(np.stack([s < t, s <= t], 1)),
        "c_level": np.ascontiguousarray(np.stack(level + [level[0].T], 1).astype(np.int32)),
        "c_back": f(np.stack([lead <= t, lead == t, s > t], 1)),
        "c_rot": f(rot), "c_rope": f(rope), "c_bucket": f(hot),
        "c_causal": f(np.where(np.arange(LAT) <= rows, 0.0, NEG)),
        "c_valid": f(rows >= CMP_STRIDE * np.arange(CMP) + CMP_LEN - 1),
        "c_pairs": f(s // 64 == t // 64),
        "c_residue": f(np.concatenate([s % 4 == r for r in range(4)] + [s % 2 == r for r in range(2)], 1)),
    }


def kernel(**inputs):
    import numpy as _np
    import concourse.bacc as _bacc
    from concourse import mybir as _mybir
    from concourse.bass_utils import run_bass_kernel_spmd as _run

    nc = _bacc.Bacc("TRN2", target_bir_lowering=False, num_devices=1)
    g = Names()
    arrays = {}
    for name, a in list(inputs.items()) + list(constants().items()):
        a = _np.ascontiguousarray(a)
        arrays[f"in_{name}_dram"] = a
        vars(g)[name] = nc.dram_tensor(f"in_{name}_dram", a.shape, _mybir.dt.from_np(a.dtype), kind="ExternalInput").ap()
    g.out = nc.dram_tensor("out_0_dram", _OUT, F32, kind="ExternalOutput").ap()
    build(nc, g)
    r = _run(nc, [arrays], core_ids=[0])
    return r.results[0]["out_0_dram"]
```

```python
from contextlib import ExitStack

import concourse.bass as bass
from concourse import mybir

F32 = mybir.dt.float32
F32R = mybir.dt.float32r
I32 = mybir.dt.int32
ALU = mybir.AluOpType
ACT = mybir.ActivationFunctionType
AX_X = mybir.AxisListType.X

P = 128
D = 2048
KT = D // P
LAT = 256
CTX = 256
TOK = LAT + CTX
EPS = 1e-6
SLOTS = 4
SPLITS = 2
CHUNK = 2048

RW_HEADS, RW_DIM = 16, 64
RW_W = RW_HEADS * RW_DIM
RANK = 96
GATE_RANK = 64
RW_COLS = 3 * RW_W + 4 * RANK + GATE_RANK
GDN_HEADS = 8
GDN_W = GDN_HEADS * P
TAPS = 5
CONV0 = RW_COLS
Z0 = CONV0 + 3 * GDN_W
AB0 = Z0 + GDN_W
GATE0 = AB0 + 4 * GDN_HEADS
N_IN = GATE0 + 2 * D
FFN, FFN_2 = 5632, 8192
N_IN2 = 4160


class Scope:

    def __init__(self, nc, stack, name):
        self.nc, self.stack, self.name, self.sems = nc, stack, name, []
        stack.callback(self.clear)

    def clear(self):
        if self.sems:
            self.nc.clear_and_free_semaphores(self.sems)
            self.nc.all_engine_barrier()

    def sb(self, name, shape, dt=F32):
        return self.stack.enter_context(self.nc.sbuf_tensor(f"{self.name}_{name}", shape, dt))

    def ps(self, name, shape):
        return self.stack.enter_context(self.nc.psum_tensor(f"{self.name}_{name}", shape, F32))

    def sem(self, name):
        self.sems.append(self.nc.alloc_semaphore(name=f"{self.name}_{name}"))
        return self.sems[-1]


class Ring:

    def __init__(self, scope):
        self.slots = scope.sb("ring", [P, SLOTS, CHUNK])
        self.full = [scope.sem(f"slot_full{s}") for s in range(SLOTS)]
        self.used, self.highs, self.done = scope.sem("chunks_used"), scope.sem("chunks_high"), scope.sem("chunks_done")
        self.n = self.first = 0

    def place_parts(self, scope):
        self.high = scope.sb("chunk_high", [P, SPLITS, CHUNK], F32R)
        self.low = scope.sb("chunk_low", [P, SPLITS, CHUNK], F32R)
        self.x_high = scope.sb("x_high", [P, SPLITS, LAT], F32R)
        self.x_low = scope.sb("x_low", [P, SPLITS, LAT], F32R)

    def take(self, count):
        at = self.n
        self.n += count
        return at

    def load(self, sp, n, i, src, kt, width):
        sp.wait_ge(self.used, 8 * i + n + 1)
        dst = self.slots[:, n % SLOTS, 0:kt * width].rearrange("p (k n) -> p k n", k=kt)
        sp.dma_start(dst, src).then_inc(self.full[n % SLOTS], 16)

    def wait(self, eng, n, i):
        eng.wait_ge(self.full[n % SLOTS], 16 * (8 // SLOTS) * i + 16 * (n // SLOTS + 1))

    def wait_used(self, eng, n, i):
        eng.wait_ge(self.used, 8 * i + SLOTS + n + 1)

    def wait_done(self, eng, n, i):
        eng.wait_ge(self.done, 8 * i + SPLITS + n - self.first + 1)

    def split_high(self, act, n, i, size, x=None):
        self.wait(act, n, i)
        act.wait_ge(self.done, 8 * i + n - self.first + 1)
        if x is not None:
            act.activation(self.x_high[:, n % SPLITS, :], x, ACT.Copy)
        act.activation(self.high[:, n % SPLITS, 0:size], self.slots[:, n % SLOTS, 0:size], ACT.Copy).then_inc(self.highs, 1)

    def split_low(self, dve, n, i, size, x=None):
        dve.wait_ge(self.highs, 8 * i + n - self.first + 1)
        if x is not None:
            dve.tensor_tensor(self.x_low[:, n % SPLITS, :], x, self.x_high[:, n % SPLITS, :], ALU.subtract)
        dve.tensor_tensor(self.low[:, n % SPLITS, 0:size], self.slots[:, n % SLOTS, 0:size],
                          self.high[:, n % SPLITS, 0:size], ALU.subtract).then_inc(self.used, 1)

    def view(self, n, kt, width):
        return self.slots[:, n % SLOTS, 0:kt * width].rearrange("p (k n) -> p k n", k=kt)

    def parts(self, n, kt, width):
        return [t[:, n % SPLITS, 0:kt * width].rearrange("p (k n) -> p k n", k=kt) for t in (self.high, self.low)]


class Steps:

    def __init__(self, eng, sem, base=0):
        self.eng, self.sem, self.n, self.base = eng, sem, 0, base

    def __call__(self, ins):
        self.n += 1
        ins.then_inc(self.sem, 1)
        self.settle()

    def free(self, ins):
        self.n += 1
        ins.then_inc(self.sem, 1)

    def settle(self):
        self.eng.wait_ge(self.sem, self.base + self.n)


def phase_ada(nc, g):
    blocks = 6 * D // 512
    n0 = g.ring.take(blocks * 4)
    g.ring.first = g.ring.n
    with ExitStack() as stack:
        s = Scope(nc, stack, "ada")
        crow = s.sb("crow", [2 * KT, P])
        ccol = s.sb("ccol", [P, 2 * KT])
        half = s.sb("half", [P, 2 * KT])
        bias = s.sb("bias", [2, 6 * D])
        mod = s.sb("mod", [2, 6 * D])
        ps_t = s.ps("ps_t", [P, 512])
        acc = [s.ps(f"acc{i}", [P, 512]) for i in range(2)]
        rows_in, bias_in = s.sem("rows_in"), s.sem("bias_in")
        turned, halved, stepped, silu_done = s.sem("turned"), s.sem("halved"), s.sem("stepped"), s.sem("silu_done")
        bank_free, stored = s.sem("bank_free"), s.sem("stored")

        with nc.Block() as block:

            @block.sync
            def _(sp):
                w = g.w_ada[0].rearrange("(k p) n -> p k n", p=P)
                with sp.Fori(0, blocks // 2) as i:
                    for j in range(8):
                        g.ring.load(sp, n0 + j, i, w[:, 4 * (j % 4):4 * (j % 4) + 4,
                                                     bass.ds(i * 1024 + (j // 4) * 512, 512)], 4, 512)

            @block.gpsimd
            def _(pool):
                pool.dma_start(g.ident[:], g.c_ident).then_inc(rows_in, 16)
                pool.dma_start(crow[0:KT, :], g.c.rearrange("a (k p) -> (a k) p", p=P)).then_inc(rows_in, 16)
                pool.dma_start(crow[KT:2 * KT, :], g.c_ctx.rearrange("(k p) -> k p", p=P)).then_inc(rows_in, 16)
                for r in range(2):
                    pool.dma_start(bias[r:r + 1, :], g.b_ada).then_inc(bias_in, 16)
                pool.wait_ge(bank_free, blocks + 2)
                pool.dma_start(g.d_mod, mod[:]).then_inc(stored, 16)
                pool.wait_ge(stored, 16)

            @block.tensor
            def _(pe):
                pe.sem_inc(g.ring.used, SLOTS)
                pe.sem_inc(g.ring.done, SPLITS)
                pe.wait_ge(rows_in, 48)
                pe.transpose(ps_t[:, 0:2 * KT], crow[:], g.ident[0:2 * KT, 0:2 * KT]).then_inc(turned, 1)
                pe.wait_ge(silu_done, 1)
                with pe.Fori(0, blocks // 2) as i:
                    for j in range(8):
                        b, q = j // 4, j % 4
                        g.ring.wait(pe, n0 + j, i)
                        if q == 0:
                            pe.wait_ge(bank_free, 2 * i + b + 1)
                        w = g.ring.view(n0 + j, 4, 512)
                        for k in range(4):
                            kt = 4 * q + k
                            ins = pe.matmul(acc[b][0:2, :], ccol[:, kt:kt + KT + 1:KT], w[:, k, :],
                                            start=(kt == 0), stop=(kt == KT - 1))
                        ins.then_inc(g.ring.used, 1)

            @block.scalar
            def _(act):
                act.wait_ge(turned, 1)
                act.activation(half[:], ps_t[:, 0:2 * KT], ACT.Tanh, scale=0.5).then_inc(halved, 1)

            @block.vector
            def _(dve):
                dve.sem_inc(bank_free, 2)
                step = Steps(dve, stepped)
                dve.wait_ge(halved, 1)
                step(dve.tensor_scalar(half[:], half[:], 0.5, 0.5, ALU.mult, ALU.add))
                dve.tensor_tensor(ccol[:], ps_t[:, 0:2 * KT], half[:], ALU.mult).then_inc(silu_done, 1)
                dve.wait_ge(bias_in, 32)
                with dve.Fori(0, blocks // 2) as i:
                    for b in range(2):
                        g.ring.wait_used(dve, n0 + 4 * b + 3, i)
                        cols = bass.ds(i * 1024 + b * 512, 512)
                        dve.tensor_tensor(mod[:, cols], acc[b][0:2, :], bias[:, cols], ALU.add)\
                           .then_inc(bank_free, 1)



def phase_norm1(nc, g):
    with ExitStack() as stack:
        s = Scope(nc, stack, "n1")
        rows = s.sb("rows", [5 * KT, P])
        cols = s.sb("cols", [P, 5 * KT])
        gain = s.sb("gain", [P, 2, KT])
        xin = s.sb("xin", [P, 2, D])
        ctx_t = s.sb("ctx_t", [P, KT, CTX])
        sq = s.sb("sq", [P, 2, TOK])
        rstd = s.sb("rstd", [P, TOK])
        eps = s.sb("eps", [P, 1])
        ps_x = [s.ps(f"ps_x{i}", [P, 4, P]) for i in range(4)]
        ps_s = s.ps("ps_s", [P, TOK])
        ps_r = s.ps("ps_r", [P, 512])
        rows_in = s.sem("rows_in")
        x_in = [s.sem(f"x_in{i}") for i in range(2)]
        rows_turned, cols_done, turned, copied_dve, copied_act = (s.sem(n) for n in (
            "rows_turned", "cols_done", "turned", "copied_dve", "copied_act"))
        squared, summed, rooted, eps_set, stepped = (s.sem(n) for n in ("squared", "summed", "rooted", "eps_set", "stepped"))
        sources = [(g.x[0], 0), (g.x[0], P), (g.ctx[0], 0), (g.ctx[0], P)]

        def dst(t, q):
            tile, c0 = (g.x_t, t * P) if t < 2 else (ctx_t, t * P - LAT)
            return tile[:, 4 * q:4 * q + 4, c0:c0 + P]

        def tokens(kt):
            return ((g.x_t[:, kt, :], slice(0, LAT)), (ctx_t[:, kt, :], slice(LAT, TOK)))

        with nc.Block() as block:

            @block.sync
            def _(sp):
                for t in range(4):
                    src, r0 = sources[t]
                    if t >= 2:
                        sp.wait_ge(turned, 4 * (t - 1))
                    sp.dma_start(xin[:, t % 2, :], src[r0:r0 + P, :]).then_inc(x_in[t % 2], 16)

            @block.gpsimd
            def _(pool):
                m = g.d_mod
                for k, src in enumerate((g.norm1_w[0], m[0, 0:D], m[0, D:2 * D], m[1, 0:D], m[1, D:2 * D])):
                    pool.dma_start(rows[KT * k:KT * (k + 1), :], src.rearrange("(k p) -> k p", p=P)).then_inc(rows_in, 16)
                pool.dma_start(g.ones[:], g.c_ones).then_inc(rows_in, 16)

            @block.tensor
            def _(pe):
                for t in range(4):
                    pe.wait_ge(x_in[t % 2], 16 * (t // 2 + 1))
                    for q in range(4):
                        n = 4 * t + q
                        if n >= 4:
                            pe.wait_ge((copied_dve, copied_act)[n % 2], (n - 4) // 2 + 1)
                        for k in range(4):
                            ins = pe.transpose(ps_x[n % 4][:, k, :], xin[:, t % 2, (4 * q + k) * P:(4 * q + k + 1) * P], g.ident[:])
                        ins.then_inc(turned, 1)
                pe.wait_ge(rows_in, 96)
                pe.transpose(ps_r[:, 0:5 * KT], rows[:], g.ident[0:5 * KT, 0:5 * KT]).then_inc(rows_turned, 1)
                for kt in range(KT):
                    pe.wait_ge(squared, 2 * (kt + 1))
                    pe.matmul(ps_s[:], g.ones[:], sq[:, kt % 2, :], start=(kt == 0), stop=(kt == KT - 1)).then_inc(summed, 1)

            @block.vector
            def _(dve):
                step = Steps(dve, stepped)
                dve.memset(eps[:], EPS).then_inc(eps_set, 1)
                for n in range(0, 16, 2):
                    dve.wait_ge(turned, n + 1)
                    dve.tensor_copy(dst(n // 4, n % 4), ps_x[n % 4][:]).then_inc(copied_dve, 1)
                dve.wait_ge(rows_turned, 1)
                step(dve.tensor_copy(cols[:], ps_r[:, 0:5 * KT]))
                for r in range(2):
                    step(dve.scalar_tensor_tensor(gain[:, r, :], cols[:, (2 + 2 * r) * KT:(3 + 2 * r) * KT], 1.0,
                                                  cols[:, 0:KT], ALU.add, ALU.mult))
                dve.wait_ge(rooted, 1)
                step(dve.reciprocal(rstd[:], rstd[:]))
                for kt in range(KT):
                    for r, (src, tok) in enumerate(tokens(kt)):
                        step.free(dve.scalar_tensor_tensor(g.h[:, kt, tok], src, gain[:, r, kt:kt + 1], rstd[:, tok],
                                                           ALU.mult, ALU.mult))
                step.settle()
                for kt in range(KT):
                    for r, (src, tok) in enumerate(tokens(kt)):
                        step.free(dve.tensor_scalar(g.h[:, kt, tok], g.h[:, kt, tok],
                                               cols[:, (1 + 2 * r) * KT + kt:(1 + 2 * r) * KT + kt + 1], None, ALU.add))

            @block.scalar
            def _(act):
                for n in range(1, 16, 2):
                    act.wait_ge(turned, n + 1)
                    act.activation(dst(n // 4, n % 4), ps_x[n % 4][:], ACT.Copy).then_inc(copied_act, 1)
                act.wait_ge(copied_act, 8)
                act.wait_ge(copied_dve, 8)
                for kt in range(KT):
                    if kt >= 2:
                        act.wait_ge(summed, kt - 1)
                    for src, tok in tokens(kt):
                        act.activation(sq[:, kt % 2, tok], src, ACT.Square).then_inc(squared, 1)
                act.wait_ge(summed, KT)
                act.wait_ge(eps_set, 1)
                act.activation(rstd[:], ps_s[:], ACT.Sqrt, bias=eps[:, 0:1], scale=1.0 / D).then_inc(rooted, 1)


def wide_loads(sp, g, n0, source, blocks, width=512):
    with sp.Fori(0, blocks // 2) as i:
        for j in range(8):
            g.ring.load(sp, n0 + j, i, source(2 * i + j // 4, j % 4), 4, width)


def split_products(pe, out, w, x, start, stop):
    pe.matmul(out, w[0], x[0], start=start, stop=False)
    pe.matmul(out, w[0], x[1], start=False, stop=False)
    return pe.matmul(out, w[1], x[0], start=False, stop=stop)


def wide_products(pe, g, n0, act, tokens, blocks, banks, summed, wait_free):
    with pe.Fori(0, blocks // 2) as i:
        for j in range(8):
            b, q = j // 4, j % 4
            g.ring.wait_used(pe, n0 + j, i)
            w = g.ring.parts(n0 + j, 4, 512)
            for ct in range(4):
                if q == 0:
                    wait_free(i, b, ct)
                for k in range(4):
                    kt = 4 * q + k
                    ins = split_products(pe, banks[4 * b + ct][:, 0:tokens], [a[:, k, P * ct:P * ct + P] for a in w],
                                         [a[:, kt, 0:tokens] for a in act], kt == 0, kt == KT - 1)
                if q == 3 and ct < 3:
                    ins.then_inc(summed, 1)
            ins.then_inc(g.ring.done, 1)


def wide_rounds(eng, n0, blocks, split, evacuate, ahead):
    def one(i, following):
        for j in (2, 3, 4):
            split(n0 + j, i)
        evacuate(i, 0, 0)
        split(n0 + 5, i)
        evacuate(i, 0, 1)
        split(n0 + 6, i)
        split(n0 + 7, i)
        following[0]()
        evacuate(i, 1, 0)
        following[1]()
        evacuate(i, 1, 1)

    if blocks > 2:
        with eng.Fori(0, blocks // 2 - 1) as i:
            one(i, [lambda j=j: split(n0 + j, i + 1) for j in range(2)])
    one(blocks // 2 - 1, ahead)


def split_act(s, h, tokens):
    return s.sb("high", [P, KT, tokens], F32R), s.sb("low", [P, KT, tokens], F32R), s.sem("act_high"), s.sem("act_low")


def split_act_high(act, h, parts):
    for q in range(4):
        act.activation(parts[0][:, 4 * q:4 * q + 4, :], h[:, 4 * q:4 * q + 4, :], ACT.Copy).then_inc(parts[2], 1)


def split_act_low(dve, h, parts):
    for q in range(4):
        dve.wait_ge(parts[2], q + 1)
        dve.tensor_tensor(parts[1][:, 4 * q:4 * q + 4, :], h[:, 4 * q:4 * q + 4, :], parts[0][:, 4 * q:4 * q + 4, :], ALU.subtract)\
           .then_inc(parts[3], 1)


def phase_project(nc, g, name, weights, dst, h, segments, odd):
    with ExitStack() as stack:
        s = Scope(nc, stack, name)
        g.ring.place_parts(s)
        stage = s.sb("stage", [P, 8, TOK])
        banks = [s.ps(f"bank{i}", [P, TOK]) for i in range(8)]
        summed, staged_dve, staged_act = s.sem("summed"), s.sem("staged_dve"), s.sem("staged_act")
        stored = [s.sem(f"stored{i}") for i in range(8)]
        staged = (staged_dve, staged_act)
        starts, done = [], 0
        for _, blocks, _ in segments:
            starts.append((g.ring.take(4 * blocks), done))
            done += blocks
        tiles, chunks = [], []
        for c0, width, tokens in odd:
            per = 4 if width > P else KT
            n = g.ring.take(KT // per)
            chunks.append((n, c0, width, per))
            tiles.append([(len(sum(tiles, [])) + k, min(P, width - k * P), c0 + k * P, k * P, tokens) for k in range(-(-width // P))])
        assert len(sum(tiles, [])) <= 8 and done % 2 == 0
        w = weights.rearrange("(k p) n -> p k n", p=P)
        parts = split_act(s, h, h.shape[2])

        def source(c0):
            return lambda b, q: w[:, 4 * q:4 * q + 4, bass.ds(c0 + b * 512, 512)]

        def evacuate(eng, mine, copy, split, store=None):
            sizes = [4 * 512] * 4 * done + sum([[per * width] * (KT // per) for _, _, width, per in chunks], [])
            first = starts[0][0]

            def chunk(n, i=0):
                split(eng, n, i, sizes[n - first])

            chunk(first)
            chunk(first + 1)
            for k, ((c0, blocks, tokens), (n0, base)) in enumerate(zip(segments, starts)):

                def half(i, b, part):
                    ct = mine + 2 * part
                    if ct < 3:
                        eng.wait_ge(summed, 3 * base + 6 * i + 3 * b + ct + 1)
                    else:
                        g.ring.wait_done(eng, n0 + 4 * b + 3, i)
                    eng.wait_ge(stored[4 * b + ct], 16 * i + 8 * base + 16)
                    copy(stage[:, 4 * b + ct, 0:tokens], banks[4 * b + ct][:, 0:tokens]).then_inc(staged[mine], 1)
                    if store:
                        for ct in (2 * part, 2 * part + 1):
                            eng.wait_ge(staged[ct % 2], 4 + 2 * base + 4 * i + 2 * b + part + 1)
                            store(dst[bass.ds(i * 1024 + (c0 + b * 512 + ct * P), P), 0:tokens],
                                  stage[:, 4 * b + ct, 0:tokens]).then_inc(stored[4 * b + ct], 16)

                following = n0 + 4 * blocks
                wide_rounds(eng, n0, blocks, chunk, half,
                            [(lambda n=n: chunk(n)) if n < first + len(sizes) else (lambda: None) for n in (following, following + 1)])
            for n in range(first + 4 * done + 2, first + len(sizes)):
                chunk(n)
            counts = 3 * done
            for (n, _, _, per), group in zip(chunks, tiles):
                for bank, m, _, _, tokens in group:
                    last = (bank, m) == group[-1][0:2]
                    counts += not last
                    if bank % 2 != mine:
                        continue
                    if last:
                        g.ring.wait_done(eng, n + KT // per - 1, 0)
                    else:
                        eng.wait_ge(summed, counts)
                    eng.wait_ge(stored[bank], 16 + 8 * done)
                    copy(stage[0:m, bank, 0:tokens], banks[bank][0:m, 0:tokens]).then_inc(staged[mine], 1)
            if store:
                for bank, m, r0, _, tokens in sum(tiles, []):
                    eng.wait_ge(staged[bank % 2], 4 + 2 * done + bank // 2 + 1)
                    store(dst[r0:r0 + m, 0:tokens], stage[0:m, bank, 0:tokens]).then_inc(stored[bank], 16)
                for bank in range(8):
                    eng.wait_ge(stored[bank], 16 + 8 * done + 16 * (bank < len(sum(tiles, []))))

        with nc.Block() as block:

            @block.sync
            def _(sp):
                for (c0, blocks, _), (n0, _) in zip(segments, starts):
                    wide_loads(sp, g, n0, source(c0), blocks)
                for n, c0, width, per in chunks:
                    for j in range(KT // per):
                        g.ring.load(sp, n + j, 0, w[:, per * j:per * j + per, c0:c0 + width], per, width)

            @block.tensor
            def _(pe):
                pe.wait_ge(parts[3], 4)
                for (_, blocks, tokens), (n0, base) in zip(segments, starts):
                    wide_products(pe, g, n0, parts[0:2], tokens, blocks, banks, summed,
                                  lambda i, b, ct, base=base: pe.wait_ge(staged[ct % 2], base * 2 + 4 * i + 2 * b + ct // 2 + 1))
                for (n, _, width, per), group in zip(chunks, tiles):
                    for j in range(KT // per):
                        g.ring.wait_used(pe, n + j, 0)
                        wj = g.ring.parts(n + j, per, width)
                        for bank, m, _, off, tokens in group:
                            if j == 0:
                                pe.wait_ge(staged[bank % 2], 2 * done + bank // 2 + 1)
                            for k in range(per):
                                kt = per * j + k
                                ins = split_products(pe, banks[bank][0:m, 0:tokens], [a[:, k, off:off + m] for a in wj],
                                                     [a[:, kt, 0:tokens] for a in parts[0:2]], kt == 0, kt == KT - 1)
                            if kt == KT - 1 and bank != group[-1][0]:
                                ins.then_inc(summed, 1)
                        ins.then_inc(g.ring.done, 1)

            @block.vector
            def _(dve):
                dve.sem_inc(staged_dve, 4)
                split_act_low(dve, h, parts)
                evacuate(dve, 0, lambda o, i: dve.tensor_copy(o, i), g.ring.split_low)

            @block.scalar
            def _(act):
                act.sem_inc(staged_act, 4)
                for i in range(8):
                    act.sem_inc(stored[i], 16)
                split_act_high(act, h, parts)
                evacuate(act, 1, lambda o, i: act.activation(o, i, ACT.Copy), g.ring.split_high, act.dma_start)


def deep_loads(sp, g, n0, w, k_tiles, early=False):
    if early:
        for j in range(SLOTS, k_tiles):
            g.ring.load(sp, n0 + j, 0, w[j * P:(j + 1) * P, :].unsqueeze(1), 1, D)
        return
    if k_tiles // 8:
        with sp.Fori(0, k_tiles // 8) as i:
            for j in range(8):
                g.ring.load(sp, n0 + j, i, w[bass.ds(i * 1024 + j * P, P), :].unsqueeze(1), 1, D)
    for j in range(k_tiles // 8 * 8, k_tiles):
        g.ring.load(sp, n0 + j, 0, w[j * P:(j + 1) * P, :].unsqueeze(1), 1, D)


def deep_splits(eng, split, n0, act, k_tiles):
    if k_tiles // 8:
        with eng.Fori(0, k_tiles // 8) as i:
            for j in range(8):
                split(eng, n0 + j, i, D, act[:, bass.ds(8 * i + j, 1), :].rearrange("p a t -> p (a t)"))
    for j in range(k_tiles // 8 * 8, k_tiles):
        split(eng, n0 + j, 0, D, act[:, j, :])


def deep_products(pe, g, n0, k_tiles, banks, zeros):
    for b in banks:
        pe.matmul(b[:, 0:2], zeros, zeros[:, 0:2], start=True, stop=False, skip_group_check=True)

    def k_tile(n, i):
        g.ring.wait_used(pe, n, i)
        w = g.ring.parts(n, 1, D)
        x = [t[:, n % SPLITS, :] for t in (g.ring.x_high, g.ring.x_low)]
        for ct in range(KT):
            out = banks[ct // 2][:, LAT * (ct % 2):LAT * (ct % 2) + LAT]
            for a, b in ((0, 0), (0, 1), (1, 0)):
                ins = pe.matmul(out, w[a][:, 0, P * ct:P * ct + P], x[b], start=False, stop=False, skip_group_check=True)
        ins.then_inc(g.ring.done, 1)

    with pe.Fori(0, k_tiles // 8) as i:
        for j in range(8):
            k_tile(n0 + j, i)
    for j in range(k_tiles // 8 * 8, k_tiles):
        k_tile(n0 + j, 0)


def phase_norm(nc, g, name, vectors, out, cols, modulated):
    count = len(vectors) * KT
    with ExitStack() as stack:
        s = Scope(nc, stack, name)
        rows = s.sb("rows", [count, P])
        gain = s.sb("gain", [P, KT])
        sq = s.sb("sq", [P, 4, 4, LAT])
        rstd = s.sb("rstd", [P, LAT])
        eps = s.sb("eps", [P, 1])
        ps_s, ps_r = s.ps("ps_s", [P, 512]), s.ps("ps_r", [P, 512])
        rows_in, turned, squared, summed, rooted, stepped, eps_set = (s.sem(n) for n in (
            "rows_in", "turned", "squared", "summed", "rooted", "stepped", "eps_set"))

        with nc.Block() as block:

            @block.sync
            def _(sp):
                for k, v in enumerate(vectors):
                    sp.dma_start(rows[KT * k:KT * (k + 1), :], v.rearrange("(k p) -> k p", p=P)).then_inc(rows_in, 16)

            @block.tensor
            def _(pe):
                pe.wait_ge(rows_in, 16 * len(vectors))
                pe.transpose(ps_r[:, 0:count], rows[:], g.ident[0:count, 0:count]).then_inc(turned, 1)
                for q in range(4):
                    pe.wait_ge(squared, q + 1)
                    for k in range(4):
                        ins = pe.matmul(ps_s[:, 0:LAT], g.ones[:], sq[:, q, k, :], start=(q + k == 0), stop=(q + k == 6))
                ins.then_inc(summed, 1)

            @block.scalar
            def _(act):
                for q in range(4):
                    act.activation(sq[:, q], g.x_t[:, 4 * q:4 * q + 4, :], ACT.Square).then_inc(squared, 1)
                act.wait_ge(summed, 1)
                act.wait_ge(eps_set, 1)
                act.activation(rstd[:], ps_s[:, 0:LAT], ACT.Sqrt, bias=eps[:, 0:1], scale=1.0 / D).then_inc(rooted, 1)

            @block.vector
            def _(dve):
                step = Steps(dve, stepped)
                dve.memset(eps[:], EPS).then_inc(eps_set, 1)
                dve.wait_ge(turned, 1)
                step(dve.tensor_copy(cols[:], ps_r[:, 0:count]))
                if modulated:
                    step(dve.scalar_tensor_tensor(gain[:], cols[:, 2 * KT:3 * KT], 1.0, cols[:, 0:KT], ALU.add, ALU.mult))
                else:
                    step(dve.tensor_copy(gain[:], cols[:, 0:KT]))
                dve.wait_ge(rooted, 1)
                step(dve.reciprocal(rstd[:], rstd[:]))
                for kt in range(KT):
                    step.free(dve.scalar_tensor_tensor(out[:, kt, :], g.x_t[:, kt, :], gain[:, kt:kt + 1], rstd[:], ALU.mult, ALU.mult))
                if modulated:
                    step.settle()
                    for kt in range(KT):
                        step.free(dve.tensor_scalar(out[:, kt, :], out[:, kt, :], cols[:, KT + kt:KT + kt + 1], None, ALU.add))


def phase_merge(nc, g):
    with ExitStack() as stack:
        s = Scope(nc, stack, "me")
        g.ring.place_parts(s)
        gates = s.sb("gates", [P, 2, KT, LAT])
        m = s.sb("m", [P, KT, LAT])
        t = s.sb("t", [P, 2, LAT])
        rows, cols = s.sb("rows", [KT, P]), s.sb("cols", [P, KT])
        zeros = s.sb("zeros", [P, P])
        banks = [s.ps(f"bank{i}", [P, 512]) for i in range(8)]
        gates_in, rows_in, gates_bent, stepped, zeroed, turned, cols_done, read, merged = (s.sem(n) for n in (
            "gates_in", "rows_in", "gates_bent", "stepped", "zeroed", "turned", "cols_done", "read", "merged"))
        n_a, n_b, n_o = g.ring.take(8), g.ring.take(8), g.ring.take(KT)

        with nc.Block() as block:

            @block.sync
            def _(sp):
                deep_loads(sp, g, n_a, g.merge_p_a[0], 8)
                deep_loads(sp, g, n_b, g.merge_p_b[0], 8)
                deep_loads(sp, g, n_o, g.w_out[0], KT)

            @block.scalar
            def _(act):
                act.dma_start(rows[:], g.d_mod[0, 2 * D:3 * D].rearrange("(k p) -> k p", p=P)).then_inc(rows_in, 16)
                for r in range(2):
                    act.dma_start(gates[:, r], g.d_p[GATE0 + r * D:GATE0 + (r + 1) * D, 0:LAT].rearrange("(k p) t -> p k t", p=P))\
                        .then_inc(gates_in, 16)
                deep_splits(act, g.ring.split_high, n_a, g.o_a, 8)
                act.wait_ge(gates_in, 32)
                for r in range(2):
                    act.activation(gates[:, r], gates[:, r], ACT.Tanh, scale=0.5).then_inc(gates_bent, 1)
                deep_splits(act, g.ring.split_high, n_b, g.o_b, 8)
                act.wait_ge(merged, 1)
                deep_splits(act, g.ring.split_high, n_o, m, KT)

            @block.tensor
            def _(pe):
                pe.wait_ge(zeroed, 1)
                pe.wait_ge(rows_in, 16)
                pe.transpose(banks[0][:, 0:KT], rows[:], g.ident[0:KT, 0:KT]).then_inc(turned, 1)
                pe.wait_ge(cols_done, 1)
                deep_products(pe, g, n_a, 8, banks, zeros[:])
                pe.wait_ge(read, 1)
                deep_products(pe, g, n_b, 8, banks, zeros[:])
                pe.wait_ge(merged, 1)
                deep_products(pe, g, n_o, KT, banks, zeros[:])

            @block.vector
            def _(dve):
                step = Steps(dve, stepped)
                dve.memset(zeros[:], 0.0).then_inc(zeroed, 1)
                dve.wait_ge(turned, 1)
                dve.tensor_copy(cols[:], banks[0][:, 0:KT]).then_inc(cols_done, 1)
                dve.wait_ge(cols_done, 1)
                for r, (n, o, then) in enumerate(((n_a, g.o_a, read), (n_b, g.o_b, merged))):
                    deep_splits(dve, g.ring.split_low, n, o, 8)
                    dve.wait_ge(gates_bent, r + 1)
                    step(dve.tensor_scalar(gates[:, r], gates[:, r], 0.5, 0.5, ALU.mult, ALU.add))
                    g.ring.wait_done(dve, n + 7, 0)
                    for b in range(8):
                        ga = gates[:, r, 2 * b:2 * b + 2, :]
                        ps = banks[b][:].rearrange("p (k t) -> p k t", k=2)
                        step.free(dve.tensor_tensor(m[:, 2 * b:2 * b + 2, :] if r == 0 else ga, ga, ps, ALU.mult))
                    step.settle()
                    if r == 1:
                        step(dve.tensor_tensor(m[:], m[:], gates[:, 1], ALU.add))
                    dve.sem_inc(then, 1)
                deep_splits(dve, g.ring.split_low, n_o, m, KT)
                g.ring.wait_done(dve, n_o + KT - 1, 0)
                add_scaled(dve, step, g, banks, cols)


def add_scaled(dve, step, g, banks, cols):
    for kt in range(KT):
        ps = banks[kt // 2][:, LAT * (kt % 2):LAT * (kt % 2) + LAT]
        x = g.x_t[:, kt, :]
        if cols is None:
            step.free(dve.tensor_tensor(x, x, ps, ALU.add))
        else:
            step.free(dve.scalar_tensor_tensor(x, ps, cols[:, kt:kt + 1], x, ALU.mult, ALU.add))


def phase_ffn(nc, g, name, h, w_up, w_down, hidden, gated, cols):
    tiles = hidden // P
    blocks = tiles // (2 if gated else 4)
    with ExitStack() as stack:
        s = Scope(nc, stack, name)
        g.ring.place_parts(s)
        hid = s.sb("hid", [P, tiles, LAT])
        zeros = s.sb("zeros", [P, P])
        t = s.sb("t", [P, 8, LAT])
        banks = [s.ps(f"bank{i}", [P, 512]) for i in range(8)]
        summed, bent, gate_done, hidden_done, stepped, zeroed = (s.sem(n) for n in (
            "summed", "bent", "gate_done", "hidden_done", "stepped", "zeroed"))
        n_up, n_down = g.ring.take(4 * blocks), g.ring.take(tiles)
        v = w_up.rearrange("(k p) n -> p k n", p=P)
        parts = split_act(s, h, LAT)

        def up_columns(b, q):
            return v[:, 4 * q:4 * q + 4, bass.ds(b * 512, 512)]

        def load_up(sp):
            if not gated:
                return wide_loads(sp, g, n_up, up_columns, blocks)
            with sp.Fori(0, blocks // 2) as i:
                for j in range(8):
                    g.ring.load(sp, n_up + j, i, v[:, 4 * (j % 4):4 * (j % 4) + 4,
                                                   bass.ds(i * 512 + (j // 4) * hidden, 512)], 4, 512)

        def wait_free(pe, i, b, ct):
            if gated:
                pe.wait_ge((gate_done, hidden_done)[b], 4 * i + ct + 1)
            else:
                pe.wait_ge(hidden_done, 8 * i + 4 * b + ct + 1)

        with nc.Block() as block:

            @block.sync
            def _(sp):
                load_up(sp)
                deep_loads(sp, g, n_down, w_down, tiles)

            @block.tensor
            def _(pe):
                pe.wait_ge(parts[3], 4)
                wide_products(pe, g, n_up, parts[0:2], LAT, blocks, banks, summed, lambda i, b, ct: wait_free(pe, i, b, ct))
                pe.wait_ge(zeroed, 1)
                pe.wait_ge(hidden_done, tiles + (4 if gated else 8))
                deep_products(pe, g, n_down, tiles, banks, zeros[:])

            @block.scalar
            def _(act):
                split_act_high(act, h, parts)

                def chunk(n, i=0):
                    g.ring.split_high(act, n, i, 4 * 512)

                def bend(i, b, part):
                    if gated and b:
                        return
                    for ct in (2 * part, 2 * part + 1):
                        if ct < 3:
                            act.wait_ge(summed, 6 * i + 3 * b + ct + 1)
                        else:
                            g.ring.wait_done(act, n_up + 4 * b + 3, i)
                        act.wait_ge(hidden_done, (4 if gated else 8) * i + 4 * b + ct + 1)
                        act.activation(t[:, 4 * b + ct, :], banks[4 * b + ct][:, 0:LAT],
                                       ACT.Tanh if gated else ACT.Relu, scale=0.5 if gated else 1.0).then_inc(bent, 1)

                chunk(n_up)
                chunk(n_up + 1)
                wide_rounds(act, n_up, blocks, chunk, bend, [lambda: None] * 2)
                act.wait_ge(hidden_done, tiles + (4 if gated else 8))
                deep_splits(act, g.ring.split_high, n_down, hid, tiles)

            @block.vector
            def _(dve):
                dve.memset(zeros[:], 0.0).then_inc(zeroed, 1)
                dve.sem_inc(hidden_done, 4 if gated else 8)
                dve.sem_inc(gate_done, 4)
                split_act_low(dve, h, parts)

                def chunk(n, i=0):
                    g.ring.split_low(dve, n, i, 4 * 512)

                def tile(i, ct):
                    return hid[:, bass.ds(ct + i * (4 if gated else 8), 1), :].rearrange("p a t -> p (a t)")

                def finish(i, b, part):
                    for ct in (2 * part, 2 * part + 1):
                        if not gated:
                            dve.wait_ge(bent, 8 * i + 4 * b + ct + 1)
                            dve.tensor_tensor(tile(i, 4 * b + ct), t[:, 4 * b + ct, :], banks[4 * b + ct][:, 0:LAT], ALU.mult)\
                               .then_inc(hidden_done, 1)
                        elif b == 0:
                            dve.wait_ge(bent, 4 * i + ct + 1)
                            dve.scalar_tensor_tensor(t[:, ct, :], t[:, ct, :], 1.0, banks[ct][:, 0:LAT], ALU.add, ALU.mult)\
                               .then_inc(gate_done, 1)
                        else:
                            dve.wait_ge(gate_done, 4 * i + ct + 5)
                            if ct < 3:
                                dve.wait_ge(summed, 6 * i + ct + 4)
                            else:
                                g.ring.wait_done(dve, n_up + 7, i)
                            dve.scalar_tensor_tensor(tile(i, ct), t[:, ct, :], 0.5, banks[4 + ct][:, 0:LAT], ALU.mult, ALU.mult)\
                               .then_inc(hidden_done, 1)

                chunk(n_up)
                chunk(n_up + 1)
                wide_rounds(dve, n_up, blocks, chunk, finish, [lambda: None] * 2)
                deep_splits(dve, g.ring.split_low, n_down, hid, tiles)
                g.ring.wait_done(dve, n_down + tiles - 1, 0)
                step = Steps(dve, stepped)
                add_scaled(dve, step, g, banks, cols)


def phase_out(nc, g, h):
    with ExitStack() as stack:
        s = Scope(nc, stack, "out")
        o = s.sb("o", [P, 2, D])
        ps = [s.ps(f"ps{i}", [P, 512]) for i in range(2)]
        turned, copied, stored = s.sem("turned"), s.sem("copied"), s.sem("stored")
        with nc.Block() as block:

            @block.tensor
            def _(pe):
                for n in range(8):
                    t, q = n // 4, n % 4
                    if n >= 2:
                        pe.wait_ge(copied, n - 1)
                    for k in range(4):
                        ins = pe.transpose(ps[n % 2][:, P * k:P * k + P], h[:, 4 * q + k, t * P:(t + 1) * P], g.ident[:])
                    ins.then_inc(turned, 1)

            @block.vector
            def _(dve):
                for n in range(8):
                    dve.wait_ge(turned, n + 1)
                    dve.tensor_copy(o[:, n // 4, 512 * (n % 4):512 * (n % 4) + 512], ps[n % 2][:]).then_inc(copied, 1)

            @block.sync
            def _(sp):
                for t in range(2):
                    sp.wait_ge(copied, 4 * t + 4)
                    sp.dma_start(g.out[0, t * P:(t + 1) * P, :], o[:, t, :]).then_inc(stored, 16)
                sp.wait_ge(stored, 32)


class Signal:

    def __init__(self, scope, name, per=1):
        self.sem, self.per = scope.sem(name), per

    def wait(self, eng, i, k=1):
        eng.wait_ge(self.sem, self.per * i + k)


class Chain:

    def __init__(self, eng, signal, i):
        self.eng, self.source, self.i, self.n = eng, signal, i, 0

    def __call__(self, ins):
        self.n += 1
        ins.then_inc(self.source.sem, 1)
        self.source.wait(self.eng, self.i, self.n)

    def free(self, ins):
        self.n += 1
        ins.then_inc(self.source.sem, 1)

    def tell(self, ins, signal, k=1):
        ins.then_inc(signal.sem, 1)
        signal.wait(self.eng, self.i, k)

    def end(self):
        assert self.n == self.source.per, (self.source.sem, self.n)


def shift_mix(dve, step, out, src, co, ctx):
    step(dve.tensor_scalar(out, src, co[:, 0:1], None, ALU.mult))
    og, sg = (a[:, 0:LAT].rearrange("p (r c) -> p r c", c=64) for a in (out, src))
    moves = [(og[:, :, 1:64], sg[:, :, 0:63]), (og[:, :, 0:63], sg[:, :, 1:64]),
             (out[:, 64:LAT], src[:, 0:LAT - 64]), (out[:, 0:LAT - 64], src[:, 64:LAT])]
    if ctx:
        moves += [(out[:, LAT + 1:TOK], src[:, LAT:TOK - 1]), (out[:, LAT:TOK - 1], src[:, LAT + 1:TOK])]
    for k, (o, s) in enumerate(moves):
        step(dve.scalar_tensor_tensor(o, s, co[:, k + 1:k + 2], o, ALU.mult, ALU.add))


def phase_lora(nc, g, lora_w, lora_a, lora_g):
    with ExitStack() as stack:
        s = Scope(nc, stack, "lo")
        raw = s.sb("raw", [P, 5, TOK])
        mixed = s.sb("mixed", [P, 2, TOK])
        rows = s.sb("rows", [80, P])
        mu_rows = s.sb("mu_rows", [5, RANK])
        mu = s.sb("mu", [P, 5])
        co = s.sb("co", [P, 5, 7])
        ps_a, ps_b = s.ps("ps_a", [P, 512]), s.ps("ps_b", [P, 512])
        loaded, rows_in, mu_in = s.sem("loaded"), s.sem("rows_in"), s.sem("mu_in")
        turned, stepped, mixed_wd, ones_set, mu_zero = (s.sem(n) for n in ("turned", "stepped", "mixed_wd", "ones_set", "mu_zero"))
        r0 = 3 * RW_W

        with nc.Block() as block:

            @block.sync
            def _(sp):
                for j in range(4):
                    sp.dma_start(raw[0:RANK, j, :], g.d_p[r0 + RANK * j:r0 + RANK * (j + 1), :]).then_inc(loaded, 16)
                sp.dma_start(raw[0:GATE_RANK, 4, 0:LAT], g.d_p[r0 + 4 * RANK:RW_COLS, 0:LAT]).then_inc(loaded, 16)
                for dst, src in ((g.tri, g.c_tri), (g.mid, g.c_mid), (g.mask, g.c_mask), (g.level, g.c_level),
                                 (g.pairs, g.c_pairs), (g.residue, g.c_residue)):
                    sp.dma_start(dst[:], src).then_inc(loaded, 16)

            @block.scalar
            def _(act):
                src = [g.rw_mu[0, 0:RW_W], g.rw_mu[0, RW_W:2 * RW_W], g.rw_mu[0, 2 * RW_W:3 * RW_W],
                       g.rw_a0[0, 0], g.rw_a0[0, 1], g.rw_k_k[0], g.rw_k_a[0], g.rw_r_k[0].rearrange("h c -> (h c)"),
                       g.rw_ln_w[0], g.rw_ln_b[0]]
                for k, v in enumerate(src):
                    act.dma_start(rows[8 * k:8 * k + 8, :], v.rearrange("(a p) -> a p", p=P)).then_inc(rows_in, 16)
                act.wait_ge(mu_zero, 1)
                act.dma_start(mu_rows[0:4, :], g.rw_mu[0, r0:r0 + 4 * RANK].rearrange("(a p) -> a p", p=RANK)).then_inc(mu_in, 16)
                act.dma_start(mu_rows[4:5, 0:GATE_RANK], g.rw_mu[0, r0 + 4 * RANK:RW_COLS].unsqueeze(0)).then_inc(mu_in, 16)
                for d in range(2):
                    act.wait_ge(mixed_wd, d + 1)
                    act.activation(lora_w[0:RANK, d, :], mixed[0:RANK, d, :], ACT.Tanh).then_inc(ones_set, 1)
                act.wait_ge(mixed_wd, 3)
                act.activation(lora_g[0:GATE_RANK, :], lora_g[0:GATE_RANK, :], ACT.Tanh, scale=0.5).then_inc(ones_set, 1)

            @block.tensor
            def _(pe):
                pe.wait_ge(rows_in, 160)
                pe.transpose(ps_a[:, 0:80], rows[:], g.ident[0:80, 0:80]).then_inc(turned, 1)
                pe.wait_ge(mu_in, 32)
                pe.transpose(ps_b[0:RANK, 0:5], mu_rows[:], g.ident[0:5, 0:5]).then_inc(turned, 1)

            @block.vector
            def _(dve):
                step = Steps(dve, stepped)
                dve.memset(mu_rows[:], 0.0).then_inc(mu_zero, 1)
                step(dve.memset(lora_w[RANK:RANK + 1, :, :], 1.0))
                dve.wait_ge(turned, 1)
                step(dve.tensor_copy(g.prm[:], ps_a[:, 0:80].rearrange("p (k a) -> p k a", a=8)))
                dve.wait_ge(turned, 2)
                step(dve.tensor_copy(mu[0:RANK, :], ps_b[0:RANK, 0:5]))
                dve.wait_ge(loaded, 16 * 11)
                for j in range(5):
                    m = RANK if j < 4 else GATE_RANK
                    step(dve.tensor_scalar(co[0:m, j, 0:1], mu[0:m, j:j + 1], -1.0, 1.0, ALU.mult, ALU.add))
                    step(dve.tensor_scalar(co[0:m, j, 1:7], g.residue[0:m, :], mu[0:m, j:j + 1], None, ALU.mult))
                    if j == 4:
                        shift_mix(dve, step, lora_g[0:m, :], raw[0:m, 4, 0:LAT], co[0:m, 4, :], False)
                    else:
                        out = mixed[0:m, j, :] if j < 2 else lora_a[0:m, j - 2, :]
                        shift_mix(dve, step, out, raw[0:m, j, :], co[0:m, j, :], True)
                    if j in (0, 1, 4):
                        dve.sem_inc(mixed_wd, 1)
                dve.wait_ge(ones_set, 3)
                step(dve.tensor_scalar(lora_g[0:GATE_RANK, :], lora_g[0:GATE_RANK, :], 0.5, 0.5, ALU.mult, ALU.add))


DECAY = 0.6065306597126334
RW_EPS = 64e-5
LEVELS = (2, 4, 8, 16, 32, 64)


def phase_rwkv(nc, g):
    with ExitStack() as stack:
        s = Scope(nc, stack, "rw")
        lora_w = s.sb("lora_w", [RANK + 1, 2, TOK])
        lora_a = s.sb("lora_a", [RANK, 2, TOK])
        lora_g = s.sb("lora_g", [GATE_RANK, LAT])
        g.prm, g.mid, g.pairs, g.residue = (s.sb(n, sh) for n, sh in (
            ("prm", [P, 10, 8]), ("mid", [P, 2]), ("pairs", [P, P]), ("residue", [P, 6])))
        phase_lora(nc, g, lora_w, lora_a, lora_g)

        raw = {"r": s.sb("raw_r", [P, LAT]), "k": s.sb("raw_k", [P, TOK]), "v": s.sb("raw_v", [P, TOK])}
        mix = {"r": s.sb("mix_r", [P, LAT]), "k": s.sb("mix_k", [P, TOK]), "v": s.sb("mix_v", [P, TOK])}
        w2, a2, g2 = s.sb("w2", [RANK + 1, 2, P]), s.sb("a2", [RANK, 2, P]), s.sb("g2", [GATE_RANK, P])
        cur = s.sb("cur", [P, 13])
        co = s.sb("co", [P, 3, 7])
        kk = s.sb("kk", [P, TOK])
        tmp = s.sb("tmp", [P, TOK])
        iclr = s.sb("iclr", [P, 2, TOK])
        kdir = s.sb("kdir", [P, 2, TOK])
        logw = s.sb("logw", [P, 2, 4, P])
        gate, bonus, gate_next, bonus_next = (s.sb(n, [P, LAT]) for n in ("gate", "bonus", "gate_next", "bonus_next"))
        root = s.sb("root", [P, TOK])
        ln = s.sb("ln", [P, 2])
        e_mid = s.sb("e_mid", [P, 4])
        b_s, k_s, v_s = (s.sb(n, [P, 4, P]) for n in ("b_s", "k_s", "v_s"))
        carry = [s.sb(f"carry{d}", [P, 3]) for d in range(2)]
        kk_s = [s.sb(f"kk_s{d}", [P, 4, P]) for d in range(2)]
        r_s = [s.sb(f"r_s{d}", [P, 2, P]) for d in range(2)]
        k_tok, b_tok, v_tok = ([s.sb(f"{n}{d}", [P, 4, P]) for d in range(2)] for n in ("k_tok", "b_tok", "v_tok"))
        a_t, n_t, m_t = ([s.sb(f"{n}{h}", [P, 4, P]) for h in range(2)] for n in ("a_t", "n_t", "m_t"))
        inv = [s.sb(f"inv{h}", [P, 4, P]) for h in range(2)]
        inv_t = [s.sb(f"inv_t{h}", [P, 4, P]) for h in range(2)]
        e_in, e_neg, e_ex = a_t[0], inv[0], inv[1]
        inv2 = [s.sb(f"inv2_{h}", [P, 4, P]) for h in range(2)]
        inv2_t = [s.sb(f"inv2_t{h}", [P, 4, P]) for h in range(2)]
        grown = [[s.sb(f"grown{h}_{n}", [P, 4, P]) for n in LEVELS] for h in range(2)]
        rhs, u, state = (s.sb(n, [P, P]) for n in ("rhs", "u", "state"))
        y = s.sb("y", [P, LAT])
        eps = s.sb("eps", [P, 2])
        held = s.sb("held", [1, 1])
        bank = [s.ps(f"bank{b}", [P, 512]) for b in range(8)]
        b4 = [b[:].rearrange("p (c t) -> p c t", c=4) for b in bank]

        pair_loaded = s.sem("pair_loaded")
        (v_step, a_step, shifted, k_squared, k_summed, k_rooted, lora_summed, lora_bent, decay_logged, gate_copied,
         decay_summed, exps_done, scaled, bonus_in, bonus_summed, turned, turned_copied, products, at_copied, products_masked,
         inv2_ready, x_summed, x_masked, t_summed, t_copied, r_summed, r_copied, u_summed, u_copied, s_summed,
         s_ready, y_summed, y_added, stats_in, stats_summed, var_rooted, round_done, x_filled,
         p_step, cur_ready, bonus_read, d_step) = (
            Signal(s, n, per) for n, per in (
                ("v_step", 13), ("a_step", 6), ("shifted", 1), ("k_squared", 1), ("k_summed", 1), ("k_rooted", 1),
                ("lora_summed", 5), ("lora_bent", 4), ("decay_logged", 2), ("gate_copied", 1), ("decay_summed", 2),
                ("exps_done", 2), ("scaled", 2), ("bonus_in", 1), ("bonus_summed", 1), ("turned", 2),
                ("turned_copied", 6), ("products", 16), ("at_copied", 4), ("products_masked", 8), ("inv2_ready", 8),
                ("x_summed", 24), ("x_masked", 24), ("t_summed", 44), ("t_copied", 44), ("r_summed", 8), ("r_copied", 8),
                ("u_summed", 8), ("u_copied", 8), ("s_summed", 6), ("s_ready", 6), ("y_summed", 4), ("y_added", 4),
                ("stats_in", 2), ("stats_summed", 2), ("var_rooted", 1), ("round_done", 3), ("x_filled", 1), ("p_step", 38), ("cur_ready", 1),
                ("bonus_read", 1), ("d_step", 22)))

        def end_round(eng, i):
            round_done.wait(eng, i, 3)

        def seq(ap, d, n, count=1):
            out = []
            for m in range(n, n + count):
                c = (2, 3, 0, 1)[m] if d == 0 else (3, 2, 1, 0)[m]
                out.append(ap[:, c * P:(c + 1) * P] if d == 0 else ap[:, c * P:(c + 1) * P][:, ::-1])
            return out

        with nc.Block() as block:

            @block.sync
            def _(sp):
                def load(i):
                    rows = bass.ds(i * P, P)
                    sp.dma_start(raw["r"][:], g.d_p[rows, 0:LAT]).then_inc(pair_loaded, 16)
                    sp.dma_start(raw["k"][:], g.d_p[bass.ds(i * P + RW_W, P), :]).then_inc(pair_loaded, 16)
                    sp.dma_start(raw["v"][:], g.d_p[bass.ds(i * P + 2 * RW_W, P), :]).then_inc(pair_loaded, 16)
                    sp.dma_start(w2[0:RANK, :, :], g.rw_w2[0].rearrange("d r c -> r d c")[:, :, rows]).then_inc(pair_loaded, 16)
                    sp.dma_start(w2[RANK:RANK + 1, :, :], g.rw_w0[:, :, rows]).then_inc(pair_loaded, 16)
                    sp.dma_start(a2[:], g.rw_a2[0].rearrange("d r c -> r d c")[:, :, rows]).then_inc(pair_loaded, 16)
                    sp.dma_start(g2[:], g.rw_g2[0][:, rows]).then_inc(pair_loaded, 16)

                load(0)
                with sp.Fori(0, 7) as i:
                    shifted.wait(sp, i)
                    lora_summed.wait(sp, i, 5)
                    load(i + 1)

            @block.tensor
            def _(pe):
                def prepare(j, part):
                    if part == 0:
                        pe.wait_ge(pair_loaded, 112 * j + 112)
                        for d in range(2):
                            pe.matmul(bank[6 + d][:], a2[:, d, :], lora_a[:, d, :], start=True, stop=True).then_inc(lora_summed.sem, 1)
                    elif part == 1:
                        for d in range(2):
                            lora_bent.wait(pe, j, d + 1)
                            for c in range(4):
                                ch = (2, 3, 0, 1)[c] if d == 0 else (3, 2, 1, 0)[c]
                                ins = pe.matmul(b4[6 + d][:, c, :], lora_w[:, d, ch * P:(ch + 1) * P], w2[:, d, :], start=True, stop=True)
                            ins.then_inc(lora_summed.sem, 1)
                    elif part == 2:
                        lora_bent.wait(pe, j, 3)
                        pe.matmul(bank[6][:, 0:LAT], g2[:], lora_g[:], start=True, stop=True).then_inc(lora_summed.sem, 1)
                        lora_bent.wait(pe, j, 4)
                        k_squared.wait(pe, j)
                        pe.matmul(bank[7][:], g.pairs[:], tmp[:], start=True, stop=True).then_inc(k_summed.sem, 1)
                    elif part == 4:
                        bonus_in.wait(pe, j)
                        gate_copied.wait(pe, j)
                        pe.matmul(bank[6][:, 0:LAT], g.pairs[:], tmp[:, 0:LAT], start=True, stop=True).then_inc(bonus_summed.sem, 1)

                def sum_logs(i, d, chunks):
                    if chunks[0] == 0:
                        decay_logged.wait(pe, i, d + 1)
                    for c in chunks:
                        pe.matmul(b4[3][:, c, :], logw[:, d, c, :], g.tri[:, d, 0, :], start=True, stop=True)
                        pe.matmul(b4[4][:, c, :], logw[:, d, c, :], g.tri[:, d, 1, :], start=True, stop=True)
                        ins = pe.matmul(bank[5][:, c:c + 1], logw[:, d, c, :], g.mid[:, d:d + 1], start=True, stop=True)
                    if c == 3:
                        ins.then_inc(decay_summed.sem, 1)

                def turn(i, d, k):
                    if k == 0:
                        scaled.wait(pe, i, d + 1)
                    for c in range(4):
                        ins = pe.transpose(b4[3 + k][:, c, :], (k_s, b_s, v_s)[k][:, c, :], g.ident[:])
                    if k == 2:
                        ins.then_inc(turned.sem, 1)

                def pair(i, following):
                    for d in range(2):
                        ahead = (i, 1) if d == 0 else (following, 0) if following is not None else None
                        if d == 1:
                            y_added.wait(pe, i, 2)
                        for h in range(2):
                            ch = slice(64 * h, 64 * h + 64)
                            ba = (0, 1, 2, 6) if h == 0 else (3, 4, 5, 7)
                            if h == 0:
                                exps_done.wait(pe, i, d + 1)
                            else:
                                turned_copied.wait(pe, i, 3 * d + 3)
                            for k, (l, r) in enumerate(((b_s, kk_s[d]), (kk_s[d], b_s), (k_s, kk_s[d]))):
                                for c in range(4):
                                    ins = pe.matmul(b4[ba[k]][:, c, :], l[ch, c, :], r[ch, c, :], start=True, stop=True)
                                ins.then_inc(products.sem, 1)
                            for k, l in enumerate((k_s, b_s)):
                                for c in range(2):
                                    ins = pe.matmul(b4[ba[3]][:, 2 * k + c, :], l[ch, 2 + c, :], r_s[d][ch, c, :], start=True, stop=True)
                            ins.then_inc(products.sem, 1)
                        for lv, _ in enumerate(LEVELS):
                            for h in range(2):
                                ba = (0, 1, 2) if h == 0 else (3, 4, 5)
                                if lv == 0:
                                    at_copied.wait(pe, i, 2 * d + h + 1)
                                    inv2_ready.wait(pe, i, 4 * d + 2 * h + 2)
                                    products_masked.wait(pe, i, 4 * d + 2 * h + 1)
                                else:
                                    t_copied.wait(pe, i, 22 * d + 4 * lv + 2 * h - 2)
                                    x_masked.wait(pe, i, 12 * d + 2 * lv + h - 1)
                                src = inv2[h] if lv == 0 else inv[h]
                                for c in range(4):
                                    ins = pe.matmul(b4[ba[0]][:, c, :], a_t[h][:, c, :], src[:, c, :], start=True, stop=True)
                                ins.then_inc(x_summed.sem, 1)
                            for h in range(2):
                                ba = (0, 1, 2) if h == 0 else (3, 4, 5)
                                src_t = inv2_t[h] if lv == 0 else inv_t[h]
                                x_masked.wait(pe, i, 12 * d + 2 * lv + h + 1)
                                if lv < 5:
                                    for c in range(4):
                                        ins = pe.matmul(b4[ba[1]][:, c, :], src_t[:, c, :], grown[h][lv][:, c, :], start=True, stop=True)
                                    ins.then_inc(t_summed.sem, 1)
                                for c in range(4):
                                    ins = pe.matmul(b4[ba[2]][:, c, :], grown[h][lv][:, c, :], src_t[:, c, :], start=True, stop=True)
                                ins.then_inc(t_summed.sem, 1)
                            if d == 1 and following is not None:
                                if lv == 0:
                                    products_masked.wait(pe, i, 8)
                                prepare(following, lv)
                        for n in range(4):
                            last = n == 3
                            if n == 0:
                                t_copied.wait(pe, i, 22 * d + 22)
                                products_masked.wait(pe, i, 4 * d + 4)
                            else:
                                s_ready.wait(pe, i, 3 * d + n)
                                pe.matmul(bank[0][:, 0:P], kk_s[d][:, n, :], state[:], start=True, stop=False, skip_group_check=True)
                            for h in range(2):
                                ins = pe.matmul(bank[0][:, 64 * h:64 * h + 64], n_t[h][:, n, :], v_tok[d][:, n, 64 * h:64 * h + 64],
                                                start=(n == 0), stop=(h == 1), skip_group_check=True)
                            ins.then_inc(r_summed.sem, 1)
                            if ahead and n == 0:
                                sum_logs(*ahead, (0, 1))
                            elif ahead and n == 3:
                                turn(*ahead, 0)
                            r_copied.wait(pe, i, 4 * d + n + 1)
                            for h in range(2):
                                ins = pe.matmul(bank[1][:, 64 * h:64 * h + 64], inv_t[h][:, n, :], rhs[:, 64 * h:64 * h + 64],
                                                start=True, stop=True, skip_group_check=True)
                            ins.then_inc(u_summed.sem, 1)
                            if ahead and n == 0:
                                sum_logs(*ahead, (2, 3))
                            elif ahead and n == 3:
                                turn(*ahead, 1)
                            u_copied.wait(pe, i, 4 * d + n + 1)
                            if not last:
                                pe.matmul(bank[2][:, 0:P], k_tok[d][:, n, :], v_tok[d][:, n, :], start=True, stop=False)
                                pe.matmul(bank[2][:, 0:P], b_tok[d][:, n, :], u[:], start=False, stop=True).then_inc(s_summed.sem, 1)
                            if n >= 2:
                                yb = bank[4 + n]
                                if d == 1 and n == 2 and following is not None:
                                    k_rooted.wait(pe, following)
                                    bonus_read.wait(pe, following)
                                pe.matmul(yb[:, 0:P], state[:], r_s[d][:, n - 2, :], start=True, stop=False, skip_group_check=True)
                                for h in range(2):
                                    ch = slice(64 * h, 64 * h + 64)
                                    pe.matmul(yb[ch, 0:P], v_tok[d][:, n, ch], m_t[h][:, n - 2, :], start=False, stop=False, skip_group_check=True)
                                    ins = pe.matmul(yb[ch, 0:P], u[:, ch], m_t[h][:, n, :], start=False, stop=(h == 1), skip_group_check=True)
                                ins.then_inc(y_summed.sem, 1)
                        if ahead:
                            turn(*ahead, 2)
                    stats_in.wait(pe, i, 1)
                    pe.matmul(bank[0][:, 0:LAT], g.pairs[:], y[:], start=True, stop=True).then_inc(stats_summed.sem, 1)
                    stats_in.wait(pe, i, 2)
                    pe.matmul(bank[1][:, 0:LAT], g.pairs[:], tmp[:, 0:LAT], start=True, stop=True).then_inc(stats_summed.sem, 1)
                    end_round(pe, i)

                for part in (0, 1, 2, 4):
                    prepare(0, part)
                bonus_read.wait(pe, 0)
                sum_logs(0, 0, (0, 1, 2, 3))
                for n in range(3):
                    turn(0, 0, n)
                with pe.Fori(0, 7) as i:
                    pair(i, i + 1)
                pair(7, None)

            @block.scalar
            def _(act):

                def prepare(j, part):
                    if part == 0:
                        cur_ready.wait(act, j)
                        for d in range(2):
                            lora_summed.wait(act, j, d + 1)
                            act.activation(iclr[:, d, :], bank[6 + d][:], ACT.Tanh, scale=0.5, bias=cur[:, 10 + d:11 + d])\
                               .then_inc(lora_bent.sem, 1)
                    elif part == 1:
                        for d in range(2):
                            lora_summed.wait(act, j, d + 3)
                            act.activation(logw[:, d], b4[6 + d][:], ACT.Tanh, scale=0.5).then_inc(lora_bent.sem, 1)
                    elif part == 2:
                        k_summed.wait(act, j)
                        act.activation(root[:], bank[7][:], ACT.Sqrt, bias=eps[:, 0:1]).then_inc(k_rooted.sem, 1)

                def raise_logs(i, d):
                    decay_summed.wait(act, i, d + 1)
                    act.activation(e_mid[:], bank[5][:, 0:4], ACT.Exp).then_inc(a_step.sem, 1)
                    act.activation(e_in[:], b4[3][:], ACT.Exp).then_inc(a_step.sem, 1)
                    act.activation(e_neg[:], b4[3][:], ACT.Exp, scale=-1.0).then_inc(a_step.sem, 1)
                    a_step.wait(act, i, 3 * d + 3)
                    act.activation(e_ex[:], b4[4][:], ACT.Exp).then_inc(exps_done.sem, 1)

                def copy_turned(i, d):
                    turned.wait(act, i, d + 1)
                    for b, dst in ((3, k_tok[d]), (4, b_tok[d]), (5, v_tok[d])):
                        act.activation(dst[:], b4[b][:], ACT.Copy).then_inc(turned_copied.sem, 1)

                def pair(i, following):
                    for d in range(2):
                        ahead = (i, 1) if d == 0 else (following, 0) if following is not None else None
                        for h in range(2):
                            products.wait(act, i, 8 * d + 4 * h + 1)
                            inv2_ready.wait(act, i, 4 * d + 2 * h + 1)
                            act.activation(a_t[h][:], b4[3 * h][:], ACT.Copy).then_inc(at_copied.sem, 1)
                        for lv in range(6):
                            for h in range(2):
                                if lv < 5:
                                    t_summed.wait(act, i, 22 * d + 4 * lv + 2 * h + 2)
                                    act.activation(inv[h][:], b4[3 * h + 1][:], ACT.Copy).then_inc(t_copied.sem, 1)
                                else:
                                    t_summed.wait(act, i, 22 * d + 20 + h + 1)
                                act.activation(inv_t[h][:], b4[3 * h + 2][:], ACT.Copy).then_inc(t_copied.sem, 1)
                            if d == 1 and following is not None:
                                prepare(following, lv)
                        for n in range(4):
                            r_summed.wait(act, i, 4 * d + n + 1)
                            act.activation(rhs[:], bank[0][:, 0:P], ACT.Copy).then_inc(r_copied.sem, 1)
                            u_summed.wait(act, i, 4 * d + n + 1)
                            act.activation(u[:], bank[1][:, 0:P], ACT.Copy).then_inc(u_copied.sem, 1)
                            if ahead and n == 0:
                                raise_logs(*ahead)
                        if ahead:
                            copy_turned(*ahead)
                    stats_summed.wait(act, i, 2)
                    act.activation(bonus_root(tmp), bank[1][:, 0:LAT], ACT.Sqrt, bias=eps[:, 1:2], scale=1.0 / RW_DIM).then_inc(var_rooted.sem, 1)
                    var_rooted.wait(act, i)
                    act.sem_inc(round_done.sem, 1)
                    end_round(act, i)

                for part in range(3):
                    prepare(0, part)
                raise_logs(0, 0)
                copy_turned(0, 0)
                with act.Fori(0, 7) as i:
                    pair(i, i + 1)
                pair(7, None)

            @block.gpsimd
            def _(pool):
                for t in inv2 + inv2_t + grown[0] + grown[1]:
                    for c in range(4):
                        ins = pool.tensor_copy(t[:, c, :], g.ident[:])
                ins.then_inc(x_filled.sem, 1)

            @block.vector
            def _(dve):
                boot = Steps(dve, s.sem("boot"))
                boot(dve.memset(eps[:, 0:1], EPS))
                boot(dve.memset(eps[:, 1:2], RW_EPS))

                def prepare(step, j, part):
                    if part == 0:
                        step(dve.tensor_copy(cur[:, 0:10], g.prm[:, :, bass.ds(j, 1)].rearrange("p k a -> p (k a)")))
                        step(dve.tensor_scalar(cur[:, 10:12], cur[:, 3:5], 0.5, None, ALU.mult))
                        step(dve.tensor_scalar(cur[:, 12:13], cur[:, 6:7], -1.0, 1.0, ALU.mult, ALU.add))
                        dve.sem_inc(cur_ready.sem, 1)
                        for n in range(3):
                            step(dve.tensor_scalar(co[:, n, 0:1], cur[:, n:n + 1], -1.0, 1.0, ALU.mult, ALU.add))
                            step(dve.tensor_scalar(co[:, n, 1:7], g.residue[:], cur[:, n:n + 1], None, ALU.mult))
                    elif part == 1:
                        dve.wait_ge(pair_loaded, 112 * j + 112)
                        shift_mix(dve, step, mix["k"][:], raw["k"][:], co[:, 1, :], True)
                    elif part == 2:
                        shift_mix(dve, step, mix["v"][:], raw["v"][:], co[:, 2, :], True)
                    elif part == 3:
                        shift_mix(dve, step, mix["r"][:], raw["r"][:], co[:, 0, :], False)
                        step.tell(dve.tensor_scalar(kk[:], mix["k"][:], cur[:, 5:6], None, ALU.mult), shifted)
                        step.tell(dve.tensor_tensor(tmp[:], kk[:], kk[:], ALU.mult), k_squared)
                    elif part == 4:
                        for d in range(2):
                            lora_bent.wait(dve, j, d + 1)
                            step(dve.tensor_scalar(iclr[:, d, :], iclr[:, d, :], 0.5, 0.5, ALU.mult, ALU.add))
                            step(dve.tensor_scalar(kdir[:, d, :], iclr[:, d, :], cur[:, 6:7], cur[:, 12:13], ALU.mult, ALU.add))
                            step(dve.tensor_tensor(kdir[:, d, :], kdir[:, d, :], mix["k"][:], ALU.mult))
                    elif part == 5:
                        k_summed.wait(dve, j)
                        step(dve.tensor_tensor(tmp[:, 0:LAT], kdir[:, 0, 0:LAT], kdir[:, 1, 0:LAT], ALU.add))
                        step(dve.scalar_tensor_tensor(tmp[:, 0:LAT], tmp[:, 0:LAT], 0.5, mix["r"][:], ALU.mult, ALU.mult))
                        step.tell(dve.tensor_scalar(tmp[:, 0:LAT], tmp[:, 0:LAT], cur[:, 7:8], None, ALU.mult), bonus_in)
                        lora_summed.wait(dve, j, 5)
                        step.tell(dve.tensor_copy(gate_next[:], bank[6][:, 0:LAT]), gate_copied)
                        for d in range(2):
                            lora_bent.wait(dve, j, d + 3)
                            step.tell(dve.tensor_scalar(logw[:, d], logw[:, d], -0.5 * DECAY, -0.5 * DECAY, ALU.mult, ALU.add),
                                      decay_logged, d + 1)
                    elif part == 6:
                        k_rooted.wait(dve, j)
                        step(dve.reciprocal(root[:], root[:]))
                        step(dve.tensor_tensor(kk[:], kk[:], root[:], ALU.mult))
                    elif part == 7:
                        bonus_summed.wait(dve, j)
                        step.tell(dve.tensor_tensor(bonus_next[:], bank[6][:, 0:LAT], mix["v"][:, 0:LAT], ALU.mult), bonus_read)
                        step.end()

                def scale(step, i, d, chunks):
                    if chunks[0] == 0:
                        exps_done.wait(dve, i, d + 1)
                        step(dve.tensor_tensor(carry[d][:], e_in[:, 0:3, P - 1], e_mid[:, 1:4], ALU.mult))
                    for n in chunks:
                        kkn, = seq(kk[:], d, n)
                        icn, = seq(iclr[:, d, :], d, n)
                        kdn, = seq(kdir[:, d, :], d, n)
                        vn, = seq(mix["v"][:], d, n)
                        dve.tensor_tensor(kk_s[d][:, n, :], kkn, e_ex[:, n, :], ALU.mult).then_inc(d_step.sem, 1)
                        dve.scalar_tensor_tensor(b_s[:, n, :], kkn, -1.0, icn, ALU.mult, ALU.mult).then_inc(d_step.sem, 1)
                        dve.tensor_tensor(k_s[:, n, :], kdn, e_neg[:, n, :], ALU.mult).then_inc(d_step.sem, 1)
                        dve.tensor_copy(v_s[:, n, :], vn).then_inc(d_step.sem, 1)
                        step.n += 4
                    d_step.wait(dve, step.i, step.n)
                    for n in chunks:
                        step.free(dve.tensor_tensor(b_s[:, n, :], b_s[:, n, :], e_neg[:, n, :], ALU.mult))
                    if chunks[-1] == 3:
                        for n in (2, 3):
                            rn, = seq(mix["r"][:], d, n)
                            ins = dve.tensor_tensor(r_s[d][:, n - 2, :], rn, e_in[:, n, :], ALU.mult)
                            if n == 2:
                                step.free(ins)
                            else:
                                ins.then_inc(scaled.sem, 1)
                                scaled.wait(dve, i, d + 1)
                        assert step.n == d_step.per

                def pair(i, following):
                    step = Chain(dve, v_step, i)
                    shared = Chain(dve, p_step, following)
                    step(dve.tensor_copy(ln[:], cur[:, 8:10]))
                    step(dve.tensor_copy(gate[:], gate_next[:]))
                    step(dve.tensor_copy(bonus[:], bonus_next[:]))
                    for d in range(2):
                        ahead = (i, 1) if d == 0 else (following, 0) if following is not None else None
                        for h in range(2):
                            lo = 3 * h
                            products.wait(dve, i, 8 * d + 4 * h + 1)
                            x_filled.wait(dve, 0)
                            dve.memset(held[:], 0.0)
                            step.tell(dve.copy_predicated(inv2_t[h][:], g.level[:, 7, :].unsqueeze(1).broadcast_to([P, 4, P]), b4[lo][:]),
                                      inv2_ready, 4 * d + 2 * h + 1)
                            products.wait(dve, i, 8 * d + 4 * h + 2)
                            dve.memset(held[:], 0.0)
                            step.tell(dve.copy_predicated(inv2[h][:], g.level[:, 0, :].unsqueeze(1).broadcast_to([P, 4, P]), b4[lo + 1][:]),
                                      inv2_ready, 4 * d + 2 * h + 2)
                            products.wait(dve, i, 8 * d + 4 * h + 3)
                            step.tell(dve.tensor_tensor(n_t[h][:], b4[lo + 2][:], g.mask[:, 0, :].unsqueeze(1).broadcast_to([P, 4, P]), ALU.mult),
                                      products_masked, 4 * d + 2 * h + 1)
                            products.wait(dve, i, 8 * d + 4 * h + 4)
                            step.tell(dve.tensor_tensor(m_t[h][:], b4[6 + h][:], g.mask[:, 1, :].unsqueeze(1).broadcast_to([P, 4, P]), ALU.mult),
                                      products_masked, 4 * d + 2 * h + 2)
                        for lv in range(6):
                            for h in range(2):
                                x_summed.wait(dve, i, 12 * d + 2 * lv + h + 1)
                                dve.memset(held[:], 0.0)
                                step.tell(dve.copy_predicated(grown[h][lv][:], g.level[:, lv + 1, :].unsqueeze(1).broadcast_to([P, 4, P]),
                                                              b4[3 * h][:]), x_masked, 12 * d + 2 * lv + h + 1)
                            if following is not None and (d == 1 or lv < 2):
                                prepare(shared, following, lv if d == 0 else lv + 2)
                        if ahead:
                            own = Chain(dve, d_step, 2 * ahead[0] + ahead[1])
                        for n in range(4):
                            if ahead and n in (1, 2):
                                scale(own, *ahead, (2 * n - 2, 2 * n - 1))
                            if n < 3:
                                s_summed.wait(dve, i, 3 * d + n + 1)
                                if n == 0:
                                    step.tell(dve.scalar_tensor_tensor(state[:], bank[2][:, 0:P], carry[d][:, 0:1], g.pairs[:], ALU.mult, ALU.mult),
                                              s_ready, 3 * d + 1)
                                else:
                                    if n == 2:
                                        y_summed.wait(dve, i, 2 * d + 1)
                                    step(dve.tensor_tensor(state[:], state[:], bank[2][:, 0:P], ALU.add))
                                    step.tell(dve.scalar_tensor_tensor(state[:], state[:], carry[d][:, n:n + 1], g.pairs[:], ALU.mult, ALU.mult),
                                              s_ready, 3 * d + n + 1)
                            if n >= 2:
                                y_summed.wait(dve, i, 2 * d + n - 1)
                                dst, = seq(y[:], d, n)
                                if d == 0:
                                    ins = dve.tensor_copy(dst, bank[4 + n][:, 0:P])
                                else:
                                    ins = dve.tensor_tensor(dst, dst, bank[4 + n][:, 0:P], ALU.add)
                                step.tell(ins, y_added, 2 * d + n - 1)
                    dve.sem_inc(stats_in.sem, 1)
                    stats_summed.wait(dve, i, 1)
                    step(dve.scalar_tensor_tensor(y[:], bank[0][:, 0:LAT], -1.0 / RW_DIM, y[:], ALU.mult, ALU.add))
                    step.tell(dve.tensor_tensor(tmp[:, 0:LAT], y[:], y[:], ALU.mult), stats_in, 2)
                    var_rooted.wait(dve, i)
                    step(dve.reciprocal(bonus_root(tmp), bonus_root(tmp)))
                    step(dve.tensor_tensor(y[:], y[:], bonus_root(tmp), ALU.mult))
                    step(dve.tensor_scalar(y[:], y[:], ln[:, 0:1], ln[:, 1:2], ALU.mult, ALU.add))
                    step(dve.tensor_tensor(y[:], y[:], bonus[:], ALU.add))
                    step(dve.tensor_tensor(g.o_a[:, bass.ds(i, 1), :].rearrange("p a t -> p (a t)"), y[:], gate[:], ALU.mult))
                    step.end()
                    dve.sem_inc(round_done.sem, 2)
                    end_round(dve, i)

                first = Chain(dve, p_step, 0)
                for part in range(8):
                    prepare(first, 0, part)
                scale(Chain(dve, d_step, 0), 0, 0, (0, 1, 2, 3))
                with dve.Fori(0, 7) as i:
                    pair(i, i + 1)
                pair(7, None)


def bonus_root(tmp):
    return tmp[:, LAT:TOK]


def phase_gdn_gates(nc, g, g_seq, gc_seq, be_seq, taps, norm_w):
    with ExitStack() as stack:
        s = Scope(nc, stack, "gg")
        a, b = s.sb("a", [16, TOK]), s.sb("b", [16, TOK])
        t = s.sb("t", [16, TOK])
        par = s.sb("par", [16, 3])
        rows = s.sb("rows", [120, P])
        nrow = s.sb("nrow", [1, P])
        b_seq = s.sb("b_seq", [P, 2, 4, 8])
        ps_g, ps_b, ps_c, ps_t = (s.ps(n, [P, 512]) for n in ("ps_g", "ps_b", "ps_c", "ps_t"))
        loaded, bent, stepped, ready, turned, ordered, summed = (s.sem(n) for n in (
            "loaded", "bent", "stepped", "ready", "turned", "ordered", "summed"))

        with nc.Block() as block:

            @block.sync
            def _(sp):
                for dst, src in ((a[:], g.d_p[AB0:AB0 + 16, :]), (b[:], g.d_p[AB0 + 16:AB0 + 32, :]),
                                 (par[:, 0:1], g.gdn_a_log[0].rearrange("d h -> (d h)").unsqueeze(1)),
                                 (par[:, 1:2], g.gdn_dt_bias[0].rearrange("d h -> (d h)").unsqueeze(1)),
                                 (rows[:], g.gdn_conv_w[0].rearrange("t (a p) -> (t a) p", p=P)),
                                 (nrow[:], g.gdn_norm_w), (g.back[:], g.c_back)):
                    sp.dma_start(dst, src).then_inc(loaded, 16)

            @block.scalar
            def _(act):
                act.wait_ge(loaded, 112)
                act.activation(par[:, 2:3], par[:, 0:1], ACT.Exp).then_inc(bent, 1)
                act.activation(b[:], b[:], ACT.Tanh, scale=0.5).then_inc(bent, 1)
                act.wait_ge(ready, 1)
                act.activation(t[:], t[:], ACT.Exp).then_inc(bent, 1)
                act.wait_ge(ready, 2)
                act.activation(t[:], t[:], ACT.Ln).then_inc(bent, 1)

            @block.vector
            def _(dve):
                step = Steps(dve, stepped)
                dve.wait_ge(loaded, 112)
                step(dve.tensor_scalar(a[:], a[:], par[:, 1:2], None, ALU.add))
                step(dve.tensor_scalar(t[:], a[:], -1.0, None, ALU.mult))
                dve.tensor_tensor(t[:], t[:], a[:], ALU.min).then_inc(ready, 1)
                dve.wait_ge(bent, 3)
                dve.tensor_scalar(t[:], t[:], 1.0, None, ALU.add).then_inc(ready, 1)
                step(dve.tensor_scalar(b[:], b[:], 0.5, 0.5, ALU.mult, ALU.add))
                dve.wait_ge(bent, 4)
                step(dve.scalar_tensor_tensor(a[:], a[:], 0.0, t[:], ALU.max, ALU.add))
                step(dve.tensor_scalar(par[:, 2:3], par[:, 2:3], -1.0, None, ALU.mult))
                dve.tensor_scalar(a[:], a[:], par[:, 2:3], None, ALU.mult).then_inc(ready, 1)
                dve.wait_ge(turned, 1)
                for src, dst in ((ps_g, g_seq), (ps_b, b_seq)):
                    v = src[:, 0:64].rearrange("p (c d h) -> p c d h", c=4, d=2)
                    for d in range(2):
                        for n in range(4):
                            c = (2, 3, 0, 1)[n] if d == 0 else (3, 2, 1, 0)[n]
                            step(dve.tensor_copy(dst[:, d, n, :], v[:, c, d, :]))
                dve.sem_inc(ordered, 1)
                step(dve.tensor_copy(taps[:], ps_t[:, 0:120].rearrange("p (t j a) -> p t j a", t=5, j=3)))
                step(dve.tensor_copy(norm_w[:], ps_t[:, 120:121]))
                dve.wait_ge(summed, 1)
                step(dve.tensor_copy(gc_seq[:], ps_c[:, 0:64].rearrange("p (d n h) -> p d n h", d=2, n=4)))
                step(dve.tensor_copy(be_seq[:], ps_c[:, 64:128].rearrange("p (d n h) -> p d n h", d=2, n=4)))

            @block.tensor
            def _(pe):
                pe.wait_ge(loaded, 112)
                pe.transpose(ps_t[:, 0:120], rows[:], g.ident[0:120, 0:120])
                pe.transpose(ps_t[:, 120:121], nrow[:], g.ident[0:1, 0:1])
                pe.wait_ge(ready, 3)
                for src, dst in ((a, ps_g), (b, ps_b)):
                    for c in range(4):
                        ins = pe.transpose(dst[:, 16 * c:16 * c + 16], src[:, c * P:(c + 1) * P], g.ident[0:16, 0:16])
                ins.then_inc(turned, 1)
                pe.wait_ge(ordered, 1)
                for d in range(2):
                    order = g.mask[:, 1, :] if d == 0 else g.back[:, 0, :]
                    pe.matmul(ps_c[:, 32 * d:32 * d + 32], order, g_seq[:, d].rearrange("p n h -> p (n h)"), start=True, stop=True)
                for d in range(2):
                    order = g.ident[:] if d == 0 else g.back[:, 1, :]
                    ins = pe.matmul(ps_c[:, 64 + 32 * d:96 + 32 * d], order, b_seq[:, d].rearrange("p n h -> p (n h)"), start=True, stop=True)
                ins.then_inc(summed, 1)


def phase_gdn(nc, g):
    with ExitStack() as stack:
        s = Scope(nc, stack, "gd")
        g_seq, gc_seq, be_seq = (s.sb(n, [P, 2, 4, 8]) for n in ("g_seq", "gc_seq", "be_seq"))
        taps = s.sb("taps", [P, 5, 3, 8])
        norm_w = s.sb("norm_w", [P, 1])
        g.back = s.sb("back", [P, 3, P])
        phase_gdn_gates(nc, g, g_seq, gc_seq, be_seq, taps, norm_w)

        raw = [s.sb("raw_q", [P, LAT]), s.sb("raw_k", [P, TOK]), s.sb("raw_v", [P, TOK])]
        conv = [s.sb("q", [P, LAT]), s.sb("k", [P, TOK]), s.sb("v", [P, TOK])]
        half = s.sb("half", [P, 3, TOK])
        z = s.sb("z", [P, LAT])
        cur_g, cur_gc, cur_be, g_end, e_end, tail, nbe, nbeta = (s.sb(n, [P, 2, 4]) for n in (
            "cur_g", "cur_gc", "cur_be", "g_end", "e_end", "tail", "nbe", "nbeta"))
        cur_w = s.sb("cur_w", [P, 5, 3])
        g_wide = s.sb("g_wide", [P, 2, 4, P])
        k_s = [s.sb(f"k_s{d}", [P, 4, P]) for d in range(2)]
        v_s = [s.sb(f"v_s{d}", [P, 4, P]) for d in range(2)]
        q_s = [s.sb(f"q_s{d}", [P, 2, P]) for d in range(2)]
        qd = [s.sb(f"qd{d}", [P, 2, P]) for d in range(2)]
        k_tok = [s.sb(f"k_tok{d}", [P, 4, P]) for d in range(2)]
        v_tok = [s.sb(f"v_tok{d}", [P, 4, P]) for d in range(2)]
        low = [s.sb(f"low{d}", [P, 4, P]) for d in range(2)]
        m_t = [s.sb(f"m_t{d}", [P, 2, P]) for d in range(2)]
        a_t = [s.sb(f"a_t{d}", [P, 4, P]) for d in range(2)]
        inv = [s.sb(f"inv{d}", [P, 4, P]) for d in range(2)]
        inv_t = [s.sb(f"inv_t{d}", [P, 4, P]) for d in range(2)]
        inv2 = [s.sb(f"inv2_{d}", [P, 4, P]) for d in range(2)]
        inv2_t = [s.sb(f"inv2_t{d}", [P, 4, P]) for d in range(2)]
        grown = [[s.sb(f"grown{d}_{n}", [P, 4, P]) for n in LEVELS] for d in range(2)]
        rhs, u, state = ([s.sb(f"{n}{d}", [P, P]) for d in range(2)] for n in ("rhs", "u", "state"))
        o = s.sb("o", [P, LAT])
        eps = s.sb("eps", [P, 1])
        held = s.sb("held", [1, 1])
        bank = [s.ps(f"bank{b}", [P, 512]) for b in range(8)]
        b4 = [b[:].rearrange("p (c t) -> p c t", c=4) for b in bank]

        head_loaded = s.sem("head_loaded")
        (v_step, a_step, convolved, bent, squared, sq_summed, rooted, widened, g_summed, end_read, sides_ready, turned,
         tok_copied, grams, low_ready, low_turned, at_copied, inv2_ready, m_summed, m_ready, qd_ready, d_bent, dt_bent, d_in, dt_in,
         x_summed, x_masked, t_summed, t_copied, r_summed, r_ready, u_summed, u_copied, s_summed, s_ready,
         y_summed, y_added, o_squared, o_summed, o_rooted, round_done, x_filled, cols_bent,
         p_step, z_bent, d_step, v_sides) = (
            Signal(s, n, per) for n, per in (
                ("v_step", 18), ("a_step", 2), ("convolved", 3), ("bent", 3), ("squared", 2), ("sq_summed", 2),
                ("rooted", 2), ("widened", 1), ("g_summed", 2), ("end_read", 1), ("sides_ready", 2), ("turned", 4),
                ("tok_copied", 4), ("grams", 2), ("low_ready", 2), ("low_turned", 2), ("at_copied", 2), ("inv2_ready", 2),
                ("m_summed", 1), ("m_ready", 2), ("qd_ready", 2), ("d_bent", 2), ("dt_bent", 2), ("d_in", 2), ("dt_in", 2),
                ("x_summed", 12), ("x_masked", 12), ("t_summed", 22), ("t_copied", 22), ("r_summed", 6), ("r_ready", 8),
                ("u_summed", 8), ("u_copied", 8), ("s_summed", 6), ("s_ready", 6), ("y_summed", 4), ("y_added", 4),
                ("o_squared", 1), ("o_summed", 1), ("o_rooted", 1), ("round_done", 3), ("x_filled", 1), ("cols_bent", 3), ("p_step", 21), ("z_bent", 1), ("d_step", 24), ("v_sides", 2)))

        def seq(ap, d, n):
            c = (2, 3, 0, 1)[n] if d == 0 else (3, 2, 1, 0)[n]
            return ap[:, c * P:(c + 1) * P] if d == 0 else ap[:, c * P:(c + 1) * P][:, ::-1]

        def wide(ap):
            return ap.unsqueeze(1).broadcast_to([P, 4, P])

        with nc.Block() as block:

            @block.sync
            def _(sp):
                def load(i):
                    for j, cols in ((0, LAT), (1, TOK), (2, TOK)):
                        sp.dma_start(raw[j][:], g.d_p[bass.ds(i * P + (CONV0 + j * GDN_W), P), 0:cols]).then_inc(head_loaded, 16)
                load(0)
                with sp.Fori(0, 7) as i:
                    convolved.wait(sp, i, 3)
                    load(i + 1)

            @block.gpsimd
            def _(pool):
                for t in inv2 + inv2_t + grown[0] + grown[1]:
                    for c in range(4):
                        ins = pool.tensor_copy(t[:, c, :], g.ident[:])
                ins.then_inc(x_filled.sem, 1)

            @block.tensor
            def _(pe):
                def prepare(j, part):
                    if part == 2:
                        squared.wait(pe, j, 1)
                        pe.matmul(bank[7][:], g.ones[:], half[:, 1, :], start=True, stop=True).then_inc(sq_summed.sem, 1)
                    elif part == 4:
                        squared.wait(pe, j, 2)
                        pe.matmul(bank[6][:, 0:LAT], g.ones[:], half[:, 0, 0:LAT], start=True, stop=True).then_inc(sq_summed.sem, 1)

                def sum_decays(j):
                    widened.wait(pe, j)
                    for d in range(2):
                        order = g.mask[:, 1, :] if d == 0 else g.back[:, 0, :]
                        for n in range(4):
                            ins = pe.matmul(b4[2 + d][:, n, :], g_wide[:, d, n, :], order, start=True, stop=True)
                        ins.then_inc(g_summed.sem, 1)

                def turn(d):
                    for k, src in enumerate((k_s[d], v_s[d])):
                        for c in range(4):
                            ins = pe.transpose(b4[k][:, c, :], src[:, c, :], g.ident[:])
                        ins.then_inc(turned.sem, 1)

                def open_head(j):
                    for d in range(2):
                        sides_ready.wait(pe, j, d + 1)
                        if d == 0:
                            v_sides.wait(pe, j, 1)
                            turn(0)
                        for c in range(4):
                            ins = pe.matmul(b4[4 + d][:, c, :], k_s[d][:, c, :], k_s[d][:, c, :], start=True, stop=True)
                        ins.then_inc(grams.sem, 1)
                        for c in range(2):
                            ins = pe.matmul(b4[6][:, 2 * d + c, :], k_s[d][:, 2 + c, :], q_s[d][:, c, :], start=True, stop=True)
                        if d == 1:
                            ins.then_inc(m_summed.sem, 1)

                def head(i, following):
                    v_sides.wait(pe, i, 2)
                    tok_copied.wait(pe, i, 2)
                    turn(1)
                    for d in range(2):
                        tok_copied.wait(pe, i, 4)
                        low_ready.wait(pe, i, d + 1)
                        for c in range(4):
                            ins = pe.transpose(b4[d][:, c, :], low[d][:, c, :], g.ident[:])
                        ins.then_inc(low_turned.sem, 1)
                    for lv, _ in enumerate(LEVELS):
                        for d in range(2):
                            if lv == 0:
                                at_copied.wait(pe, i, d + 1)
                                inv2_ready.wait(pe, i, d + 1)
                                qd_ready.wait(pe, i, 2)
                                m_ready.wait(pe, i, 2)
                                inv2_ready.wait(pe, i, 2)
                                at_copied.wait(pe, i, 2)
                            else:
                                t_copied.wait(pe, i, 4 * lv + 2 * d - 2)
                                x_masked.wait(pe, i, 2 * lv + d - 1)
                            src = inv2[d] if lv == 0 else inv[d]
                            for c in range(4):
                                ins = pe.matmul(b4[3 * d][:, c, :], a_t[d][:, c, :], src[:, c, :], start=True, stop=True)
                            ins.then_inc(x_summed.sem, 1)
                        for d in range(2):
                            src_t = inv2_t[d] if lv == 0 else inv_t[d]
                            x_masked.wait(pe, i, 2 * lv + d + 1)
                            if lv < 5:
                                for c in range(4):
                                    ins = pe.matmul(b4[3 * d + 1][:, c, :], src_t[:, c, :], grown[d][lv][:, c, :], start=True, stop=True)
                                ins.then_inc(t_summed.sem, 1)
                            for c in range(4):
                                ins = pe.matmul(b4[3 * d + 2][:, c, :], grown[d][lv][:, c, :], src_t[:, c, :], start=True, stop=True)
                            ins.then_inc(t_summed.sem, 1)
                        if following is not None:
                            prepare(following, lv)
                    for n in range(4):
                        for d in range(2):
                            if n:
                                s_ready.wait(pe, i, 2 * (n - 1) + d + 1)
                                pe.matmul(bank[3 * d][:, 0:P], k_s[d][:, n, :], state[d][:], start=True, stop=True).then_inc(r_summed.sem, 1)
                            else:
                                t_copied.wait(pe, i, 22)
                        for d in range(2):
                            r_ready.wait(pe, i, 2 * n + d + 1)
                            pe.matmul(bank[3 * d + 1][:, 0:P], inv_t[d][:, n, :], rhs[d][:], start=True, stop=True).then_inc(u_summed.sem, 1)
                        for d in range(2):
                            u_copied.wait(pe, i, 2 * n + d + 1)
                            if n < 3:
                                pe.matmul(bank[3 * d + 2][:, 0:P], k_tok[d][:, n, :], u[d][:], start=True, stop=True).then_inc(s_summed.sem, 1)
                            if n >= 2:
                                if n == 3:
                                    y_added.wait(pe, i, d + 1)
                                elif following is not None:
                                    rooted.wait(pe, following, 2)
                                pe.matmul(bank[6 + d][:, 0:P], state[d][:], qd[d][:, n - 2, :], start=True, stop=False)
                                pe.matmul(bank[6 + d][:, 0:P], u[d][:], m_t[d][:, n - 2, :], start=False, stop=True).then_inc(y_summed.sem, 1)
                    if following is not None:
                        sum_decays(following)
                    o_squared.wait(pe, i)
                    pe.matmul(bank[7][:, 0:LAT], g.ones[:], half[:, 0, 0:LAT], start=True, stop=True).then_inc(o_summed.sem, 1)
                    if following is not None:
                        open_head(following)
                    round_done.wait(pe, i, 3)

                for part in (2, 4):
                    prepare(0, part)
                rooted.wait(pe, 0, 2)
                sum_decays(0)
                open_head(0)
                with pe.Fori(0, 7) as i:
                    head(i, i + 1)
                head(7, None)

            @block.scalar
            def _(act):
                z_in = s.sem("z_in")

                def prepare(j, part):
                    if part in (1, 2):
                        for n in ((1,), (2, 0))[part - 1]:
                            cols = LAT if n == 0 else TOK
                            convolved.wait(act, j, (3, 1, 2)[n])
                            act.activation(half[:, n, 0:cols], conv[n][:], ACT.Tanh, scale=0.5).then_inc(bent.sem, 1)
                    elif part == 3:
                        sq_summed.wait(act, j, 1)
                        act.activation(half[:, 1, :], bank[7][:], ACT.Sqrt, bias=eps[:, 0:1], scale=0.25).then_inc(rooted.sem, 1)
                    elif part == 4:
                        sq_summed.wait(act, j, 2)
                        act.activation(half[:, 0, 0:LAT], bank[6][:, 0:LAT], ACT.Sqrt, bias=eps[:, 0:1], scale=0.25).then_inc(rooted.sem, 1)

                def bend_decays(j):
                    for d in range(2):
                        for n in range(4):
                            ins = act.activation(v_s[d][:, n, :], seq(conv[2][:], d, n), ACT.Copy, scale=0.5)
                        ins.then_inc(v_sides.sem, 1)
                    for d in range(2):
                        d_in.wait(act, j, d + 1)
                        act.activation(low[d][:], low[d][:], ACT.Exp, scale=-1.0).then_inc(d_bent.sem, 1)
                        dt_in.wait(act, j, d + 1)
                        act.activation(m_t[d][:], m_t[d][:], ACT.Exp).then_inc(dt_bent.sem, 1)
                    end_read.wait(act, j)
                    act.activation(e_end[:], g_end[:], ACT.Exp).then_inc(cols_bent.sem, 1)
                    act.activation(tail[:], tail[:], ACT.Exp).then_inc(cols_bent.sem, 1)
                    act.activation(nbe[:], cur_gc[:], ACT.Exp).then_inc(cols_bent.sem, 1)
                    for d in range(2):
                        g_summed.wait(act, j, d + 1)
                        act.activation(qd[d][:], b4[2 + d][:, 2:4, :], ACT.Exp).then_inc(a_step.sem, 1)

                def head(i, following):
                    act.dma_start(z[:], g.d_p[bass.ds(i * P + Z0, P), 0:LAT]).then_inc(z_in, 16)
                    cols_bent.wait(act, i, 3)
                    for d in range(2):
                        for k, (dst, col) in enumerate(((k_tok[d], tail), (v_tok[d], cur_be))):
                            turned.wait(act, i, 2 * d + k + 1)
                            for n in range(4):
                                ins = act.activation(dst[:, n, :], b4[k][:, n, :], ACT.Copy, scale=col[:, d, n:n + 1])
                            ins.then_inc(tok_copied.sem, 1)
                    for d in range(2):
                        low_turned.wait(act, i, d + 1)
                        inv2_ready.wait(act, i, d + 1)
                        act.activation(a_t[d][:], b4[d][:], ACT.Copy).then_inc(at_copied.sem, 1)
                    for lv in range(6):
                        for d in range(2):
                            if lv < 5:
                                t_summed.wait(act, i, 4 * lv + 2 * d + 2)
                                act.activation(inv[d][:], b4[3 * d + 1][:], ACT.Copy).then_inc(t_copied.sem, 1)
                            else:
                                t_summed.wait(act, i, 20 + d + 1)
                            act.activation(inv_t[d][:], b4[3 * d + 2][:], ACT.Copy).then_inc(t_copied.sem, 1)
                        if following is not None:
                            prepare(following, lv)
                    for n in range(4):
                        for d in range(2):
                            u_summed.wait(act, i, 2 * n + d + 1)
                            act.activation(u[d][:], bank[3 * d + 1][:, 0:P], ACT.Copy).then_inc(u_copied.sem, 1)
                    act.wait_ge(z_in, 16 * i + 16)
                    act.activation(half[:, 2, 0:LAT], z[:], ACT.Tanh, scale=0.5).then_inc(z_bent.sem, 1)
                    if following is not None:
                        bend_decays(following)
                    o_summed.wait(act, i)
                    act.activation(half[:, 0, 0:LAT], bank[7][:, 0:LAT], ACT.Sqrt, bias=eps[:, 0:1], scale=1.0 / P).then_inc(o_rooted.sem, 1)
                    o_rooted.wait(act, i)
                    act.sem_inc(round_done.sem, 1)
                    round_done.wait(act, i, 3)

                for part in range(1, 5):
                    prepare(0, part)
                bend_decays(0)
                with act.Fori(0, 7) as i:
                    head(i, i + 1)
                head(7, None)

            @block.vector
            def _(dve):
                boot = Steps(dve, s.sem("boot"))
                boot(dve.memset(eps[:], EPS))

                def convolve(step, j, n, count):
                    parts = 1 if n == 0 else 2
                    src = raw[n][:].rearrange("p (a t) -> p a t", a=parts)
                    out = conv[n][:].rearrange("p (a t) -> p a t", a=parts)
                    step(dve.tensor_scalar(out, src, cur_w[:, 2, n:n + 1], None, ALU.mult))
                    for tap in (0, 1, 3, 4):
                        by = tap - 2
                        lo, hi = max(0, -by), min(LAT, LAT - by)
                        ins = dve.scalar_tensor_tensor(out[:, :, lo:hi], src[:, :, lo + by:hi + by], cur_w[:, tap, n:n + 1],
                                                       out[:, :, lo:hi], ALU.mult, ALU.add)
                        if tap == 4:
                            step.tell(ins, convolved, count)
                        else:
                            step(ins)

                def silu(step, j, n, count):
                    cols = LAT if n == 0 else TOK
                    bent.wait(dve, j, count)
                    step(dve.scalar_tensor_tensor(conv[n][:], half[:, n, 0:cols], 1.0, conv[n][:], ALU.add, ALU.mult))
                    if n != 2:
                        step.tell(dve.tensor_tensor(half[:, n, 0:cols], conv[n][:], conv[n][:], ALU.mult), squared, 1 if n else 2)

                def prepare(step, j, part):
                    if part == 0:
                        step(dve.tensor_copy(cur_w[:], taps[:, :, :, bass.ds(j, 1)].rearrange("p t j a -> p t (j a)")))
                        dve.wait_ge(head_loaded, 48 * j + 48)
                        convolve(step, j, 1, 1)
                    elif part == 1:
                        convolve(step, j, 2, 2)
                        convolve(step, j, 0, 3)
                    elif part == 2:
                        silu(step, j, 1, 1)
                    elif part == 3:
                        silu(step, j, 2, 2)
                        silu(step, j, 0, 3)
                    else:
                        n = 5 - part
                        rooted.wait(dve, j, part - 3)
                        cols = LAT if n == 0 else TOK
                        step(dve.reciprocal(half[:, n, 0:cols], half[:, n, 0:cols]))
                        step(dve.scalar_tensor_tensor(conv[n][:], conv[n][:], 0.5 if n else 0.5 * P ** -0.5, half[:, n, 0:cols],
                                                      ALU.mult, ALU.mult))
                        if part == 5:
                            step(dve.tensor_copy(cur_g[:], g_seq[:, :, :, bass.ds(j, 1)].rearrange("p d n a -> p d (n a)")))
                            step.tell(dve.tensor_copy(g_wide[:], cur_g[:].unsqueeze(3).broadcast_to([P, 2, 4, P])), widened)
                            step.end()

                def copy_sides(step, j):
                    for d in range(2):
                        for n in range(4):
                            step.free(dve.tensor_copy(k_s[d][:, n, :], seq(conv[1][:], d, n)))
                        step.free(dve.tensor_copy(q_s[d][:, 0, :], seq(conv[0][:], d, 2)))
                        step.tell(dve.tensor_copy(q_s[d][:, 1, :], seq(conv[0][:], d, 3)), sides_ready, d + 1)

                def weigh_decays(step, j):
                    copy_sides(step, j)
                    at = bass.ds(j, 1)
                    for dst, src in ((cur_gc, gc_seq), (cur_be, be_seq)):
                        step(dve.tensor_copy(dst[:], src[:, :, :, at].rearrange("p d n a -> p d (n a)")))
                    for d in range(2):
                        g_summed.wait(dve, j, d + 1)
                        step(dve.tensor_copy(g_end[:, d, :], b4[2 + d][:, :, P - 1]))
                        for n in range(4):
                            ins = dve.tensor_scalar(low[d][:, n, :], b4[2 + d][:, n, :], cur_gc[:, d, n:n + 1], 0.0, ALU.subtract, ALU.max)
                            if n == 3:
                                step.tell(ins, d_in, d + 1)
                            else:
                                step.free(ins)
                        for n in (2, 3):
                            ins = dve.tensor_scalar(m_t[d][:, n - 2, :], b4[2 + d][:, n, :], cur_gc[:, d, n:n + 1], 0.0, ALU.subtract, ALU.min)
                            if n == 3:
                                step.tell(ins, dt_in, d + 1)
                            else:
                                step.free(ins)
                    step.tell(dve.tensor_tensor(tail[:], g_end[:], cur_gc[:], ALU.subtract), end_read)
                    step(dve.tensor_scalar(nbeta[:], cur_be[:], -1.0, None, ALU.mult))
                    cols_bent.wait(dve, j, 3)
                    step(dve.tensor_tensor(nbe[:], nbe[:], nbeta[:], ALU.mult))
                    step.end()

                def head(i, following):
                    step = Chain(dve, v_step, i)
                    ahead = Chain(dve, p_step, following)
                    at = bass.ds(i, 1)
                    a_step.wait(dve, i, 2)
                    for d in range(2):
                        step(dve.tensor_tensor(qd[d][:], qd[d][:], q_s[d][:], ALU.mult))
                    dve.sem_inc(qd_ready.sem, 2)
                    for d in range(2):
                        d_bent.wait(dve, i, d + 1)
                        grams.wait(dve, i, d + 1)
                        step(dve.tensor_tensor(low[d][:], low[d][:], b4[4 + d][:], ALU.mult))
                        for n in range(4):
                            ins = dve.scalar_tensor_tensor(low[d][:, n, :], low[d][:, n, :], nbeta[:, d, n:n + 1], g.back[:, 2, :],
                                                           ALU.mult, ALU.mult)
                            if n == 3:
                                step.tell(ins, low_ready, d + 1)
                            else:
                                step.free(ins)
                        x_filled.wait(dve, 0)
                        dve.memset(held[:], 0.0)
                        step(dve.copy_predicated(inv2[d][:], wide(g.level[:, 0, :]), low[d][:]))
                    for d in range(2):
                        dt_bent.wait(dve, i, d + 1)
                        m_summed.wait(dve, i)
                        step(dve.tensor_tensor(m_t[d][:], m_t[d][:], g.mask[:, 1, :].unsqueeze(1).broadcast_to([P, 2, P]), ALU.mult))
                        step.tell(dve.tensor_tensor(m_t[d][:], m_t[d][:], b4[6][:, 2 * d:2 * d + 2, :], ALU.mult), m_ready, d + 1)
                    for d in range(2):
                        low_turned.wait(dve, i, d + 1)
                        dve.memset(held[:], 0.0)
                        step.tell(dve.copy_predicated(inv2_t[d][:], wide(g.level[:, 7, :]), b4[d][:]), inv2_ready, d + 1)
                    for lv in range(6):
                        for d in range(2):
                            x_summed.wait(dve, i, 2 * lv + d + 1)
                            dve.memset(held[:], 0.0)
                            step.tell(dve.copy_predicated(grown[d][lv][:], wide(g.level[:, lv + 1, :]), b4[3 * d][:]),
                                      x_masked, 2 * lv + d + 1)
                        if following is not None:
                            prepare(ahead, following, lv)
                    for n in range(4):
                        for d in range(2):
                            if n == 0:
                                step.tell(dve.tensor_copy(rhs[d][:], v_tok[d][:, 0, :]), r_ready, d + 1)
                            else:
                                r_summed.wait(dve, i, 2 * (n - 1) + d + 1)
                                step.tell(dve.scalar_tensor_tensor(rhs[d][:], bank[3 * d][:, 0:P], nbe[:, d, n:n + 1], v_tok[d][:, n, :],
                                                                   ALU.mult, ALU.add), r_ready, 2 * n + d + 1)
                        for d in range(2):
                            if n == 0:
                                s_summed.wait(dve, i, d + 1)
                                step.tell(dve.tensor_copy(state[d][:], bank[3 * d + 2][:, 0:P]), s_ready, d + 1)
                            elif n < 3:
                                s_summed.wait(dve, i, 2 * n + d + 1)
                                if n == 2:
                                    y_summed.wait(dve, i, d + 1)
                                step.tell(dve.scalar_tensor_tensor(state[d][:], state[d][:], e_end[:, d, n:n + 1], bank[3 * d + 2][:, 0:P],
                                                                   ALU.mult, ALU.add), s_ready, 2 * n + d + 1)
                            if n >= 2:
                                y_summed.wait(dve, i, 2 * (n - 2) + d + 1)
                                dst = seq(o[:], d, n)
                                first = (n == 2)
                                ins = (dve.tensor_copy(dst, bank[6 + d][:, 0:P]) if first else
                                       dve.tensor_tensor(dst, dst, bank[6 + d][:, 0:P], ALU.add))
                                step.tell(ins, y_added, 2 * (n - 2) + d + 1)
                    step.tell(dve.tensor_tensor(half[:, 0, 0:LAT], o[:], o[:], ALU.mult), o_squared)
                    if following is not None:
                        weigh_decays(Chain(dve, d_step, following), following)
                    o_rooted.wait(dve, i)
                    step(dve.reciprocal(half[:, 0, 0:LAT], half[:, 0, 0:LAT]))
                    step(dve.scalar_tensor_tensor(o[:], o[:], norm_w[:, 0:1], half[:, 0, 0:LAT], ALU.mult, ALU.mult))
                    z_bent.wait(dve, i)
                    step(dve.scalar_tensor_tensor(half[:, 2, 0:LAT], half[:, 2, 0:LAT], 1.0, z[:], ALU.add, ALU.mult))
                    step(dve.scalar_tensor_tensor(g.o_b[:, at, :].rearrange("p a t -> p (a t)"), o[:], 0.5, half[:, 2, 0:LAT],
                                                  ALU.mult, ALU.mult))
                    step.end()
                    dve.sem_inc(round_done.sem, 2)
                    round_done.wait(dve, i, 3)

                first = Chain(dve, p_step, 0)
                for part in range(6):
                    prepare(first, 0, part)
                weigh_decays(Chain(dve, d_step, 0), 0)
                with dve.Fori(0, 7) as i:
                    head(i, i + 1)
                head(7, None)


HD = 64
HEADS = 8
MLA_Q, MLA_DK = 384, 96
C_KV, K_PE = 384, 512
FOX_Q, FOX_K, FOX_V, FOX_F = 544, 1056, 1568, 2080
NSA_Q, NSA_KC, NSA_VC, NSA_KS, NSA_VS, NSA_KW, NSA_VW, NSA_GATE = 2088, 2600, 2728, 2856, 2984, 3112, 3240, 3368
SWA_Q, SWA_K, SWA_V = 3392, 3904, 4032
CMP_LEN, CMP_STRIDE = 32, 16
CMP = (LAT - CMP_LEN) // CMP_STRIDE + 1
REL_MAX = 128
NEG = -1e30
V_COLS = 2 * 512 + 3 * P


def phase_latent(nc, g):
    with ExitStack() as stack:
        s = Scope(nc, stack, "la")
        lat = s.sb("lat", [P, 4, LAT])
        sq = s.sb("sq", [P, 4, LAT])
        rows, cols = s.sb("rows", [4, P]), s.sb("cols", [P, 4])
        rstd = s.sb("rstd", [P, 2, LAT])
        eps = s.sb("eps", [P, 1])
        rot, cs = s.sb("rot", [MLA_DK, MLA_DK]), s.sb("cs", [MLA_DK, 2, LAT])
        kp, ko, kr = (s.sb(n, [MLA_DK, LAT]) for n in ("kp", "ko", "kr"))
        w_q, w_kv = s.sb("w_q", [P, 3, HEADS * MLA_DK]), s.sb("w_kv", [P, HEADS * P])
        qh, qr = s.sb("qh", [MLA_DK, 2, LAT]), s.sb("qr", [MLA_DK, 2, LAT])
        qo, kvh, vo = s.sb("qo", [MLA_DK, HEADS, LAT]), s.sb("kvh", [P, HEADS, LAT]), s.sb("vo", [P, 2, HEADS, HD])
        bank = [s.ps(f"bank{i}", [P, 512]) for i in range(8)]
        loaded, pe_in, zeroed, w_in, stored, pe_stored = (s.sem(n) for n in ("loaded", "pe_in", "zeroed", "w_in", "stored", "pe_stored"))
        squared, turned, summed, rooted, stepped, latents_ready, kp_turned, kp_done = (s.sem(n) for n in (
            "squared", "turned", "summed", "rooted", "stepped", "latents_ready", "kp_turned", "kp_done"))
        q_summed, kv_summed, q_copied, kv_copied, rotated, v_turned, q_done, v_done, q_turned = (s.sem(n) for n in (
            "q_summed", "kv_summed", "q_copied", "kv_copied", "rotated", "v_turned", "q_done", "v_done", "q_turned"))

        with nc.Block() as block:

            @block.sync
            def _(sp):
                sp.dma_start(w_q[:], g.mla_w_uq_2[0].rearrange("(k p) n -> p k n", p=P)).then_inc(w_in, 16)
                sp.dma_start(w_kv[:], g.mla_w_ukv_2[0]).then_inc(w_in, 16)
                sp.dma_start(lat[:], g.d_p2[0:512, :].rearrange("(k p) t -> p k t", p=P)).then_inc(loaded, 16)
                sp.dma_start(rows[0:3, :], g.mla_q_norm_2[0].rearrange("(k p) -> k p", p=P)).then_inc(loaded, 16)
                sp.dma_start(rows[3:4, :], g.mla_kv_norm_2).then_inc(loaded, 16)
                sp.dma_start(rot[:], g.c_rot).then_inc(loaded, 16)
                sp.dma_start(cs[:], g.c_rope).then_inc(loaded, 16)
                sp.wait_ge(zeroed, 1)
                sp.dma_start(kp[HD:MLA_DK, :], g.d_p2[K_PE:K_PE + 32, :]).then_inc(pe_in, 16)

            @block.tensor
            def _(pe):
                pe.wait_ge(loaded, 80)
                pe.transpose(bank[7][:, 0:4], rows[:], g.ident[0:4, 0:4]).then_inc(turned, 1)
                pe.wait_ge(squared, 1)
                for k in range(3):
                    pe.matmul(bank[0][:, 0:LAT], g.ones[:], sq[:, k, :], start=(k == 0), stop=(k == 2))
                pe.matmul(bank[1][:, 0:LAT], g.ones[:], sq[:, 3, :], start=True, stop=True).then_inc(summed, 1)
                pe.wait_ge(pe_in, 16)
                pe.matmul(bank[6][0:MLA_DK, 0:LAT], rot[:], kp[:], start=True, stop=True).then_inc(kp_turned, 1)
                pe.wait_ge(latents_ready, 1)
                pe.wait_ge(w_in, 32)
                pe.wait_ge(kp_done, 1)
                for h in range(HEADS + 1):
                    if h < HEADS:
                        b = h % 2
                        if h >= 2:
                            pe.wait_ge(q_copied, h - 1)
                            pe.wait_ge(kv_copied, h - 1)
                        for k in range(3):
                            ins = pe.matmul(bank[2 + b][0:MLA_DK, 0:LAT], w_q[:, k, MLA_DK * h:MLA_DK * (h + 1)], lat[:, k, :],
                                            start=(k == 0), stop=(k == 2))
                        ins.then_inc(q_summed, 1)
                        pe.matmul(bank[4 + b][:, 0:LAT], w_kv[:, P * h:P * (h + 1)], lat[:, 3, :], start=True, stop=True)\
                          .then_inc(kv_summed, 1)
                    if h:
                        n, b = h - 1, (h - 1) % 2
                        pe.wait_ge(q_copied, n + 1)
                        if n:
                            pe.wait_ge(q_turned, n)
                        pe.matmul(bank[6][0:MLA_DK, 0:LAT], rot[:], qh[:, b, :], start=True, stop=True).then_inc(rotated, 1)
                        pe.wait_ge(kv_copied, n + 1)
                        if n >= 2:
                            pe.wait_ge(v_done, n - 1)
                        for t in range(2):
                            ins = pe.transpose(bank[b][:, P * t:P * t + P], kvh[:, n, P * t:P * t + P], g.ident[:])
                        ins.then_inc(v_turned, 1)

            @block.scalar
            def _(act):
                act.wait_ge(loaded, 80)
                act.activation(sq[:], lat[:], ACT.Square).then_inc(squared, 1)
                act.wait_ge(summed, 1)
                act.wait_ge(zeroed, 2)
                act.activation(rstd[:, 0, :], bank[0][:, 0:LAT], ACT.Sqrt, bias=eps[:, 0:1], scale=1.0 / MLA_Q).then_inc(rooted, 1)
                act.activation(rstd[:, 1, :], bank[1][:, 0:LAT], ACT.Sqrt, bias=eps[:, 0:1], scale=1.0 / P).then_inc(rooted, 1)
                act.wait_ge(kp_done, 1)
                act.dma_start(g.d_mk[:, HD:MLA_DK, :].rearrange("h r t -> r h t"),
                              ko[HD:MLA_DK, :].unsqueeze(1).broadcast_to([32, HEADS, LAT])).then_inc(pe_stored, 16)
                for h in range(HEADS):
                    act.wait_ge(q_summed, h + 1)
                    if h >= 2:
                        act.wait_ge(q_done, h - 1)
                    act.activation(qh[:, h % 2, :], bank[2 + h % 2][0:MLA_DK, 0:LAT], ACT.Copy).then_inc(q_copied, 1)
                    act.wait_ge(kv_summed, h + 1)
                    act.activation(kvh[:, h, :], bank[4 + h % 2][:, 0:LAT], ACT.Copy).then_inc(kv_copied, 1)
                act.wait_ge(kv_copied, HEADS)
                act.dma_start(g.d_mk[:, 0:HD, :].rearrange("h r t -> r h t"), kvh[0:HD, :, :]).then_inc(stored, 16)
                act.wait_ge(q_done, HEADS)
                act.dma_start(g.d_mq.rearrange("h r t -> r h t"), qo[:]).then_inc(stored, 16)
                act.wait_ge(v_done, HEADS)
                act.dma_start(g.d_v[:, 0:HEADS * HD].rearrange("(t p) c -> p t c", p=P), vo[:].rearrange("p t h c -> p t (h c)"))\
                   .then_inc(stored, 16)
                act.wait_ge(stored, 48)
                act.wait_ge(pe_stored, 16)

            @block.vector
            def _(dve):
                step = Steps(dve, stepped)
                dve.memset(kp[:], 0.0).then_inc(zeroed, 1)
                dve.memset(eps[:], EPS).then_inc(zeroed, 1)
                dve.wait_ge(turned, 1)
                step(dve.tensor_copy(cols[:], bank[7][:, 0:4]))
                dve.wait_ge(rooted, 2)
                step(dve.reciprocal(rstd[:], rstd[:]))
                for k in range(4):
                    step.free(dve.scalar_tensor_tensor(lat[:, k, :], lat[:, k, :], cols[:, k:k + 1], rstd[:, k // 3, :], ALU.mult, ALU.mult))
                step.settle()
                dve.sem_inc(latents_ready, 1)
                dve.wait_ge(pe_in, 16)
                step(dve.tensor_tensor(ko[:], kp[:], cs[:, 0, :], ALU.mult))
                dve.wait_ge(kp_turned, 1)
                step(dve.tensor_tensor(kr[:], bank[6][0:MLA_DK, 0:LAT], cs[:, 1, :], ALU.mult))
                dve.tensor_tensor(ko[:], ko[:], kr[:], ALU.add).then_inc(kp_done, 1)
                for h in range(HEADS):
                    b = h % 2
                    dve.wait_ge(q_copied, h + 1)
                    step.free(dve.tensor_tensor(qo[:, h, :], qh[:, b, :], cs[:, 0, :], ALU.mult))
                    dve.wait_ge(rotated, h + 1)
                    dve.tensor_tensor(qr[:, b, :], bank[6][0:MLA_DK, 0:LAT], cs[:, 1, :], ALU.mult).then_inc(q_turned, 1)
                    dve.wait_ge(q_turned, h + 1)
                    step.settle()
                    dve.tensor_tensor(qo[:, h, :], qo[:, h, :], qr[:, b, :], ALU.add).then_inc(q_done, 1)
                    dve.wait_ge(v_turned, h + 1)
                    dve.tensor_copy(vo[:, :, h, :], bank[b][:, 0:LAT].rearrange("p (t c) -> p t c", t=2)[:, :, HD:P]).then_inc(v_done, 1)


def phase_tables(nc, g):
    tiles = [FOX_V + P * k for k in range(4)] + [NSA_VS, NSA_VW, SWA_V]
    with ExitStack() as stack:
        s = Scope(nc, stack, "tb")
        vch = s.sb("vch", [P, 7, LAT])
        vt = s.sb("vt", [P, 2, 7 * P])
        f, ft = s.sb("f", [HEADS, LAT]), s.sb("ft", [HEADS, LAT])
        bf = s.sb("bf", [HEADS, 1])
        f_tok, f_sum = s.sb("f_tok", [P, 2, HEADS]), s.sb("f_sum", [P, 2, HEADS])
        f_row = s.sb("f_row", [HEADS, LAT])
        fb = s.sb("fb", [P, HEADS, LAT])
        fox = s.sb("fox", [P, HEADS, 2, LAT])
        causal = s.sb("causal", [P, 2, LAT])
        mask = s.sb("mask", [P, 2, P])
        rel = s.sb("rel", [33, 2 * HEADS])
        rel_w = s.sb("rel_w", [33, 2 * HEADS, P])
        hot = s.sb("hot", [33, 2, 512])
        tz = s.sb("tz", [P, 4, 512])
        bank = [s.ps(f"bank{i}", [P, 512]) for i in range(8)]
        loaded, rel_in, ones_set, turned, v_copied, v_stored = (s.sem(n) for n in (
            "loaded", "rel_in", "ones_set", "turned", "v_copied", "v_stored"))
        neg_ready, bent, stepped, f_ready, f_turned, f_tok_ready, f_summed, row_ready, row_out, row_in, fox_ready, fox_out = (
            s.sem(n) for n in ("neg_ready", "bent", "stepped", "f_ready", "f_turned", "f_tok_ready", "f_summed",
                               "row_ready", "row_out", "row_in", "fox_ready", "fox_out"))
        rel_ready, tz_summed, tz_copied = s.sem("rel_ready"), s.sem("tz_summed"), s.sem("tz_copied")
        tz_out = [s.sem(f"tz_out{k}") for k in range(4)]

        with nc.Block() as block:

            @block.sync
            def _(sp):
                sp.wait_ge(ones_set, 1)
                sp.dma_start(rel[0:32, :], g.rel_bias_2).then_inc(rel_in, 16)
                for dst, src in ((f[:], g.d_p2[FOX_F:FOX_F + HEADS, :]), (bf[:], g.fox_b_f_2[0].unsqueeze(1)),
                                 (hot[:], g.c_bucket), (mask[:], g.c_mask), (causal[:], g.c_causal),
                                 (vch[:, 0:4, :], g.d_p2[FOX_V:FOX_V + 512, :].rearrange("(k p) t -> p k t", p=P))):
                    sp.dma_start(dst, src).then_inc(loaded, 16)
                for k in range(4, 7):
                    sp.dma_start(vch[:, k, :], g.d_p2[tiles[k]:tiles[k] + P, :]).then_inc(loaded, 16)
                sp.wait_ge(row_ready, 1)
                sp.dma_start(g.d_frow, f_row[:]).then_inc(row_out, 16)
                sp.wait_ge(row_out, 16)
                for h in range(HEADS):
                    sp.dma_start(fb[:, h, :], g.d_frow[h].partition_broadcast(P)).then_inc(row_in, 16)
                for h in range(2 * HEADS):
                    sp.wait_ge(tz_copied, h + 1)
                    sp.dma_start(g.d_skew[h, 0:P * 512].rearrange("(p x) -> p x", p=P), tz[:, h % 4, :]).then_inc(tz_out[h % 4], 16)
                sp.wait_ge(fox_ready, 1)
                sp.dma_start(g.d_fox.rearrange("h p q k -> p h (q k)"), fox[:].rearrange("p h q k -> p h (q k)")).then_inc(fox_out, 16)
                sp.wait_ge(fox_out, 16)
                for k in range(4):
                    sp.wait_ge(tz_out[k], 64)

            @block.tensor
            def _(pe):
                pe.wait_ge(rel_ready, 1)
                pe.wait_ge(loaded, 144)
                for k in range(7):
                    if k >= 2:
                        pe.wait_ge(v_copied, k - 1)
                    for t in range(2):
                        ins = pe.transpose(bank[k % 2][:, P * t:P * t + P], vch[:, k, P * t:P * t + P], g.ident[:])
                    ins.then_inc(turned, 1)
                pe.wait_ge(f_ready, 1)
                for t in range(2):
                    ins = pe.transpose(bank[2][:, HEADS * t:HEADS * t + HEADS], f[:, P * t:P * t + P], g.ident[0:HEADS, 0:HEADS])
                ins.then_inc(f_turned, 1)
                pe.wait_ge(f_tok_ready, 1)
                upto = mask[:, 1, :]
                pe.matmul(bank[3][:, 0:HEADS], upto, f_tok[:, 0, :], start=True, stop=True)
                pe.matmul(bank[3][:, 16:16 + HEADS], upto, f_tok[:, 1, :], start=True, stop=False)
                pe.matmul(bank[3][:, 16:16 + HEADS], g.ones[:], f_tok[:, 0, :], start=False, stop=True)
                pe.matmul(bank[4][0:HEADS, 0:P], f_tok[:, 0, :], upto, start=True, stop=True)
                pe.matmul(bank[4][0:HEADS, P:LAT], f_tok[:, 1, :], upto, start=True, stop=False)
                pe.matmul(bank[4][0:HEADS, P:LAT], f_tok[:, 0, :], g.ones[:], start=False, stop=True).then_inc(f_summed, 1)
                for h in range(2 * HEADS):
                    if h >= 2:
                        pe.wait_ge(tz_copied, h - 1)
                    pe.matmul(bank[6 + h % 2][:], rel_w[:, h, :], hot[:, h // HEADS, :], start=True, stop=True).then_inc(tz_summed, 1)

            @block.scalar
            def _(act):
                act.wait_ge(neg_ready, 1)
                act.activation(ft[:], ft[:], ACT.Exp).then_inc(bent, 1)
                act.wait_ge(neg_ready, 2)
                act.activation(ft[:], ft[:], ACT.Ln).then_inc(bent, 1)
                for k in range(7):
                    act.wait_ge(turned, k + 1)
                    act.activation(vt[:, :, P * k:P * k + P], bank[k % 2][:, 0:LAT].rearrange("p (t c) -> p t c", t=2), ACT.Copy)\
                       .then_inc(v_copied, 1)
                act.wait_ge(v_copied, 7)
                act.dma_start(g.d_v[:, 512:V_COLS].rearrange("(t p) c -> p t c", p=P), vt[:]).then_inc(v_stored, 16)
                for h in range(2 * HEADS):
                    act.wait_ge(tz_summed, h + 1)
                    if h >= 4:
                        act.wait_ge(tz_out[h % 4], 16 * (h // 4))
                    act.activation(tz[:, h % 4, :], bank[6 + h % 2][:], ACT.Copy).then_inc(tz_copied, 1)
                act.wait_ge(v_stored, 16)

            @block.vector
            def _(dve):
                step = Steps(dve, stepped)
                dve.memset(rel[32:33, :], 1.0).then_inc(ones_set, 1)
                dve.wait_ge(rel_in, 16)
                dve.tensor_copy(rel_w[:], rel[:].unsqueeze(2).broadcast_to([33, 2 * HEADS, P])).then_inc(rel_ready, 1)
                dve.wait_ge(loaded, 144)
                step(dve.tensor_scalar(f[:], f[:], bf[:, 0:1], None, ALU.add))
                step(dve.tensor_scalar(ft[:], f[:], -1.0, None, ALU.mult))
                dve.tensor_tensor(ft[:], ft[:], f[:], ALU.min).then_inc(neg_ready, 1)
                dve.wait_ge(bent, 1)
                dve.tensor_scalar(ft[:], ft[:], 1.0, None, ALU.add).then_inc(neg_ready, 1)
                dve.wait_ge(bent, 2)
                dve.scalar_tensor_tensor(f[:], f[:], 0.0, ft[:], ALU.min, ALU.subtract).then_inc(f_ready, 1)
                dve.wait_ge(f_turned, 1)
                dve.tensor_copy(f_tok[:], bank[2][:, 0:2 * HEADS].rearrange("p (t h) -> p t h", t=2)).then_inc(f_tok_ready, 1)
                dve.wait_ge(f_summed, 1)
                dve.tensor_copy(f_row[:], bank[4][0:HEADS, 0:LAT]).then_inc(row_ready, 1)
                step(dve.tensor_copy(f_sum[:], bank[3][:, 0:32].rearrange("p (t h) -> p t h", t=2)[:, :, 0:HEADS]))
                dve.wait_ge(row_in, 16 * HEADS)
                for h in range(HEADS):
                    for t in range(2):
                        step.free(dve.tensor_scalar(fox[:, h, t, :], fb[:, h, :], -1.0, f_sum[:, t, h:h + 1], ALU.mult, ALU.add))
                step.settle()
                dve.tensor_tensor(fox[:].rearrange("p h q k -> p h (q k)"), fox[:].rearrange("p h q k -> p h (q k)"),
                                  causal[:].rearrange("p q k -> p (q k)").unsqueeze(1).broadcast_to([P, HEADS, 2 * LAT]), ALU.add)\
                   .then_inc(fox_ready, 1)


def skewed(g, h, t):
    start = LAT - 1 - P * t
    return g.d_skew[bass.ds(h, 1), start:start + P * 511].rearrange("h (p x) -> (h p) x", x=511)[:, 0:LAT]


def phase_compressed(nc, g):
    with ExitStack() as stack:
        s = Scope(nc, stack, "co")
        kv = s.sb("kv", [HD, 2, 2, LAT])
        w1, w2 = s.sb("w1", [HD, 2, CMP_LEN, HD]), s.sb("w2", [HD, 2, HD])
        pos, pos_t = s.sb("pos", [2 * CMP_LEN, HD]), s.sb("pos_t", [HD, 2, CMP_LEN])
        blk = s.sb("blk", [HD, 2, CMP_LEN, 2, CMP])
        pre, bend, hid = (s.sb(n, [HD, 2, 2 * CMP]) for n in ("pre", "bend", "hid"))
        k_cmp, v_cmp = s.sb("k_cmp", [HD, 2 * CMP]), s.sb("v_cmp", [CMP, 2, HD])
        q = s.sb("q", [HD, HEADS, LAT])
        bias = s.sb("bias", [P, 2, HEADS, LAT])
        valid = s.sb("valid", [P, 2, CMP])
        sc = s.sb("sc", [P, 2, HEADS, CMP])
        top, tot = s.sb("top", [P, 2, HEADS]), s.sb("tot", [P, 2, HEADS])
        p_t = s.sb("p_t", [CMP, HEADS, LAT])
        o = s.sb("o", [HD, HEADS, LAT])
        bank = [s.ps(f"bank{i}", [P, 512]) for i in range(8)]
        loaded, q_in, bias_in, turned, pos_ready, blk_ready = (s.sem(n) for n in (
            "loaded", "q_in", "bias_in", "turned", "pos_ready", "blk_ready"))
        h_summed, stepped, arg_ready, bent, hid_ready, kv_summed, kv_ready = (s.sem(n) for n in (
            "h_summed", "stepped", "arg_ready", "bent", "hid_ready", "kv_summed", "kv_ready"))
        scored, lowered, raised, weighed, p_turned, p_ready, mixed, copied, stored = (s.sem(n) for n in (
            "scored", "lowered", "raised", "weighed", "p_turned", "p_ready", "mixed", "copied", "stored"))

        with nc.Block() as block:

            @block.sync
            def _(sp):
                sp.dma_start(pos[:], g.nsa_cmp_pos_2[0].rearrange("k l d -> (k l) d")).then_inc(loaded, 16)
                sp.dma_start(w2[:], g.nsa_cmp_w2_2[0].rearrange("k d o -> d k o")).then_inc(loaded, 16)
                for k, row in enumerate((NSA_KC, NSA_VC)):
                    sp.dma_start(kv[:, k], g.d_p2[row:row + P, :].rearrange("(g d) t -> d g t", g=2)).then_inc(loaded, 16)
                    sp.dma_start(w1[:, k], g.nsa_cmp_w1_2[0, k].rearrange("(l d) o -> d l o", d=HD)).then_inc(loaded, 16)
                sp.dma_start(valid[:], g.c_valid).then_inc(loaded, 16)
                sp.dma_start(q[:], g.d_p2[NSA_Q:NSA_Q + 512, :].rearrange("(h d) t -> d h t", d=HD)).then_inc(q_in, 16)

            @block.scalar
            def _(act):
                for h in range(HEADS):
                    for t in range(2):
                        act.dma_start(bias[:, t, h, :], skewed(g, h, t)).then_inc(bias_in, 16)
                act.wait_ge(arg_ready, 1)
                act.activation(bend[:], bend[:], ACT.Tanh, scale=(2 / 3.141592653589793) ** 0.5).then_inc(bent, 1)
                act.wait_ge(lowered, 1)
                act.activation(sc[:], sc[:], ACT.Exp).then_inc(raised, 1)
                for b in range(4):
                    act.wait_ge(mixed, b + 1)
                    act.activation(o[:, 2 * b:2 * b + 2, :], bank[4 + b][0:HD, :].rearrange("p (h t) -> p h t", h=2), ACT.Copy)\
                       .then_inc(copied, 1)
                act.wait_ge(copied, 4)
                act.dma_start(g.d_n[0:512, :].rearrange("(h d) t -> d h t", d=HD), o[:]).then_inc(stored, 16)
                act.wait_ge(stored, 16)

            @block.tensor
            def _(pe):
                pe.wait_ge(loaded, 16 * 7)
                pe.transpose(bank[0][0:HD, 0:2 * CMP_LEN], pos[:], g.ident[0:2 * CMP_LEN, 0:2 * CMP_LEN]).then_inc(turned, 1)
                for k in range(2):
                    pe.wait_ge(blk_ready, k + 1)
                    for l in range(CMP_LEN):
                        ins = pe.matmul(bank[1 + k][0:HD, 0:2 * CMP], w1[:, k, l, :], blk[:, k, l].rearrange("p g c -> p (g c)"),
                                        start=(l == 0), stop=(l == CMP_LEN - 1))
                    ins.then_inc(h_summed, 1)
                pe.wait_ge(hid_ready, 1)
                pe.matmul(bank[0][0:HD, 0:2 * CMP], w2[:, 0, :], hid[:, 0, :], start=True, stop=True)
                for gr in range(2):
                    ins = pe.matmul(bank[3][0:CMP, HD * gr:HD * gr + HD], hid[:, 1, CMP * gr:CMP * gr + CMP], w2[:, 1, :],
                                    start=True, stop=True)
                ins.then_inc(kv_summed, 1)
                pe.wait_ge(kv_ready, 2)
                pe.wait_ge(q_in, 16)
                for t in range(2):
                    for h in range(HEADS):
                        at = CMP * (HEADS * t + h)
                        gr = h // 4
                        ins = pe.matmul(bank[4][:, at:at + CMP], q[:, h, P * t:P * t + P], k_cmp[:, CMP * gr:CMP * gr + CMP],
                                        start=True, stop=True)
                ins.then_inc(scored, 1)
                pe.wait_ge(weighed, 1)
                for h in range(HEADS):
                    for t in range(2):
                        ins = pe.transpose(bank[h // 2][0:CMP, LAT * (h % 2) + P * t:LAT * (h % 2) + P * t + P], sc[:, t, h, :], g.ident[:])
                    if h % 2:
                        ins.then_inc(p_turned, 1)
                for h in range(HEADS):
                    if h % 2 == 0:
                        pe.wait_ge(p_ready, h // 2 + 1)
                    ins = pe.matmul(bank[4 + h // 2][0:HD, LAT * (h % 2):LAT * (h % 2) + LAT], v_cmp[:, h // 4, :], p_t[:, h, :],
                                    start=True, stop=True)
                    if h % 2:
                        ins.then_inc(mixed, 1)

            @block.vector
            def _(dve):
                step = Steps(dve, stepped)
                dve.wait_ge(turned, 1)
                step(dve.tensor_copy(pos_t[:], bank[0][0:HD, 0:2 * CMP_LEN].rearrange("p (k l) -> p k l", k=2)))
                dve.wait_ge(loaded, 16 * 7)
                for k in range(2):
                    for a in range(2):
                        for gr in range(2):
                            src = kv[:, k, gr, 16 * a:16 * a + 16 * CMP].rearrange("p (c b) -> p b c", b=16)
                            step(dve.tensor_tensor(blk[:, k, 16 * a:16 * a + 16, gr, :], src,
                                                   pos_t[:, k, 16 * a:16 * a + 16].unsqueeze(2).broadcast_to([HD, 16, CMP]), ALU.add))
                    dve.sem_inc(blk_ready, 1)
                dve.wait_ge(h_summed, 2)
                for k in range(2):
                    step(dve.tensor_copy(pre[:, k, :], bank[1 + k][0:HD, 0:2 * CMP]))
                step(dve.tensor_tensor(bend[:], pre[:], pre[:], ALU.mult))
                step(dve.tensor_scalar(bend[:], bend[:], 0.044715, 1.0, ALU.mult, ALU.add))
                dve.tensor_tensor(bend[:], bend[:], pre[:], ALU.mult).then_inc(arg_ready, 1)
                step(dve.tensor_scalar(pre[:], pre[:], 0.5, None, ALU.mult))
                dve.wait_ge(bent, 1)
                dve.scalar_tensor_tensor(hid[:], bend[:], 1.0, pre[:], ALU.add, ALU.mult).then_inc(hid_ready, 1)
                dve.wait_ge(kv_summed, 1)
                dve.tensor_copy(k_cmp[:], bank[0][0:HD, 0:2 * CMP]).then_inc(kv_ready, 1)
                dve.tensor_copy(v_cmp[:], bank[3][0:CMP, 0:2 * HD].rearrange("p (g d) -> p g d", g=2)).then_inc(kv_ready, 1)
                dve.wait_ge(scored, 1)
                dve.wait_ge(bias_in, 16 * 2 * HEADS)
                ends = bias[:, :, :, CMP_LEN - 1:LAT:CMP_STRIDE]
                for t in range(2):
                    step(dve.scalar_tensor_tensor(sc[:, t], bank[4][:, CMP * HEADS * t:CMP * HEADS * (t + 1)].rearrange("p (h c) -> p h c", h=HEADS),
                                                  HD ** -0.5, ends[:, t], ALU.mult, ALU.add))
                step(dve.tensor_reduce(top[:], sc[:], AX_X, ALU.max))
                for t in range(2):
                    step(dve.tensor_tensor(sc[:, t], sc[:, t], top[:, t].unsqueeze(2).broadcast_to([P, HEADS, CMP]), ALU.subtract))
                dve.sem_inc(lowered, 1)
                dve.wait_ge(raised, 1)
                step(dve.tensor_reduce(tot[:], sc[:], AX_X, ALU.add))
                step(dve.reciprocal(tot[:], tot[:]))
                for t in range(2):
                    step(dve.tensor_tensor(sc[:, t], sc[:, t], tot[:, t].unsqueeze(2).broadcast_to([P, HEADS, CMP]), ALU.mult))
                    step(dve.tensor_tensor(sc[:, t], sc[:, t], valid[:, t].unsqueeze(1).broadcast_to([P, HEADS, CMP]), ALU.mult))
                dve.sem_inc(weighed, 1)
                for b in range(4):
                    dve.wait_ge(p_turned, b + 1)
                    dve.tensor_copy(p_t[:, 2 * b:2 * b + 2, :], bank[b][0:CMP, :].rearrange("p (h t) -> p h t", h=2)).then_inc(p_ready, 1)


def phase_attend(nc, g):
    rows = lambda c0, h: g.d_p2[bass.ds(h * HD + c0, HD), :]
    one = lambda a, h: a[bass.ds(h, 1)].rearrange("h r t -> (h r) t")
    kinds = [
        (MLA_DK, lambda h, gr: one(g.d_mq, h), lambda h, gr: one(g.d_mk, h), lambda h, gr: h * HD,
         lambda h, t: g.c_causal[:, t, :], (g.d_o, 0), 0),
        (HD, lambda h, gr: rows(FOX_Q, h), lambda h, gr: rows(FOX_K, h), lambda h, gr: h * HD + 512,
         lambda h, t: g.d_fox[bass.ds(h, 1), :, t, :].rearrange("h p k -> (h p) k"), (g.d_o, 512), 0),
        (HD, lambda h, gr: rows(NSA_Q, h), lambda h, gr: rows(NSA_KS, gr), lambda h, gr: gr * HD + 1024,
         lambda h, t: skewed(g, h, t), (g.d_n, 512), 0),
        (HD, lambda h, gr: rows(NSA_Q, h), lambda h, gr: rows(NSA_KW, gr), lambda h, gr: gr * HD + 1152,
         lambda h, t: skewed(g, h, t), (g.d_n, 1024), 0),
        (HD, lambda h, gr: rows(SWA_Q, h), lambda h, gr: rows(SWA_K, gr), lambda h, gr: gr * HD + 1280,
         lambda h, t: skewed(g, h + HEADS, t), (g.d_o, 1536), 1),
    ]
    W0, W1 = P + 1, LAT + 1
    with ExitStack() as stack:
        s = Scope(nc, stack, "at")
        q, k = s.sb("q", [MLA_DK, 4, LAT]), s.sb("k", [MLA_DK, 4, W1])
        v = s.sb("v", [P, 4, 2, HD])
        bias, p = s.sb("bias", [P, 4, W0 + W1]), s.sb("p", [P, 4, W0 + W1])
        p_t = s.sb("p_t", [P, 2, 3 * P])
        neg, tot = s.sb("neg", [P, 4, 2]), s.sb("tot", [P, 4, 2])
        sinks = s.sb("sinks", [P, 2, HEADS])
        o = s.sb("o", [HD, 2, LAT])
        ps_s = [s.ps(f"ps_s{j}", [P, 512]) for j in range(4)]
        ps_t = [s.ps(f"ps_t{j}", [P, 512]) for j in range(2)]
        ps_o = [s.ps(f"ps_o{j}", [P, 512]) for j in range(2)]
        sinks_in, zero_keys, no_sinks = s.sem("sinks_in"), s.sem("zero_keys"), s.sem("no_sinks")
        in_done = [s.sem(f"in_done{j}") for j in range(4)]
        v_in = [s.sem(f"v_in{j}") for j in range(4)]
        o_stored = [s.sem(f"o_stored{j}") for j in range(2)]
        (scored, biased, peaked, raised, weighed, turned, p_copied, mixed, o_copied, v_step) = (Signal(s, n, per) for n, per in (
            ("scored", 4), ("biased", 4), ("peaked", 4), ("raised", 8), ("weighed", 4), ("turned", 4),
            ("p_copied", 4), ("mixed", 4), ("o_copied", 4), ("v_step", 16)))

        def rounds(eng, body):
            for n, kind in enumerate(kinds):
                with eng.Fori(0, 2) as gr:
                    body(kind, gr + 2 * n, gr)

        with nc.Block() as block:

            @block.sync
            def _(sp):
                sp.dma_start(sinks[:, 1, :], g.swa_sinks_2[0].partition_broadcast(P)).then_inc(sinks_in, 16)

                def body(kind, i, gr):
                    dk, q_of, k_of, v_of, bias_of, _, _ = kind
                    for j in range(4):
                        h = gr * 4 + j
                        biased.wait(sp, i, j + 1)
                        for dst, src in ((q[0:dk, j, :], q_of(h, gr)), (k[0:dk, j, 1:W1], k_of(h, gr)),
                                         (bias[:, j, 1:W0], bias_of(h, 0)[:, 0:P]), (bias[:, j, W0 + 1:W0 + W1], bias_of(h, 1))):
                            sp.dma_start(dst, src).then_inc(in_done[j], 16)
                    for j in range(4):
                        mixed.wait(sp, i, j + 1)
                        sp.dma_start(v[:, j], g.d_v[:, bass.ds(v_of(gr * 4 + j, gr), HD)].rearrange("(t p) c -> p t c", p=P))\
                          .then_inc(v_in[j], 16)

                rounds(sp, body)
                for j in range(SLOTS):
                    g.ring.load(sp, g.n_out_2 + j, 0, g.w_out_2[0, j * P:(j + 1) * P, :].unsqueeze(1), 1, D)

            @block.tensor
            def _(pe):
                pe.sem_inc(mixed.sem, 4)
                pe.wait_ge(zero_keys, 1)

                def mix(i, j):
                    p_copied.wait(pe, i, j + 1)
                    pe.wait_ge(v_in[j], 16 * i + 16)
                    o_copied.wait(pe, i, j + 1)
                    pe.matmul(ps_o[j % 2][0:HD, 0:LAT], v[:, j, 0, :], p_t[:, j % 2, 0:LAT], start=True, stop=False)
                    pe.matmul(ps_o[j % 2][0:HD, P:LAT], v[:, j, 1, :], p_t[:, j % 2, LAT:3 * P], start=False, stop=True)\
                      .then_inc(mixed.sem, 1)

                def body(kind, i, gr):
                    dk = kind[0]
                    for j in range(4):
                        pe.wait_ge(in_done[j], 64 * i + 64)
                        pe.matmul(ps_s[j][:, 0:W0], q[0:dk, j, 0:P], k[0:dk, j, 0:W0], start=True, stop=True)
                        pe.matmul(ps_s[j][:, W0:W0 + W1], q[0:dk, j, P:LAT], k[0:dk, j, :], start=True, stop=True).then_inc(scored.sem, 1)
                    for j in range(4):
                        weighed.wait(pe, i, j + 1)
                        for b, at in enumerate((1, W0 + 1, W0 + 1 + P)):
                            ins = pe.transpose(ps_t[j % 2][:, P * b:P * b + P], p[:, j, at:at + P], g.ident[:])
                        ins.then_inc(turned.sem, 1)
                        if j:
                            mix(i, j - 1)
                    mix(i, 3)

                rounds(pe, body)

            @block.vector
            def _(dve):
                dve.sem_inc(biased.sem, 4)
                dve.memset(k[:, :, 0:1], 0.0).then_inc(zero_keys, 1)
                dve.memset(sinks[:, 0, :], NEG).then_inc(no_sinks, 1)
                dve.wait_ge(sinks_in, 16)
                dve.wait_ge(no_sinks, 1)

                def body(kind, i, gr):
                    scale = kind[0] ** -0.5
                    step = Chain(dve, v_step, i)
                    for j in range(4):
                        at = bass.ds(gr * 4 + j, 1)
                        step(dve.tensor_copy(bias[:, j, 0:W0 + 1:W0], sinks[:, kind[6], at].broadcast_to([P, 2])))
                        scored.wait(dve, i, j + 1)
                        step.tell(dve.scalar_tensor_tensor(p[:, j, :], ps_s[j][:, 0:W0 + W1], scale, bias[:, j, :], ALU.mult, ALU.add),
                                  biased, j + 5)
                        step(dve.tensor_reduce(neg[:, j, 0:1], p[:, j, 0:W0], AX_X, ALU.max, negate=True))
                        step.tell(dve.tensor_reduce(neg[:, j, 1:2], p[:, j, W0:W0 + W1], AX_X, ALU.max, negate=True), peaked, j + 1)
                    for j in range(5):
                        if j < 4:
                            raised.wait(dve, i, 2 * j + 2)
                            step(dve.reciprocal(tot[:, j, :], tot[:, j, :]))
                            step.free(dve.tensor_scalar(p[:, j, 0:W0], p[:, j, 0:W0], tot[:, j, 0:1], None, ALU.mult))
                            step.tell(dve.tensor_scalar(p[:, j, W0:W0 + W1], p[:, j, W0:W0 + W1], tot[:, j, 1:2], None, ALU.mult),
                                      weighed, j + 1)
                        if j:
                            turned.wait(dve, i, j)
                            step.tell(dve.tensor_copy(p_t[:, (j - 1) % 2, :], ps_t[(j - 1) % 2][:, 0:3 * P]), p_copied, j)
                    step.end()

                rounds(dve, body)

            @block.scalar
            def _(act):
                act.sem_inc(o_copied.sem, 2)
                for j in range(2):
                    act.sem_inc(o_stored[j], 16)

                def body(kind, i, gr):
                    dram, r0 = kind[5]
                    for j in range(4):
                        peaked.wait(act, i, j + 1)
                        for t, cols in enumerate((slice(0, W0), slice(W0, W0 + W1))):
                            act.activation(p[:, j, cols], p[:, j, cols], ACT.Exp, bias=neg[:, j, t:t + 1],
                                           accum_out=tot[:, j, t:t + 1]).then_inc(raised.sem, 1)
                    for j in range(4):
                        mixed.wait(act, i, j + 5)
                        act.wait_ge(o_stored[j % 2], 32 * i + 16 * (j // 2) + 16)
                        act.activation(o[:, j % 2, :], ps_o[j % 2][0:HD, 0:LAT], ACT.Copy).then_inc(o_copied.sem, 1)
                        o_copied.wait(act, i, j + 3)
                        act.dma_start(dram[bass.ds(gr * 256 + (r0 + HD * j), HD), :], o[:, j % 2, :]).then_inc(o_stored[j % 2], 16)

                rounds(act, body)
                for j in range(2):
                    act.wait_ge(o_stored[j], 32 * 2 * len(kinds) + 16)


def phase_gather(nc, g):
    with ExitStack() as stack:
        s = Scope(nc, stack, "ga")
        g.ring.place_parts(s)
        o = s.sb("o", [P, KT, LAT])
        gates, parts = s.sb("gates", [P, 3, 4, LAT]), s.sb("parts", [P, 3, 4, LAT])
        sq = s.sb("sq", [P, 4, LAT])
        rstd = s.sb("rstd", [P, 4, LAT])
        rows, cols, eps = s.sb("rows", [KT, P]), s.sb("cols", [P, KT]), s.sb("eps", [P, 1])
        zeros = s.sb("zeros", [P, P])
        banks = [s.ps(f"bank{i}", [P, 512]) for i in range(8)]
        parts_in, gates_in, o_in, rows_in, bent, stepped, mixed, turned, squared, summed, rooted, ready = (s.sem(n) for n in (
            "parts_in", "gates_in", "o_in", "rows_in", "bent", "stepped", "mixed", "turned", "squared", "summed", "rooted", "ready"))
        eps_set = s.sem("eps_set")
        n_o = g.n_out_2

        with nc.Block() as block:

            @block.sync
            def _(sp):
                deep_loads(sp, g, n_o, g.w_out_2[0], KT, early=True)

            @block.scalar
            def _(act):
                act.dma_start(rows[:], g.group_norm_2[0].rearrange("(k p) -> k p", p=P)).then_inc(rows_in, 16)
                for h in range(HEADS):
                    half = slice(HD * (h % 2), HD * (h % 2) + HD)
                    row = NSA_GATE + 3 * h
                    act.dma_start(gates[half, :, h // 2, :], g.d_p2[row:row + 3, :].partition_broadcast(HD)).then_inc(gates_in, 16)
                for j in range(3):
                    act.dma_start(parts[:, j], g.d_n[512 * j:512 * j + 512, :].rearrange("(k p) t -> p k t", p=P)).then_inc(parts_in, 16)
                for k in (0, 4, 12):
                    act.dma_start(o[:, k:k + 4, :], g.d_o[P * k:P * (k + 4), :].rearrange("(k p) t -> p k t", p=P)).then_inc(o_in, 16)
                act.wait_ge(gates_in, 16 * HEADS)
                act.activation(gates[:], gates[:], ACT.Tanh, scale=0.5).then_inc(bent, 1)
                act.wait_ge(o_in, 48)
                act.wait_ge(eps_set, 1)
                for n, k in enumerate((0, 4, 12, 8)):
                    if n == 3:
                        act.wait_ge(mixed, 1)
                    if n:
                        act.wait_ge(summed, n)
                    act.activation(sq[:], o[:, k:k + 4, :], ACT.Square).then_inc(squared, 1)
                for n in range(4):
                    act.wait_ge(summed, n + 1)
                    act.activation(rstd[:, n, :], banks[n][:, 0:LAT], ACT.Sqrt, bias=eps[:, 0:1], scale=1.0 / 512).then_inc(rooted, 1)
                act.wait_ge(ready, 1)
                deep_splits(act, g.ring.split_high, n_o, o, KT)

            @block.tensor
            def _(pe):
                pe.wait_ge(rows_in, 16)
                pe.transpose(banks[4][:, 0:KT], rows[:], g.ident[0:KT, 0:KT]).then_inc(turned, 1)
                for n in range(4):
                    pe.wait_ge(squared, n + 1)
                    for k in range(4):
                        ins = pe.matmul(banks[n][:, 0:LAT], g.ones[:], sq[:, k, :], start=(k == 0), stop=(k == 3))
                    ins.then_inc(summed, 1)
                pe.wait_ge(ready, 1)
                deep_products(pe, g, n_o, KT, banks, zeros[:])

            @block.vector
            def _(dve):
                step = Steps(dve, stepped)
                dve.memset(eps[:], EPS).then_inc(eps_set, 1)
                step(dve.memset(zeros[:], 0.0))
                dve.wait_ge(turned, 1)
                step(dve.tensor_copy(cols[:], banks[4][:, 0:KT]))
                dve.wait_ge(parts_in, 48)
                dve.wait_ge(bent, 1)
                step(dve.scalar_tensor_tensor(parts[:], gates[:], 1.0, parts[:], ALU.add, ALU.mult))
                step(dve.tensor_tensor(parts[:, 0], parts[:, 0], parts[:, 1], ALU.add))
                step(dve.tensor_tensor(parts[:, 0], parts[:, 0], parts[:, 2], ALU.add))
                step(dve.tensor_scalar(o[:, 8:12, :], parts[:, 0], 0.5, None, ALU.mult))
                dve.sem_inc(mixed, 1)
                dve.wait_ge(rooted, 4)
                dve.wait_ge(o_in, 48)
                step(dve.reciprocal(rstd[:], rstd[:]))
                for n, k in enumerate((0, 4, 12, 8)):
                    for kt in range(k, k + 4):
                        step.free(dve.scalar_tensor_tensor(o[:, kt, :], o[:, kt, :], cols[:, kt:kt + 1], rstd[:, n, :], ALU.mult, ALU.mult))
                step.settle()
                dve.sem_inc(ready, 1)
                deep_splits(dve, g.ring.split_low, n_o, o, KT)
                g.ring.wait_done(dve, n_o + KT - 1, 0)
                add_scaled(dve, step, g, banks, None)


def build(nc, g):
    with ExitStack() as stack:
        top = Scope(nc, stack, "all")
        g.ring = Ring(top)
        g.ident = top.sb("ident", [P, P])
        g.ones = top.sb("ones", [P, P])
        g.x_t = top.sb("x_t", [P, KT, LAT])
        cols = top.sb("cols", [P, 4 * KT])
        g.d_mod = nc.dram_tensor("mod", (2, 6 * D), F32).ap()
        g.d_p = nc.dram_tensor("proj", (N_IN, TOK), F32).ap()
        g.d_p2 = nc.dram_tensor("proj2", (N_IN2, LAT), F32).ap()
        g.d_mq = nc.dram_tensor("mla_q", (HEADS, MLA_DK, LAT), F32).ap()
        g.d_mk = nc.dram_tensor("mla_k", (HEADS, MLA_DK, LAT), F32).ap()
        g.d_v = nc.dram_tensor("values", (LAT, V_COLS), F32).ap()
        g.d_frow = nc.dram_tensor("fox_sums", (HEADS, LAT), F32).ap()
        g.d_fox = nc.dram_tensor("fox_bias", (HEADS, P, 2, LAT), F32).ap()
        g.d_skew = nc.dram_tensor("distance_bias", (2 * HEADS, P * 512 + P), F32).ap()
        g.d_n = nc.dram_tensor("nsa_parts", (3 * 512, LAT), F32).ap()
        g.d_o = nc.dram_tensor("mixed", (D, LAT), F32).ap()
        phase_ada(nc, g)
        with ExitStack() as inner:
            g.h = Scope(nc, inner, "h").sb("h", [P, KT, TOK])
            phase_norm1(nc, g)
            phase_project(nc, g, "wi", g.w_in[0], g.d_p, g.h,
                          [(0, 2, LAT), (RW_W, 4, TOK), (CONV0, 2, LAT), (CONV0 + GDN_W, 4, TOK), (Z0, 2, LAT), (GATE0, 8, LAT)],
                          [(3 * RW_W, RW_COLS - 3 * RW_W, TOK), (AB0, 4 * GDN_HEADS, TOK)])
        with ExitStack() as inner:
            mixers = Scope(nc, inner, "mx")
            g.o_a = mixers.sb("o_a", [P, RW_HEADS // 2, LAT])
            with ExitStack() as scans:
                shared = Scope(nc, scans, "sc")
                g.tri = shared.sb("tri", [P, 2, 2, P])
                g.mask = shared.sb("mask", [P, 2, P])
                g.level = shared.sb("level", [P, 8, P], I32)
                phase_rwkv(nc, g)
                g.o_b = shared.sb("o_b", [P, GDN_HEADS, LAT])
                phase_gdn(nc, g)
                phase_merge(nc, g)
        with ExitStack() as inner:
            h = Scope(nc, inner, "h2").sb("h", [P, KT, LAT])
            m = g.d_mod[0]
            phase_norm(nc, g, "n2", [g.norm2_w[0], m[3 * D:4 * D], m[4 * D:5 * D], m[5 * D:6 * D]], h, cols, True)
            phase_ffn(nc, g, "f1", h, g.ffn_w_gate_up[0], g.ffn_w_down[0], FFN, True, cols[:, 3 * KT:4 * KT])
        with ExitStack() as inner:
            h = Scope(nc, inner, "h3").sb("h", [P, KT, LAT])
            phase_norm(nc, g, "n3", [g.final_norm_w], g.x_t, cols[:, 0:KT], False)
            phase_norm(nc, g, "n4", [g.norm_attn_2[0]], h, cols[:, 0:KT], False)
            phase_project(nc, g, "w2", g.w_in_2[0], g.d_p2, h, [(0, 8, LAT)], [(4096, N_IN2 - 4096, LAT)])
        phase_latent(nc, g)
        phase_tables(nc, g)
        phase_compressed(nc, g)
        g.n_out_2 = g.ring.take(KT)
        phase_attend(nc, g)
        phase_gather(nc, g)
        with ExitStack() as inner:
            h = Scope(nc, inner, "h4").sb("h", [P, KT, LAT])
            phase_norm(nc, g, "n5", [g.norm_mlp_2[0]], h, cols[:, 0:KT], False)
            phase_ffn(nc, g, "f2", h, g.w_up_2[0], g.w_down_2[0], FFN_2, False, None)
        phase_norm(nc, g, "n6", [g.final_norm_2], g.x_t, cols[:, 0:KT], False)
        phase_out(nc, g, g.x_t)


class Names:
    pass


_OUT = (1, LAT, D)


def constants():
    import numpy as np

    i = np.arange(32)
    rot = np.zeros((96, 96))
    rot[80 + i[:16], 64 + i[:16]] = -1.0
    rot[64 + i[:16], 80 + i[:16]] = 1.0
    inv = np.float32(10000.0) ** (-np.arange(0, 32, 2, dtype=np.float32) / np.float32(32))
    ang = np.arange(LAT, dtype=np.float32)[None, :] * np.tile(inv, 2)[:, None]
    rope = np.concatenate([np.stack([np.ones((64, LAT)), np.zeros((64, LAT))], 1),
                           np.stack([np.cos(ang), np.sin(ang)], 1)])
    dist = LAT - 1 - np.arange(512)
    d = np.maximum(dist, 0)
    large = 16 + (np.log(np.maximum(d, 1).astype(np.float32) / np.float32(16)) / np.float32(np.log(REL_MAX / 16))
                  * np.float32(16)).astype(np.int32)
    bucket = np.where(d < 16, d, np.minimum(large, 31))
    hot = np.zeros((33, 2, 512))
    hot[bucket, :, np.arange(512)] = 1.0
    hot[32, :, :] = np.where(np.stack([dist < 0, (dist < 0) | (dist >= P)]), NEG, 0.0)
    rows = (np.arange(P)[:, None] + P * np.arange(2)[None, :])[:, :, None]
    s, t = np.arange(P)[:, None], np.arange(P)[None, :]
    lead, half = P - 1 - s, P // 2
    tri = np.stack([[(s <= t) * 1.0 - (s < half), (s < t) * 1.0 - (s < half)],
                    [(lead <= t) * 1.0 - (lead < half), (lead < t) * 1.0 - (lead < half)]])
    level = [(s // n % 2 == 1) & (t // n == s // n - 1) for n in (1, 2, 4, 8, 16, 32, 64)]
    f = lambda a: np.ascontiguousarray(a, np.float32)
    return {
        "c_ident": f(s == t), "c_ones": f(s + t >= 0),
        "c_tri": f(tri.transpose(2, 0, 1, 3)),
        "c_mid": f(np.concatenate([s < half, lead < half], 1)),
        "c_mask": f(np.stack([s < t, s <= t], 1)),
        "c_level": np.ascontiguousarray(np.stack(level + [level[0].T], 1).astype(np.int32)),
        "c_back": f(np.stack([lead <= t, lead == t, s > t], 1)),
        "c_rot": f(rot), "c_rope": f(rope), "c_bucket": f(hot),
        "c_causal": f(np.where(np.arange(LAT) <= rows, 0.0, NEG)),
        "c_valid": f(rows >= CMP_STRIDE * np.arange(CMP) + CMP_LEN - 1),
        "c_pairs": f(s // 64 == t // 64),
        "c_residue": f(np.concatenate([s % 4 == r for r in range(4)] + [s % 2 == r for r in range(2)], 1)),
    }


def kernel(**inputs):
    import numpy as _np
    import concourse.bacc as _bacc
    from concourse import mybir as _mybir
    from concourse.bass_utils import run_bass_kernel_spmd as _run

    nc = _bacc.Bacc("TRN2", target_bir_lowering=False, num_devices=1)
    g = Names()
    arrays = {}
    for name, a in list(inputs.items()) + list(constants().items()):
        a = _np.ascontiguousarray(a)
        arrays[f"in_{name}_dram"] = a
        vars(g)[name] = nc.dram_tensor(f"in_{name}_dram", a.shape, _mybir.dt.from_np(a.dtype), kind="ExternalInput").ap()
    g.out = nc.dram_tensor("out_0_dram", _OUT, F32, kind="ExternalOutput").ap()
    build(nc, g)
    r = _run(nc, [arrays], core_ids=[0])
    return r.results[0]["out_0_dram"]
```
